# Optimizing a Trainium2 kernel written in Bass

```python
import math
import jax, jax.numpy as jnp
from jax import lax
import numpy as np

D_MODEL = 1024
BATCH = 1
SEQ = 512
DEPTH = 2

CHUNK = 64

N_B_LAYERS = DEPTH // 2
N_A_LAYERS = DEPTH - N_B_LAYERS

SSM_EXPAND = 2
SSM_D_INNER = SSM_EXPAND * D_MODEL
SSM_HEAD_DIM = 64
SSM_HEADS = SSM_D_INNER // SSM_HEAD_DIM
SSM_GROUPS = 8
SSM_HEADS_PER_GROUP = SSM_HEADS // SSM_GROUPS
SSM_STATE = 128
SSM_CONV = 4
SSM_CONV_DIM = SSM_D_INNER + 2 * SSM_GROUPS * SSM_STATE
SSM_IN_DIM = 2 * SSM_D_INNER + 2 * SSM_GROUPS * SSM_STATE + SSM_HEADS
SSD_CHUNK = CHUNK
DT_MIN = 0.001
DT_MAX = 0.1

DIFF_HEAD_DIM = 64
DIFF_V_DIM = 2 * DIFF_HEAD_DIM
DIFF_HEADS = D_MODEL // DIFF_V_DIM
DIFF_WIDTH = DIFF_HEADS * DIFF_V_DIM
KV_DIM = DIFF_HEADS * 2 * DIFF_HEAD_DIM + DIFF_WIDTH
Q_BLOCK = 128
ALIBI_MAX_EXP = 8.0

EPS = 1e-5


def rms_norm(x, g):
    xf = x.astype(jnp.float32)
    y = xf * lax.rsqrt(jnp.mean(xf * xf, axis=-1, keepdims=True) + EPS)
    return (y * g.astype(jnp.float32)).astype(x.dtype)

def gated_group_rms_norm(y, z, g):
    u = y.astype(jnp.float32) * jax.nn.silu(z.astype(jnp.float32))
    shp = u.shape
    u = u.reshape(shp[:-1] + (SSM_GROUPS, SSM_D_INNER // SSM_GROUPS))
    u = u * lax.rsqrt(jnp.mean(u * u, axis=-1, keepdims=True) + EPS)
    return u.reshape(shp) * g.astype(jnp.float32)

def causal_depthwise_conv(u, w, bias):
    c = u.shape[-1]
    out = lax.conv_general_dilated(
        u, w[:, None, :].astype(u.dtype), window_strides=(1,),
        padding=[(SSM_CONV - 1, 0)], dimension_numbers=("NWC", "WIO", "NWC"),
        feature_group_count=c)
    return out + bias.astype(u.dtype)

def ssd_chunked_scan(xdt, adt, bm, cm):
    b, s = xdt.shape[:2]
    nc = s // SSD_CHUNK

    def to_chunks(t):
        return jnp.moveaxis(t.reshape((b, nc, SSD_CHUNK) + t.shape[2:]), 1, 0)

    causal = jnp.tril(jnp.ones((SSD_CHUNK, SSD_CHUNK), dtype=bool))[None, :, :, None, None]

    def step(state, inp):
        x_c, a_c, b_c, c_c = inp
        acs = jnp.cumsum(a_c, axis=1)
        seg = acs[:, :, None] - acs[:, None, :]
        decay = jnp.exp(jnp.where(causal, seg, -jnp.inf))
        cb = jnp.einsum("blgn,bsgn->blsg", c_c, b_c)
        y_diag = jnp.einsum("blsgr,bsgrp->blgrp", cb[..., None] * decay, x_c)
        y_off = jnp.einsum("blgn,bgrpn->blgrp", c_c, state) * jnp.exp(acs)[..., None]
        to_end = jnp.exp(acs[:, -1:] - acs)
        new_state = (state * jnp.exp(acs[:, -1])[..., None, None]
                     + jnp.einsum("blgn,blgrp->bgrpn", b_c, x_c * to_end[..., None]))
        return new_state, y_diag + y_off

    state0 = jnp.zeros((b, SSM_GROUPS, SSM_HEADS_PER_GROUP, SSM_HEAD_DIM, SSM_STATE), jnp.float32)
    _, ys = lax.scan(step, state0, (to_chunks(xdt), to_chunks(adt), to_chunks(bm), to_chunks(cm)))
    return jnp.moveaxis(ys, 0, 1).reshape(xdt.shape)

def mamba2_layer(x, norm_g, w_in, conv_w, conv_b, dt_bias, a_log, d_skip, gate_norm_g, w_out):
    b, s, _ = x.shape
    G, R, P, N = SSM_GROUPS, SSM_HEADS_PER_GROUP, SSM_HEAD_DIM, SSM_STATE
    h = rms_norm(x, norm_g)
    zxbcdt = h @ w_in
    z = zxbcdt[..., :SSM_D_INNER]
    xbc = zxbcdt[..., SSM_D_INNER:SSM_D_INNER + SSM_CONV_DIM]
    dt_raw = zxbcdt[..., SSM_D_INNER + SSM_CONV_DIM:]
    xbc = jax.nn.silu(causal_depthwise_conv(xbc, conv_w, conv_b))
    gn = G * N
    xs = xbc[..., :SSM_D_INNER].reshape(b, s, G, R, P).astype(jnp.float32)
    bm = xbc[..., SSM_D_INNER:SSM_D_INNER + gn].reshape(b, s, G, N).astype(jnp.float32)
    cm = xbc[..., SSM_D_INNER + gn:].reshape(b, s, G, N).astype(jnp.float32)
    dt = jax.nn.softplus(dt_raw.astype(jnp.float32) + dt_bias.astype(jnp.float32)).reshape(b, s, G, R)
    a = -jnp.exp(a_log.astype(jnp.float32)).reshape(G, R)
    y = ssd_chunked_scan(xs * dt[..., None], a * dt, bm, cm)
    y = y + d_skip.astype(jnp.float32).reshape(G, R, 1) * xs
    y = gated_group_rms_norm(y.reshape(b, s, SSM_D_INNER), z, gate_norm_g).astype(x.dtype)
    return x + y @ w_out

def shared_kv(x, kv_norm_g, w_kv):
    b, s, _ = x.shape
    kv = rms_norm(x, kv_norm_g) @ w_kv
    k = kv[..., :DIFF_HEADS * 2 * DIFF_HEAD_DIM].reshape(b, s, DIFF_HEADS, 2, DIFF_HEAD_DIM)
    v = kv[..., DIFF_HEADS * 2 * DIFF_HEAD_DIM:].reshape(b, s, DIFF_HEADS, DIFF_V_DIM)
    return k.transpose(0, 2, 3, 1, 4), v.transpose(0, 2, 1, 3)

def diff_attention_layer(x, k, v, norm_g, w_in, lam_qk, sub_g, w_out, lambda_init):
    b, s, _ = x.shape
    H, d = DIFF_HEADS, DIFF_HEAD_DIM
    nblk = s // Q_BLOCK
    qg = rms_norm(x, norm_g) @ w_in
    q = qg[..., :DIFF_WIDTH].reshape(b, nblk, Q_BLOCK, H, 2, d).transpose(1, 0, 3, 4, 2, 5)
    gate = qg[..., DIFF_WIDTH:]
    lf = lam_qk.astype(jnp.float32)
    lam = jnp.exp(jnp.sum(lf[0] * lf[1])) - jnp.exp(jnp.sum(lf[2] * lf[3])) + lambda_init
    slopes = 2.0 ** (-ALIBI_MAX_EXP * jnp.arange(1, H + 1, dtype=jnp.float32) / H)
    key_pos = jnp.arange(s)
    scale = 1.0 / math.sqrt(d)

    def attend_block(args):
        qb, blk = args
        qpos = blk * Q_BLOCK + jnp.arange(Q_BLOCK)
        dist = jnp.abs(qpos[:, None] - key_pos[None, :]).astype(jnp.float32)
        allowed = (key_pos // CHUNK)[None, :] <= (qpos // CHUNK)[:, None]
        scores = jnp.einsum("bhiqd,bhikd->bhiqk", qb, k).astype(jnp.float32) * scale
        scores = scores - slopes[None, :, None, None, None] * dist
        probs = jax.nn.softmax(jnp.where(allowed, scores, -jnp.inf), axis=-1)
        weights = probs[:, :, 0] - lam * probs[:, :, 1]
        return jnp.einsum("bhqk,bhke->bqhe", weights.astype(v.dtype), v)

    out = lax.map(attend_block, (q, jnp.arange(nblk)))
    out = jnp.moveaxis(out, 0, 1).reshape(b, s, H, DIFF_V_DIM)
    out = (rms_norm(out, sub_g) * (1.0 - lambda_init)).reshape(b, s, DIFF_WIDTH)
    return x + (out * jax.nn.silu(gate)) @ w_out

def first_inputs(seed: int = 0) -> dict:
    key = jax.random.key(seed)
    ks = jax.random.split(key, 18)
    f32 = jnp.float32

    def nrm(k, shape, scale):
        return jax.random.normal(k, shape, f32) * scale

    def gain(k, shape):
        return 1.0 + 0.05 * jax.random.normal(k, shape, f32)

    x = jax.random.normal(ks[0], (BATCH, SEQ, D_MODEL), f32)
    a_norm_g = gain(ks[1], (N_A_LAYERS, D_MODEL))
    a_w_in = nrm(ks[2], (N_A_LAYERS, D_MODEL, SSM_IN_DIM), D_MODEL ** -0.5)
    a_conv_w = nrm(ks[3], (N_A_LAYERS, SSM_CONV, SSM_CONV_DIM), SSM_CONV ** -0.5)
    a_conv_b = nrm(ks[4], (N_A_LAYERS, SSM_CONV_DIM), 0.01)
    u = jax.random.uniform(ks[5], (N_A_LAYERS, SSM_HEADS), f32)
    dt0 = jnp.exp(u * (math.log(DT_MAX) - math.log(DT_MIN)) + math.log(DT_MIN))
    a_dt_bias = dt0 + jnp.log(-jnp.expm1(-dt0))
    a_a_log = jnp.log(jax.random.uniform(ks[6], (N_A_LAYERS, SSM_HEADS), f32, 1.0, 16.0))
    a_d_skip = gain(ks[7], (N_A_LAYERS, SSM_HEADS))
    a_gate_norm_g = gain(ks[8], (N_A_LAYERS, SSM_D_INNER))
    a_w_out = nrm(ks[9], (N_A_LAYERS, SSM_D_INNER, D_MODEL), SSM_D_INNER ** -0.5)
    kv_norm_g = gain(ks[10], (D_MODEL,))
    w_kv = nrm(ks[11], (D_MODEL, KV_DIM), D_MODEL ** -0.5)
    b_norm_g = gain(ks[12], (N_B_LAYERS, D_MODEL))
    b_w_in = nrm(ks[13], (N_B_LAYERS, D_MODEL, 2 * DIFF_WIDTH), D_MODEL ** -0.5)
    b_lambda = nrm(ks[14], (N_B_LAYERS, 4, DIFF_HEAD_DIM), 0.1)
    b_sub_g = gain(ks[15], (N_B_LAYERS, DIFF_V_DIM))
    b_w_out = nrm(ks[16], (N_B_LAYERS, DIFF_WIDTH, D_MODEL), DIFF_WIDTH ** -0.5)
    final_norm_g = gain(ks[17], (D_MODEL,))
    return {"x": x, "a_norm_g": a_norm_g, "a_w_in": a_w_in, "a_conv_w": a_conv_w,
            "a_conv_b": a_conv_b, "a_dt_bias": a_dt_bias, "a_a_log": a_a_log,
            "a_d_skip": a_d_skip, "a_gate_norm_g": a_gate_norm_g, "a_w_out": a_w_out,
            "kv_norm_g": kv_norm_g, "w_kv": w_kv, "b_norm_g": b_norm_g, "b_w_in": b_w_in,
            "b_lambda": b_lambda, "b_sub_g": b_sub_g, "b_w_out": b_w_out,
            "final_norm_g": final_norm_g}

def first_block(x, a_norm_g, a_w_in, a_conv_w, a_conv_b, a_dt_bias, a_a_log, a_d_skip,
              a_gate_norm_g, a_w_out, kv_norm_g, w_kv, b_norm_g, b_w_in, b_lambda,
              b_sub_g, b_w_out, final_norm_g):
    k = v = None
    for i in range(DEPTH):
        if i < N_A_LAYERS:
            x = mamba2_layer(x, a_norm_g[i], a_w_in[i], a_conv_w[i], a_conv_b[i],
                             a_dt_bias[i], a_a_log[i], a_d_skip[i], a_gate_norm_g[i], a_w_out[i])
            if i == N_A_LAYERS - 1:
                k, v = shared_kv(x, kv_norm_g, w_kv)
        else:
            j = i - N_A_LAYERS
            lambda_init = 0.8 - 0.6 * math.exp(-0.3 * i)
            x = diff_attention_layer(x, k, v, b_norm_g[j], b_w_in[j], b_lambda[j],
                                     b_sub_g[j], b_w_out[j], lambda_init)
    return rms_norm(x, final_norm_g)


DEPTH_2 = 1

N_META = 16
D_MIX = D_MODEL
D_POOL = D_MIX // 4
POOL_WINDOWS = (2, 4, 8, 16)
POOL_GROUPS = len(POOL_WINDOWS)
POOL_GW = D_POOL // POOL_GROUPS
D_CONV = D_MIX // 4
CONV_K = 31
D_RNN = D_MIX - D_POOL - D_CONV
RG_HEADS = 8
RG_HD = D_RNN // RG_HEADS
RG_CONV_K = 4
RG_C = 8.0
D_IN = D_POOL + 2 * D_CONV + 2 * D_RNN
D_FF = 4 * D_MODEL
EPS_2 = 1e-6


def _rmsnorm(x, g):
    xf = x.astype(jnp.float32)
    y = xf * lax.rsqrt(jnp.mean(xf * xf, axis=-1, keepdims=True) + EPS_2)
    return y.astype(x.dtype) * g

def _layernorm(x, g, b):
    xf = x.astype(jnp.float32)
    mu = jnp.mean(xf, axis=-1, keepdims=True)
    var = jnp.mean(jnp.square(xf - mu), axis=-1, keepdims=True)
    return ((xf - mu) * lax.rsqrt(var + EPS_2)).astype(x.dtype) * g + b

def _causal_depthwise_conv(x, w, b):
    K, C = w.shape
    y = lax.conv_general_dilated(
        x, w[:, None, :], window_strides=(1,), padding=[(K - 1, 0)],
        dimension_numbers=('NWC', 'WIO', 'NWC'), feature_group_count=C)
    return y + b

def _pool_mixer(u, w_grp, scale):
    B_, T, _ = u.shape
    uf = u.astype(jnp.float32)
    cs = jnp.cumsum(uf, axis=1)
    pos = jnp.arange(1, T + 1, dtype=jnp.int32)
    outs = []
    for g, w in enumerate(POOL_WINDOWS):
        sl = slice(g * POOL_GW, (g + 1) * POOL_GW)
        c = cs[..., sl]
        prev = jnp.pad(c, ((0, 0), (w, 0), (0, 0)))[:, :T]
        cnt = jnp.minimum(pos, w).astype(jnp.float32)[None, :, None]
        outs.append((c - prev) / cnt - uf[..., sl])
    pooled = jnp.stack(outs, axis=2).astype(u.dtype)
    mixed = jnp.einsum('btgc,gcd->btgd', pooled, w_grp).reshape(B_, T, D_POOL)
    return mixed * scale

def _conformer_conv(v, gt, w_dw, b_dw, ln_g, ln_b, w_pw):
    u = v * jax.nn.sigmoid(gt)
    u = _causal_depthwise_conv(u, w_dw, b_dw)
    u = jax.nn.silu(_layernorm(u, ln_g, ln_b))
    return u @ w_pw

def _linear_scan(a, b):
    def comb(l, r):
        return (l[0] * r[0], r[0] * l[1] + r[1])
    _, h = lax.associative_scan(comb, (a, b), axis=1)
    return h

def _rglru_branch(gate_in, x_in, conv_w, conv_b, w_a, b_a, w_x, b_x, lam):
    B_, T, _ = x_in.shape
    f32 = jnp.float32
    xc = _causal_depthwise_conv(x_in, conv_w, conv_b)
    xh = xc.reshape(B_, T, RG_HEADS, RG_HD)
    r = jax.nn.sigmoid((jnp.einsum('bthc,hcd->bthd', xh, w_a).reshape(B_, T, D_RNN) + b_a).astype(f32))
    i = jax.nn.sigmoid((jnp.einsum('bthc,hcd->bthd', xh, w_x).reshape(B_, T, D_RNN) + b_x).astype(f32))
    log_a = -RG_C * r * jax.nn.softplus(-lam.astype(f32))
    a = jnp.exp(log_a)
    mult = jnp.sqrt(-jnp.expm1(2.0 * log_a))
    h = _linear_scan(a, mult * (i * xc.astype(f32)))
    return (jax.nn.gelu(gate_in.astype(f32)) * h).astype(x_in.dtype)

def second_inputs(seed: int = 0) -> dict:
    key = jax.random.key(seed)
    ks = jax.random.split(key, 24)
    f32 = jnp.float32
    L = DEPTH_2

    def nrm(k, shape, scale):
        return jax.random.normal(k, shape, f32) * scale

    u = jax.random.uniform(ks[15], (L, D_RNN), f32, 0.9, 0.999)
    a0 = u ** (1.0 / RG_C)
    rg_lambda = jnp.log(a0) - jnp.log1p(-a0)
    return {
        "x": nrm(ks[0], (BATCH, SEQ, D_MODEL), 1.0),
        "meta_tokens": nrm(ks[1], (N_META, D_MODEL), 1.0),
        "mix_norm_g": 1.0 + nrm(ks[2], (L, D_MODEL), 0.05),
        "w_in": nrm(ks[3], (L, D_MODEL, D_IN), D_MODEL ** -0.5),
        "pool_w": nrm(ks[4], (L, POOL_GROUPS, POOL_GW, POOL_GW), POOL_GW ** -0.5),
        "pool_scale": 1.0 + nrm(ks[5], (L, D_POOL), 0.1),
        "convb_dw_w": nrm(ks[6], (L, CONV_K, D_CONV), CONV_K ** -0.5),
        "convb_dw_b": nrm(ks[7], (L, D_CONV), 0.02),
        "convb_ln_g": 1.0 + nrm(ks[8], (L, D_CONV), 0.05),
        "convb_ln_b": nrm(ks[9], (L, D_CONV), 0.02),
        "convb_pw_w": nrm(ks[10], (L, D_CONV, D_CONV), D_CONV ** -0.5),
        "rg_conv_w": nrm(ks[11], (L, RG_CONV_K, D_RNN), RG_CONV_K ** -0.5),
        "rg_conv_b": nrm(ks[12], (L, D_RNN), 0.02),
        "rg_w_a": nrm(ks[13], (L, RG_HEADS, RG_HD, RG_HD), RG_HD ** -0.5),
        "rg_b_a": nrm(ks[14], (L, D_RNN), 0.02),
        "rg_w_x": nrm(ks[16], (L, RG_HEADS, RG_HD, RG_HD), RG_HD ** -0.5),
        "rg_b_x": nrm(ks[17], (L, D_RNN), 0.02),
        "rg_lambda": rg_lambda,
        "w_out": nrm(ks[18], (L, D_MIX, D_MODEL), D_MIX ** -0.5),
        "mlp_norm_g": 1.0 + nrm(ks[19], (L, D_MODEL), 0.05),
        "w_up": nrm(ks[20], (L, D_MODEL, D_FF), D_MODEL ** -0.5),
        "w_down": nrm(ks[21], (L, D_FF, D_MODEL), D_FF ** -0.5),
        "final_norm_g": 1.0 + nrm(ks[22], (D_MODEL,), 0.05),
    }

def second_block(x, meta_tokens, mix_norm_g, w_in, pool_w, pool_scale, convb_dw_w, convb_dw_b,
              convb_ln_g, convb_ln_b, convb_pw_w, rg_conv_w, rg_conv_b, rg_w_a, rg_b_a,
              rg_w_x, rg_b_x, rg_lambda, w_out, mlp_norm_g, w_up, w_down, final_norm_g):
    B_ = x.shape[0]
    meta = jnp.broadcast_to(meta_tokens[None].astype(x.dtype), (B_, N_META, D_MODEL))
    h = jnp.concatenate([meta, x], axis=1)
    splits = [D_POOL, D_POOL + D_CONV, D_POOL + 2 * D_CONV, D_POOL + 2 * D_CONV + D_RNN]
    for l in range(DEPTH_2):
        u = _rmsnorm(h, mix_norm_g[l])
        p = u @ w_in[l]
        p_pool, p_bval, p_bgate, p_cgate, p_cx = jnp.split(p, splits, axis=-1)
        y_a = _pool_mixer(p_pool, pool_w[l], pool_scale[l])
        y_b = _conformer_conv(p_bval, p_bgate, convb_dw_w[l], convb_dw_b[l],
                              convb_ln_g[l], convb_ln_b[l], convb_pw_w[l])
        y_c = _rglru_branch(p_cgate, p_cx, rg_conv_w[l], rg_conv_b[l], rg_w_a[l], rg_b_a[l],
                            rg_w_x[l], rg_b_x[l], rg_lambda[l])
        y = jnp.concatenate([y_a, y_b, y_c], axis=-1)
        h = h + y @ w_out[l]
        u = _rmsnorm(h, mlp_norm_g[l])
        h = h + jnp.square(jax.nn.relu(u @ w_up[l])) @ w_down[l]
    h = _rmsnorm(h, final_norm_g)
    return h[:, N_META:]


def setup_inputs(seed=0):
    out = dict(first_inputs(seed))
    for name, value in second_inputs(seed + 1).items():
        if name != "x":
            out[name + "_2"] = value
    return out


def reference(
    x, a_norm_g, a_w_in, a_conv_w, a_conv_b, a_dt_bias, a_a_log, a_d_skip, a_gate_norm_g,
    a_w_out, kv_norm_g, w_kv, b_norm_g, b_w_in, b_lambda, b_sub_g, b_w_out, final_norm_g,
    meta_tokens_2, mix_norm_g_2, w_in_2, pool_w_2, pool_scale_2, convb_dw_w_2, convb_dw_b_2,
    convb_ln_g_2, convb_ln_b_2, convb_pw_w_2, rg_conv_w_2, rg_conv_b_2, rg_w_a_2, rg_b_a_2,
    rg_w_x_2, rg_b_x_2, rg_lambda_2, w_out_2, mlp_norm_g_2, w_up_2, w_down_2, final_norm_g_2,
):
    x = first_block(
        x, a_norm_g, a_w_in, a_conv_w, a_conv_b, a_dt_bias, a_a_log, a_d_skip, a_gate_norm_g,
        a_w_out, kv_norm_g, w_kv, b_norm_g, b_w_in, b_lambda, b_sub_g, b_w_out, final_norm_g,
    )
    return second_block(
        x, meta_tokens_2, mix_norm_g_2, w_in_2, pool_w_2, pool_scale_2, convb_dw_w_2,
        convb_dw_b_2, convb_ln_g_2, convb_ln_b_2, convb_pw_w_2, rg_conv_w_2, rg_conv_b_2,
        rg_w_a_2, rg_b_a_2, rg_w_x_2, rg_b_x_2, rg_lambda_2, w_out_2, mlp_norm_g_2, w_up_2,
        w_down_2, final_norm_g_2,
    )


_drawn_inputs = setup_inputs


def setup_inputs(seed=0):
    import zlib

    import numpy as np

    out = dict(_drawn_inputs(seed))
    spreads = {}
    factors = {'a_conv_b': 4.003,
     'kv_norm_g': 2.69,
     'b_norm_g': 2.713,
     'b_sub_g': 3.797,
     'convb_dw_b_2': 5.932,
     'convb_ln_g_2': 3.73,
     'convb_ln_b_2': 8.0,
     'rg_b_a_2': 62.382,
     'rg_b_x_2': 36.152}
    for name, (base, spread) in spreads.items():
        noise = np.random.default_rng([zlib.crc32(name.encode()), seed]).standard_normal(out[name].shape)
        drawn = base * np.exp(spread * noise) if base else spread * noise
        out[name] = __import__('jax').numpy.asarray(drawn.astype(out[name].dtype))
    for name, factor in factors.items():
        out[name] = (out[name] * factor).astype(out[name].dtype)
    return out
```

```python
import math
from contextlib import ExitStack

import concourse.bass as bass
from concourse import mybir

ALU = mybir.AluOpType
ACT = mybir.ActivationFunctionType
AX = mybir.AxisListType
F32 = mybir.dt.float32
F32R = mybir.dt.float32r

P = 128
D = 1024
KT = D // P
SEQ = 512
META = 16
T2 = SEQ + META
HALF2 = T2 // 2
NT = SEQ // P
GROUPS = 8
HPG = 4
DINNER = 2048
CONV_DIM = 4096
HEADS = 8
EPS1, EPS2 = 1e-5, 1e-6
LAMBDA_INIT = 0.8 - 0.6 * math.exp(-0.3)
DW_K = 31
POOL_PAD = 16

U_DT = 0
U_MAMBA = 1
U_WOUT = U_MAMBA + 6 * GROUPS
U_ATT = U_WOUT + 16
U_BOUT = U_ATT + 4 * HEADS
U_IN2 = U_BOUT + 8
U_OUT2 = U_IN2 + 14
U_MLP = U_OUT2 + 8
U_END = U_MLP + 64
M_MAMBA = 1
M_WOUT = M_MAMBA + 6 * GROUPS
M_ATT = M_WOUT + 8
M_BOUT = M_ATT + 4 * HEADS
M_IN2 = M_BOUT + 8
M_OUT2 = M_IN2 + 14
M_MLP = M_OUT2 + 8

C_GROUP = 0
GW = 24
C_ANORM = C_GROUP + GW * GROUPS
C_KVN = C_ANORM + 8
C_BN = C_KVN + 8
C_FIN = C_BN + 8
C_MIX = C_FIN + 8
C_MLP = C_MIX + 8
C_SUBG = C_MLP + 8
C_DTB = C_SUBG + 1
C_ALOG = C_DTB + 1
C_PSC = C_ALOG + 1
C_DWW = C_PSC + 2
C_DWB = C_DWW + 2 * DW_K
C_LNG = C_DWB + 2
C_LNB = C_LNG + 2
C_RGW = C_LNB + 2
C_RGB = C_RGW + 16
C_BA = C_RGB + 4
C_BX = C_BA + 4
C_LAM = C_BX + 4
NPAR = C_LAM + 4

K_ID = 0
K_CAUSAL = K_ID + P
K_INV = K_CAUSAL + P
K_SLOPE = K_INV + 2 * POOL_PAD
K_WIN = K_SLOPE + HEADS
NCONST = K_WIN + 2


class Lin:

    def __init__(self, c, k=0, reg=None):
        self.c, self.k, self.reg = c, k, reg

    def __add__(self, n):
        return Lin(self.c + n, self.k, self.reg)

    def __sub__(self, n):
        return self + (-n)

    def __mul__(self, n):
        return Lin(self.c * n, self.k * n, self.reg)

    @property
    def half(self):
        assert self.k % 2 == 0
        return Lin(self.c // 2, self.k // 2, self.reg)

    @property
    def par(self):
        assert self.k % 2 == 0
        return self.c % 2

    @property
    def v(self):
        return self.c if self.reg is None or self.k == 0 else self.reg * self.k + self.c


class Steps:

    def __init__(self, eng, sem):
        self.eng, self.sem, self.base, self.n = eng, sem, Lin(0), 0

    def __call__(self, ins):
        ins.then_inc(self.sem, 1)
        self.n += 1

    def wait(self):
        self.eng.wait_ge(self.sem, (self.base + self.n).v)

    def mark(self, ins):
        self(ins)
        self.wait()

    def enter(self, reg, per):
        self.start, self.per = self.base.c + self.n, per
        self.base, self.n = Lin(self.start, per, reg), 0

    def leave(self, count):
        assert self.n == self.per, self.n
        self.base, self.n = Lin(self.start + count * self.per), 0


def ds(at, n):
    return bass.ds(at, n) if not isinstance(at, int) else slice(at, at + n)


TOKENS2 = [(0, 128), (128, 128), (256, 128), (384, 128), (512, META)]
LOG1P_TERMS = 7


def build(nc, t):
    with ExitStack() as ctx:
        def sb(name, shape, dt=F32):
            return ctx.enter_context(nc.sbuf_tensor(name, shape, dt))

        w_raw = sb("w_raw", [P, 2, KT, P])
        w_hi = sb("w_hi", [P, 2, KT, P], F32R)
        w_lo = sb("w_lo", [P, 2, KT, P], F32R)
        a_hi = sb("a_hi", [P, KT, T2], F32R)
        a_lo = sb("a_lo", [P, KT, T2], F32R)
        b_hi = sb("b_hi", [P, 2 * KT, T2], F32R)
        b_lo = sb("b_lo", [P, 2 * KT, T2], F32R)
        h = sb("h", [P, KT, T2])
        rt = sb("rt", [P, T2])
        par = sb("par", [P, NPAR])
        con = sb("con", [P, NCONST])
        gconv = sb("gconv", [P, 20])
        ggate = sb("ggate", [P, 4])
        gtok = sb("gtok", [P, 3, NT, HPG])
        gfm = sb("gfm", [P, KT])
        spl = sb("spl", [P, 6, 4])
        rga = sb("rga", [P, 2, 4])
        bnst = sb("bnst", [P, 5, 6])
        bnag = sb("bnag", [P, 5, 2])
        cst = sb("cst", [P, 3])
        stat = sb("stat", [P, 96])
        psum = ctx.enter_context(nc.psum_tensor("psum", [P, 8, 512], F32))
        ARENA = 14248
        arena = sb("arena", [P, ARENA])
        mixw = sb("mixw", [P, 14 * P])
        top = [0]

        def place(*shape, at=None):
            at = top[0] if at is None else at
            n = math.prod(shape)
            top[0] = at + n
            assert top[0] <= ARENA, top[0]
            v = arena[:, at:at + n]
            if len(shape) == 2:
                v = v.rearrange("p (a b) -> p a b", a=shape[0])
            if len(shape) == 3:
                v = v.rearrange("p (a b c) -> p a b c", a=shape[0], b=shape[1])
            return v

        one, eps1, eps2 = cst[:, 0:1], cst[:, 1:2], cst[:, 2:3]
        ident = con[:, K_ID:K_ID + P]
        causal = con[:, K_CAUSAL:K_CAUSAL + P]
        decay_in = place(HPG, NT, P, at=0)
        MIX = top[0]
        mix = place(HPG, NT, P)
        sx = place(4, SEQ)
        sz = place(2, 2 * SEQ)
        pre = place(3 + SEQ)
        conv = place(2, SEQ)
        y = mixw[:, 0:2 * SEQ].rearrange("p (a b) -> p a b", a=2)
        edec = mixw[:, 2 * SEQ:14 * P].rearrange("p (a b) -> p a b", a=2)
        DTS = top[0]
        cb = place(NT, P)
        b_tok = place(NT - 1, P)
        xdt = place(NT, 2 * P)
        xend = place(NT - 1, 2 * P)
        state = place(NT - 1, 2 * P)
        tok = place(3, NT, 32, at=DTS + 8 * SEQ)
        gsq = place(2, SEQ, at=MIX)
        gun = place(2, SEQ)
        yoff = place(2, SEQ - P, at=MIX)
        x_tok = place(NT, D, at=0)
        dts = [place(SEQ, at=DTS + SEQ * i) for i in range(8)]
        meta_tok = place(D, at=MIX + 2 * SEQ * 2)
        sq = place(KT, T2, at=0)
        sq2 = place(KT, T2)
        asc = place(2 * P * 10, at=0)
        awt = place(10, P)
        aq = place(2, SEQ, at=KT * T2)
        ak = place(2, SEQ)
        asg = place(2, SEQ)
        avt = place(2, NT, P)
        afm = place(SEQ)
        agt = place(SEQ)
        aon = place(SEQ)
        aog = place(SEQ)
        afm2 = place(SEQ)
        dist = place(SEQ)
        lamt = place(4 * 64)
        lamp = place(2, 64)
        mg = place(KT, META)
        bdw = mixw[:, 0:10 * P].rearrange("p (a b) -> p a b", a=10)
        pwt = mixw[:, 10 * P:14 * P].rearrange("p (a b c) -> p a b c", a=2, b=2)
        rr = place(T2, at=0)
        cu = place(2, DW_K - 1 + T2)
        pls = place(2, POOL_PAD + T2)
        bvt, bgt = pls[:, 0, 0:T2], pls[:, 1, 0:T2]
        dwo = place(2, T2)
        cxp = place(3 + T2)
        xc = place(4, T2)
        cg = place(4, T2)
        plp = place(2, POOL_PAD + T2)
        rtmp = place(8, T2)
        lnt = place(5, 2 * P, at=top[0] - 8 * T2)
        ft = place(T2, at=0)
        fs = place(T2)
        osb = place(2, D, at=0)
        gout = place(D)
        scratch = place(D)

        S = {}
        for name in (
            "par_in con_in x_in meta_in lam_in dist_in bd_in pw_in raw0 raw1 ab_in acs_out gout_in out0 out1 "
            "hi_ready lo_ready unit_done acc_read "
            "act_own dve_own "
            "consts_set x_tp x_hi x_lo x_cp meta_tp meta_cp xsum_ready xsd_ready rs_ready rb_ready rt_ready "
            "dt_pre dt_exp dt_acs dt_endexp dt_tok dt_tp tok_ready "
            "pre_silu silu_done seg_ready mexp_ready dec_ready e_ready tpx_ready cb_ready bt_ready xw_ready m_ready "
            "st_ready s_ready y_ready u_ready gsq_ready gst_ready gsd_ready grs_ready grb_ready un_ready uh_ready "
            "ul_ready "
            "sq_ready ah_ready al_ready nst_ready nsd_ready nrs_ready nrb_ready nrt_ready bh_ready bl_ready "
            "sc_ready scs_ready mx_ready ex_ready w_ready wt_tp wt_ready vt_tp vt_ready sg_ready o_ready osd_ready "
            "on_ready ont_ready og_ready oh_ready ol_ready "
            "meta_sq s2_ready h2_ready r1_ready r1b_ready rrb_ready rr_ready "
            "bg_ready cu_ready dw_ready ln_tp ln_sd ln_ready lnb_tp cs_ready pwm_ready "
            "sp_done ln_stat xc_ready rg_ready rga_ready at_ready m2_ready mu_ready scan_ready ge_ready yc_ready "
            "pool_ready poolm_ready yh_ready yl_ready "
            "lam_sum lam_exp sp_pre sp_exp "
            "ft_ready fh_ready fl_ready otp_ready osum_ready ors_ready o_done").split():
            S[name] = ctx.enter_context(nc.semaphore(name))
        block = ctx.enter_context(nc.Block())

        def bank(i):
            return psum[:, i, :]

        def acc(m):
            return psum[:, m.par, :]

        def acc2(m):
            return psum[:, 2 * m.par:2 * m.par + 2, 0:HALF2]

        def halves(v):
            return v.rearrange("p (a b) -> p a b", a=2)

        def stat_at(c, n=NT, rows=P):
            return stat[0:rows, c:c + n]

        X_SUM, X_SD, X_RS = 0, 4, 8
        G_SD, G_RS, DEC = 12, 16, 20
        A_MX, A_NB, A_SUM, A_RC = 28, 36, 44, 52
        O_SUM, O_SD, O_RS = 60, 64, 68
        LAM, SLOPE, EA, LAMS = 72, 73, 74, 94
        N_SD, N_RS, N_R2 = 76, 82, 88

        @block.sync
        def _(sp):
            def load(u, w, k0, col):
                if u.reg is not None or u.c >= 2:
                    sp.wait_ge(S["lo_ready"], (u - 1).v)
                src = w.rearrange("(k p) m -> p k m", p=P)[:, k0:k0 + KT, ds(col.v, P)]
                sp.dma_start(w_raw[:, u.par, :, :], src).then_inc(S[f"raw{u.par}"], 16)

            def group(g):
                for j, c in enumerate(ssd_cols(g)):
                    load(g * 6 + (U_MAMBA + j), t["a_w_in"], 0, c)

            sp.dma_start(x_tok, t["x"].rearrange("(t p) d -> p t d", p=P)).then_inc(S["x_in"], 16)
            load(Lin(U_DT), t["a_w_in"], 0, Lin(DINNER + CONV_DIM + 32 - P))
            group(Lin(0))
            group(Lin(1))
            with sp.Fori(0, 3) as i:
                group(Lin(2, 2, i))
                group(Lin(3, 2, i))
            with sp.Fori(0, 4) as i:
                for m in (Lin(0, 2, i), Lin(1, 2, i)):
                    for k in range(2):
                        load(m * 2 + (U_WOUT + k), t["a_w_out"], k * KT, m * P)

            def head(n):
                load(n * 4 + U_ATT, t["w_kv"], 0, n * P)
                load(n * 4 + (U_ATT + 1), t["w_kv"], 0, n * P + D)
                load(n * 4 + (U_ATT + 2), t["b_w_in"], 0, n * P)
                load(n * 4 + (U_ATT + 3), t["b_w_in"], 0, n * P + D)

            with sp.Fori(0, HEADS) as i:
                head(Lin(0, 1, i))
            with sp.Fori(0, 4) as i:
                for m in (Lin(0, 2, i), Lin(1, 2, i)):
                    load(m + U_BOUT, t["b_w_out"], 0, m * P)
            for n, c in enumerate(IN2_TILES):
                load(Lin(U_IN2 + n), t["w_in_2"], 0, Lin(c * P))
            with sp.Fori(0, 4) as i:
                for m in (Lin(0, 2, i), Lin(1, 2, i)):
                    load(m + U_OUT2, t["w_out_2"], 0, m * P)
            for half in range(2):
                u0 = U_MLP + 32 * half
                with sp.Fori(0, 8) as i:
                    for m in (Lin(0, 2, i), Lin(1, 2, i)):
                        load(m + u0, t["w_up_2"], 0, m * P + 2048 * half)
                with sp.Fori(0, 4) as i:
                    for m in (Lin(0, 2, i), Lin(1, 2, i)):
                        for k in range(2):
                            load(m * 2 + (u0 + 16 + k), t["w_down_2"], 16 * half + k * KT, m * P)
            for i in range(NT):
                sp.wait_ge(S["o_done"], i + 1)
                sp.dma_start(t["out"][P * i:P * i + P, :], osb[:, i % 2, :]).then_inc(S[f"out{i % 2}"], 16)
            for i in range(2):
                sp.wait_ge(S[f"out{i}"], 16 * NT // 2)

        @block.gpsimd
        def _(pool):
            pool.dma_start(con[:, :], t["consts"]).then_inc(S["con_in"], 16)
            pool.dma_start(par[:, :], t["params"]).then_inc(S["par_in"], 16)
            pool.dma_start(meta_tok[0:META, :], t["meta_tokens_2"]).then_inc(S["meta_in"], 16)
            pool.wait_ge(S["dt_acs"], 1)
            pool.dma_start(t["acs"], dts[6][96:128, :]).then_inc(S["acs_out"], 16)
            pool.wait_ge(S["acs_out"], 16)
            pool.wait_ge(S["xsum_ready"], 1)
            pool.wait_ge(S["x_tp"], KT)

            def spread(g):
                pool.dma_start(decay_in.rearrange("p h c l -> p (h c l)"),
                               t["acs"][ds((g * HPG).v, HPG), :].rearrange("h l -> (h l)").partition_broadcast(P)
                               ).then_inc(S["ab_in"], 16)

            spread(Lin(0))
            with pool.Fori(1, GROUPS) as i:
                pool.wait_ge(S["u_ready"], i)
                spread(Lin(0, 1, i))
            pool.wait_ge(S["ul_ready"], GROUPS)
            pool.dma_start(lamt, t["b_lambda"].rearrange("l a b -> (l a b)").partition_broadcast(P)
                           ).then_inc(S["lam_in"], 16)
            pool.dma_start(dist, t["dist"]).then_inc(S["dist_in"], 16)
            pool.dma_start(bdw, t["blockdiag"]).then_inc(S["bd_in"], 16)
            pool.dma_start(pwt, t["convb_pw_w_2"].rearrange("(k p) (m n) -> p k m n", p=P, n=P)
                           ).then_inc(S["pw_in"], 16)
            pool.wait_ge(S["fl_ready"], 32)
            pool.dma_start(gout, t["final_norm_g_2"].partition_broadcast(P)).then_inc(S["gout_in"], 16)

        @block.tensor
        def _(pe):
            mm, tp = nc.tensor.matmul, nc.tensor.transpose

            def tile_of(u, m, xh, xl, wide, k0=0, first=True, last=True):
                if first and (m.reg is not None or m.c >= 2):
                    pe.wait_ge(S["acc_read"], (m - 1).v)
                pe.wait_ge(S["lo_ready"], (u + 1).v)
                if wide:
                    outs = [(psum[:, 2 * m.par + a, 0:HALF2], HALF2 * a, HALF2) for a in range(2)]
                else:
                    outs = [(acc(m), 0, SEQ)]
                for k in range(KT):
                    for n, (wv, xv) in enumerate(((w_hi, xh), (w_hi, xl), (w_lo, xh))):
                        for out, c0, cn in outs:
                            ins = mm(out, wv[:, u.par, k, :], xv[:, k0 + k, c0:c0 + cn],
                                     start=(first and k == 0 and n == 0),
                                     stop=(last and k == KT - 1 and n == 2), skip_group_check=True)
                ins.then_inc(S["unit_done"], 1)

            def spread(out, col, tiles, ready):
                for i, (c0, cn) in enumerate(tiles):
                    ins = tp(out[:, c0:c0 + cn], col[0:cn, i:i + 1].to_broadcast([cn, P]), ident[0:cn, 0:cn])
                ins.then_inc(ready, 1)

            def sums(out, v, tiles, ready, n=KT, off=0):
                for i, (c0, cn) in enumerate(tiles):
                    for k in range(n):
                        ins = mm(out[0:cn, i:i + 1], v[:, k, off + c0:off + c0 + cn], one,
                                 start=(k == 0), stop=(k == n - 1), skip_group_check=True)
                if ready is not None:
                    ins.then_inc(ready, 1)

            TOKENS1 = TOKENS2[:NT]

            pe.wait_ge(S["con_in"], 16)
            pe.wait_ge(S["x_in"], 16)
            for k in range(KT):
                if k >= 4:
                    pe.wait_ge(S["x_cp"], k - 3)
                for i in range(NT):
                    ins = tp(bank(2 + k % 4)[:, P * i:P * i + P], x_tok[:, i, P * k:P * k + P], ident)
                ins.then_inc(S["x_tp"], 1)
            pe.wait_ge(S["x_lo"], KT)
            tile_of(Lin(U_DT), Lin(0), a_hi, a_lo, False)
            pe.wait_ge(S["meta_in"], 16)
            for k in range(KT):
                ins = tp(bank(6)[:, META * k:META * k + META], meta_tok[0:META, P * k:P * k + P],
                         ident[0:META, 0:META])
            ins.then_inc(S["meta_tp"], 1)
            pe.wait_ge(S["rs_ready"], 1)
            spread(bank(7), stat_at(X_RS), TOKENS1, S["rb_ready"])

            def ssd_turn(s):
                pe.wait_ge(S["silu_done"], (s * 6 + 6).v)
                if s.reg is not None or s.c > 0:
                    pe.wait_ge(S["u_ready"], s.v)
                for c in range(NT):
                    for j in range(2):
                        ins = tp(bank(4 + c // 2)[:, 256 * (c % 2) + P * j:256 * (c % 2) + P * j + P],
                                 sx[:, 2 + j, P * c:P * c + P], ident)
                ins.then_inc(S["tpx_ready"], 1)
                for c in range(NT - 1):
                    tp(bank(2)[:, P * c:P * c + P], sx[:, 0, P * c:P * c + P], ident)
                for c in range(NT):
                    ins = mm(bank(3)[:, P * c:P * c + P], sx[:, 0, P * c:P * c + P], sx[:, 1, P * c:P * c + P],
                             start=True, stop=True, skip_group_check=True)
                ins.then_inc(S["cb_ready"], 1)

            def ssd_states(s):
                pe.wait_ge(S["bt_ready"], (s + 1).v)
                pe.wait_ge(S["m_ready"], (s + 1).v)
                for c in range(NT - 1):
                    ins = mm(bank(2 + c // 2)[:, 256 * (c % 2):256 * (c % 2) + 256], b_tok[:, c, :],
                             xend[:, c, :], start=True, stop=True, skip_group_check=True)
                ins.then_inc(S["st_ready"], 1)

            def ssd_y(s):
                for c in range(NT):
                    for r in range(HPG):
                        mm(bank(4 + r // 2)[64 * (r % 2):64 * (r % 2) + 64, P * c:P * c + P],
                           xdt[:, c, 64 * r:64 * r + 64], mix[:, r, c, :],
                           start=True, stop=True, skip_group_check=True)
                pe.wait_ge(S["s_ready"], (s + 1).v)
                if s.reg is not None or s.c > 0:
                    pe.wait_ge(S["un_ready"], s.v)
                for c in range(1, NT):
                    for j in range(2):
                        ins = mm(bank(6 + j)[:, P * c:P * c + P], state[:, c - 1, P * j:P * j + P],
                                 sx[:, 1, P * c:P * c + P], start=True, stop=True, skip_group_check=True)
                ins.then_inc(S["y_ready"], 1)

            def group(g, project=True):
                u, m, s = g * 6 + U_MAMBA, g * 6 + M_MAMBA, g - 1
                proj = (lambda j: tile_of(u + j, m + j, a_hi, a_lo, False)) if project else (lambda j: None)
                proj(0)
                ssd_turn(s)
                proj(1)
                ssd_states(s)
                proj(2)
                ssd_y(s)
                proj(3)
                proj(4)
                pe.wait_ge(S["gsq_ready"], (s + 1).v)
                sums(bank(6), gsq, TOKENS1, S["gst_ready"], 2)
                proj(5)
                pe.wait_ge(S["grs_ready"], (s + 1).v)
                spread(bank(7), stat_at(G_RS), TOKENS1, S["grb_ready"])

            for j in range(5):
                tile_of(Lin(U_MAMBA + j), Lin(M_MAMBA + j), a_hi, a_lo, False)
            pe.wait_ge(S["dt_tok"], 1)
            pe.wait_ge(S["meta_cp"], 1)
            for n, v in enumerate((dts[6], dts[5], dts[7])):
                for c in range(NT):
                    ins = tp(bank(6)[:, P * n + 32 * c:P * n + 32 * c + 32], v[96:128, P * c:P * c + P],
                             con[96:128, K_ID + 96:K_ID + 128])
            ins.then_inc(S["dt_tp"], 1)
            tile_of(Lin(U_MAMBA + 5), Lin(M_MAMBA + 5), a_hi, a_lo, False)
            group(Lin(1))
            with pe.Fori(0, 3) as i:
                group(Lin(2, 2, i))
                group(Lin(3, 2, i))
            group(Lin(8), project=False)
            pe.wait_ge(S["ul_ready"], GROUPS)
            with pe.Fori(0, 4) as i:
                for m in (Lin(0, 2, i), Lin(1, 2, i)):
                    for k in range(2):
                        tile_of(m * 2 + (U_WOUT + k), m + M_WOUT, b_hi, b_lo, False, k * KT, k == 0, k == 1)

            pe.wait_ge(S["sq_ready"], KT)
            sums(bank(7), sq, TOKENS1, S["nst_ready"])
            pe.wait_ge(S["al_ready"], KT)

            def scores(s, q):
                for i in range(2):
                    ins = mm(bank(2 + 2 * (q % 2) + i)[:, 0:P * (q + 1)],
                             aq[64 * i:64 * i + 64, s.par, P * q:P * q + P],
                             ak[64 * i:64 * i + 64, s.par, 0:P * (q + 1)],
                             start=True, stop=True, skip_group_check=True)
                ins.then_inc(S["sc_ready"], 1)

            def turn_weights(b, q0, q1, s):
                pe.wait_ge(S["w_ready"], (s * NT + q1).v)
                n = 0
                for q in range(q0, q1):
                    for k in range(q + 1):
                        ins = tp(bank(b)[:, P * n:P * n + P], asc[:, P * q * (q + 1) + P * k:][:, 0:P], ident)
                        n += 1
                ins.then_inc(S["wt_tp"], 1)

            def values(s, q):
                for k in range(q + 1):
                    ins = mm(bank(7)[:, P * q:P * q + P], awt[:, q * (q + 1) // 2 + k, :], avt[:, s.par, k, :],
                             start=(k == 0), stop=(k == q), skip_group_check=True)
                return ins

            def turn_v(n):
                pe.wait_ge(S["acc_read"], (n * 4 + (M_ATT + 2)).v)
                for k in range(NT):
                    ins = tp(bank(2)[:, P * k:P * k + P], afm[:, P * k:P * k + P], ident)
                ins.then_inc(S["vt_tp"], 1)

            def turn_out(f):
                pe.wait_ge(S["on_ready"], (f + 1).v)
                for k in range(NT):
                    ins = tp(bank(3)[:, P * k:P * k + P], aon[:, P * k:P * k + P], ident)
                ins.then_inc(S["ont_ready"], 1)

            def head(n, project=True, attend=True, finish=True):
                u, m, s, f = n * 4 + U_ATT, n * 4 + M_ATT, n - 1, n - 2
                proj = (lambda j: tile_of(u + j, m + j, *((a_hi, a_lo) if j < 2 else (b_hi, b_lo)), False)) \
                    if project else (lambda j: None)
                proj(0)
                if project and n.reg is None and n.c == 0:
                    pe.wait_ge(S["nrs_ready"], 1)
                    spread(bank(6), stat_at(N_RS), TOKENS1, S["nrb_ready"])
                if attend:
                    pe.wait_ge(S["acc_read"], (s * 4 + (M_ATT + 3)).v)
                    pe.wait_ge(S["vt_ready"], (s + 1).v)
                    if finish:
                        pe.wait_ge(S["wt_ready"], (f * 3 + 3).v)
                    scores(s, 0)
                    scores(s, 1)
                proj(1)
                if attend:
                    pe.wait_ge(S["scs_ready"], (s * NT + 1).v)
                    scores(s, 2)
                    pe.wait_ge(S["scs_ready"], (s * NT + 2).v)
                    scores(s, 3)
                if project and n.reg is None and n.c == 0:
                    pe.wait_ge(S["bl_ready"], KT)
                proj(2)
                if attend:
                    turn_weights(6, 0, 2, s)
                    if finish:
                        pe.wait_ge(S["scs_ready"], (s * NT + 4).v)
                        turn_out(f)
                if project:
                    if attend:
                        pe.wait_ge(S["scs_ready"], (s * NT + 3).v)
                    turn_v(n)
                proj(3)
                if attend:
                    turn_weights(4, 2, 3, s)
                    turn_weights(5, 3, 4, s)
                    pe.wait_ge(S["wt_ready"], (s * 3 + 1).v)
                    if finish:
                        pe.wait_ge(S["on_ready"], (f + 1).v)
                    values(s, 0)
                    values(s, 1)
                    pe.wait_ge(S["wt_ready"], (s * 3 + 2).v)
                    values(s, 2)
                    pe.wait_ge(S["wt_ready"], (s * 3 + 3).v)
                    values(s, 3).then_inc(S["o_ready"], 1)

            head(Lin(0), attend=False, finish=False)
            head(Lin(1), finish=False)
            with pe.Fori(0, 3) as i:
                head(Lin(2, 2, i))
                head(Lin(3, 2, i))
            head(Lin(8), project=False)
            turn_out(Lin(7))
            pe.wait_ge(S["ol_ready"], HEADS)
            with pe.Fori(0, 4) as i:
                for m in (Lin(0, 2, i), Lin(1, 2, i)):
                    tile_of(m + U_BOUT, m + M_BOUT, b_hi, b_lo, False, KT)

            pe.wait_ge(S["meta_sq"], 1)
            pe.wait_ge(S["s2_ready"], KT)
            sums(bank(7), sq, TOKENS1, None, off=META)
            sums(bank(7)[:, 4:8], sq2, TOKENS1, None)
            sums(bank(7)[:, 8:9], sq, [(0, META)], S["nst_ready"])
            pe.wait_ge(S["yl_ready"], KT)

            def in2(n):
                tile_of(Lin(U_IN2 + n), Lin(M_IN2 + n), a_hi, a_lo, True)

            in2(0)
            pe.wait_ge(S["nrs_ready"], 2)
            spread(bank(4), stat_at(N_R2), TOKENS1, S["rrb_ready"])
            spread(bank(5), stat_at(N_RS), TOKENS1, S["rrb_ready"])
            tp(bank(6)[:, 0:META], stat[0:META, N_R2 + 4:N_R2 + 5].to_broadcast([META, P]),
               ident[0:META, 0:META]).then_inc(S["rrb_ready"], 1)

            def gates(j):
                pe.wait_ge(S["xc_ready"], j + 1)
                if j:
                    pe.wait_ge(S["rga_ready"], j)
                for a in range(2):
                    for c in range(2):
                        ins = mm(psum[:, 4 + 2 * a + c, 0:HALF2], bdw[:, 2 + 4 * a + j, :],
                                 xc[:, j, HALF2 * c:HALF2 * c + HALF2], start=True, stop=True, skip_group_check=True)
                ins.then_inc(S["rg_ready"], 1)

            pe.wait_ge(S["bd_in"], 16)
            pe.wait_ge(S["pw_in"], 16)
            for n in range(1, 14):
                in2(n)
                if n == 6:
                    pe.wait_ge(S["rr_ready"], 3)
                if 6 <= n < 10:
                    gates(n - 6)
            pe.wait_ge(S["pool_ready"], 2)
            for j in range(2):
                for c in range(2):
                    ins = mm(psum[:, 2 * j + c, 0:HALF2], bdw[:, j, :],
                             plp[:, j, POOL_PAD + HALF2 * c:POOL_PAD + HALF2 * c + HALF2],
                             start=True, stop=True, skip_group_check=True)
            ins.then_inc(S["poolm_ready"], 1)
            pe.wait_ge(S["rga_ready"], 4)
            pe.wait_ge(S["dw_ready"], 2)
            for i, (c0, cn) in enumerate(TOKENS2):
                for j in range(2):
                    ins = tp(psum[0:cn, 4 + i // 2, 256 * (i % 2) + P * j:256 * (i % 2) + P * j + P],
                             dwo[:, j, c0:c0 + cn], ident)
            ins.then_inc(S["ln_tp"], 1)
            pe.wait_ge(S["yl_ready"], KT + 6)
            pe.wait_ge(S["ln_ready"], 1)
            for j in range(2):
                for i, (c0, cn) in enumerate(TOKENS2):
                    ins = tp(psum[:, 2 * j + c0 // 512, c0 % 512:c0 % 512 + cn], lnt[0:cn, i, P * j:P * j + P],
                             ident[0:cn, 0:cn])
            ins.then_inc(S["lnb_tp"], 1)
            pe.wait_ge(S["cs_ready"], 2)
            for j in range(2):
                for c in range(2):
                    for k in range(2):
                        ins = mm(psum[:, 4 + 2 * j + c, 0:HALF2], pwt[:, k, j, :],
                                 dwo[:, k, HALF2 * c:HALF2 * c + HALF2],
                                 start=(k == 0), stop=(k == 1), skip_group_check=True)
            ins.then_inc(S["pwm_ready"], 1)
            pe.wait_ge(S["yl_ready"], KT + 8)
            with pe.Fori(0, 4) as i:
                for m in (Lin(0, 2, i), Lin(1, 2, i)):
                    tile_of(m + U_OUT2, m + M_OUT2, b_hi, b_lo, True)

            pe.wait_ge(S["sq_ready"], 3 * KT)
            sums(bank(7), sq, TOKENS2, S["nst_ready"])
            pe.wait_ge(S["al_ready"], 2 * KT)
            for half in range(2):
                u0, m0 = U_MLP + 32 * half, M_MLP + 24 * half
                if half == 0:
                    tile_of(Lin(u0), Lin(m0), a_hi, a_lo, True)
                    pe.wait_ge(S["nrs_ready"], 3)
                    spread(psum[:, 4:6, :].rearrange("p a b -> p (a b)"), stat_at(N_RS, 5), TOKENS2, S["nrb_ready"])
                    tile_of(Lin(u0 + 1), Lin(m0 + 1), a_hi, a_lo, True)
                with pe.Fori(0, 7 + half) as i:
                    for j in range(2):
                        m = Lin(2 * (1 - half) + j, 2, i)
                        tile_of(m + u0, m + m0, a_hi, a_lo, True)
                pe.wait_ge(S["fl_ready"], 16 * (half + 1))
                with pe.Fori(0, 4) as i:
                    for m in (Lin(0, 2, i), Lin(1, 2, i)):
                        for k in range(2):
                            tile_of(m * 2 + (u0 + 16 + k), m + (m0 + 16), b_hi, b_lo, True, k * KT, k == 0, k == 1)
            pe.wait_ge(S["acc_read"], M_MLP + 48)
            for i in range(NT):
                if i >= 2:
                    pe.wait_ge(S["o_done"], i - 1)
                for k in range(KT):
                    ins = tp(psum[:, 4 + 2 * (i % 2) + k // 4, P * (k % 4):P * (k % 4) + P],
                             h[:, k, META + P * i:META + P * i + P], ident)
                ins.then_inc(S["otp_ready"], 1)

        @block.scalar
        def _(act):
            own = Steps(act, S["act_own"])
            ac = nc.scalar.activation

            def hi(u):
                act.wait_ge(S[f"raw{u.par}"], (u.half * 16 + 16).v)
                if u.reg is not None or u.c >= 2:
                    act.wait_ge(S["unit_done"], (u - 1).v)
                ac(w_hi[:, u.par, :, :], w_raw[:, u.par, :, :], ACT.Copy).then_inc(S["hi_ready"], 1)

            def root(out, in_, eps, scale, ready):
                ac(out, in_, ACT.Sqrt, scale=scale, bias=eps[0:out.shape[0], :]).then_inc(ready, 1)

            act.wait_ge(S["par_in"], 16)
            hi(Lin(0))
            for k in range(KT):
                act.wait_ge(S["x_tp"], k + 1)
                ac(a_hi[:, k, 0:SEQ], bank(2 + k % 4), ACT.Copy,
                   scale=par[:, C_ANORM + k:C_ANORM + k + 1]).then_inc(S["x_hi"], 1)
            for i in range(NT):
                ins = ac(b_hi[:, 2 * i:2 * i + 2, 0:SEQ], x_tok[:, i, :].rearrange("p (a b) -> p a b", a=2), ACT.Square,
                         accum_out=stat[:, X_SUM + i:X_SUM + i + 1])
            ins.then_inc(S["xsum_ready"], 1)
            act.wait_ge(S["xsum_ready"], 1)
            act.wait_ge(S["consts_set"], 3)
            root(stat_at(X_SD), stat_at(X_SUM), eps1, 1.0 / D, S["xsd_ready"])
            hi(Lin(1))
            act.wait_ge(S["rb_ready"], 1)
            ac(rt[:, 0:SEQ], bank(7), ACT.Copy).then_inc(S["rt_ready"], 1)
            act.wait_ge(S["dt_pre"], 1)
            own.mark(ac(dts[1][96:128, :], dts[0][96:128, :], ACT.Abs, bias=par[96:128, C_DTB:C_DTB + 1]))
            ac(dts[1][96:128, :], dts[1][96:128, :], ACT.Exp, scale=-1.0).then_inc(S["dt_exp"], 1)
            ac(stat[96:128, EA:EA + 1], par[96:128, C_ALOG:C_ALOG + 1], ACT.Exp).then_inc(S["dt_exp"], 1)

            def silu(g, j, old=None):
                if j < 2:
                    act.wait_ge(S["acc_read"], (g * 6 + (M_MAMBA + j + 1)).v)
                    dst = sz[:, g.par, SEQ * j:SEQ * j + SEQ]
                else:
                    act.wait_ge(S["pre_silu"], (g * 4 + (j - 1)).v)
                    if old is not None:
                        act.wait_ge(S[{2: "cb_ready", 3: "y_ready", 4: "u_ready", 5: "u_ready"}[j]], (old + 1).v)
                    dst = sx[:, j - 2, :]
                ac(dst, conv[:, j % 2, :], ACT.Silu).then_inc(S["silu_done"], 1)

            def group(g, project=True):
                u, s = g * 6 + U_MAMBA, g - 1
                first = s.reg is None and s.c == 0
                silu(s, 5, None if first else s - 1)
                hi(u + 1)
                act.wait_ge(S["seg_ready"], (s + 1).v)
                ac(mix, mix, ACT.Exp).then_inc(S["mexp_ready"], 1)
                ac(stat[:, DEC:DEC + 8].rearrange("p (h c) -> p h c", h=HPG),
                   decay_in[:, :, 1:3, P - 1], ACT.Exp).then_inc(S["dec_ready"], 1)
                for r in range(HPG):
                    rows = slice(64 * (r % 2), 64 * (r % 2) + 64)
                    ac(edec[rows, r // 2, :].rearrange("p (c l) -> p c l", l=P), decay_in[rows, r, 1:NT, :],
                       ACT.Exp).then_inc(S["e_ready"], 1)
                if project:
                    silu(g, 0)
                    hi(u + 2)
                act.wait_ge(S["cb_ready"], (s + 1).v)
                ac(b_tok.rearrange("p c n -> p (c n)"), bank(2)[:, 0:(NT - 1) * P],
                   ACT.Copy).then_inc(S["bt_ready"], 1)
                if project:
                    silu(g, 1)
                    hi(u + 3)
                    silu(g, 2, s)
                    hi(u + 4)
                    silu(g, 3, s)
                    hi(u + 5)
                act.wait_ge(S["u_ready"], (s + 1).v)
                ac(gsq, y, ACT.Square).then_inc(S["gsq_ready"], 1)
                if project:
                    silu(g, 4, s)
                    hi(u + 6)
                act.wait_ge(S["gst_ready"], (s + 1).v)
                root(stat_at(G_SD), bank(6)[:, 0:NT], eps1, 1.0 / 256, S["gsd_ready"])
                act.wait_ge(S["un_ready"], (s + 1).v)
                for j in range(2):
                    ac(b_hi[:, ds((s * 2 + j).v, 1), 0:SEQ].rearrange("p a b -> p (a b)"), gun[:, j, :], ACT.Copy,
                       scale=ggate[:, 2 + j:3 + j]).then_inc(S["uh_ready"], 1)

            g, u = Lin(0), Lin(U_MAMBA)
            hi(u + 1)
            silu(g, 0)
            hi(u + 2)
            silu(g, 1)
            hi(u + 3)
            act.wait_ge(S["dt_acs"], 2)
            ac(dts[7][96:128, :], dts[7][96:128, :], ACT.Exp).then_inc(S["dt_endexp"], 1)
            silu(g, 2)
            hi(u + 4)
            silu(g, 3)
            hi(u + 5)
            silu(g, 4)
            hi(u + 6)
            act.wait_ge(S["dt_tp"], 1)
            ac(tok[:, :, :, :].rearrange("p a b c -> p (a b c)"), bank(6)[:, 0:3 * P], ACT.Copy
               ).then_inc(S["tok_ready"], 1)
            group(Lin(1))
            with act.Fori(0, 3) as i:
                group(Lin(2, 2, i))
                group(Lin(3, 2, i))
            group(Lin(8), project=False)

            with act.Fori(0, 4) as i:
                for m in (Lin(0, 2, i), Lin(1, 2, i)):
                    u = m * 2 + U_WOUT
                    hi(u + 2)
                    hi(u + 3)
                    act.wait_ge(S["acc_read"], (m + (M_WOUT + 1)).v)
                    ac(row(sq, m, 0, SEQ), row(h, m, META, T2), ACT.Square).then_inc(S["sq_ready"], 1)
                    ac(row(a_hi, m, 0, SEQ), row(h, m, META, T2), ACT.Copy,
                       scale=par[:, ds((m + C_KVN).v, 1)]).then_inc(S["ah_ready"], 1)
            act.wait_ge(S["nst_ready"], 1)
            root(stat_at(N_SD), bank(7)[:, 0:NT], eps1, 1.0 / D, S["nsd_ready"])
            act.wait_ge(S["unit_done"], U_ATT)
            for k in range(KT):
                ac(b_hi[:, k, 0:SEQ], h[:, k, META:T2], ACT.Copy,
                   scale=par[:, C_BN + k:C_BN + k + 1]).then_inc(S["bh_ready"], 1)
            act.wait_ge(S["nrb_ready"], 1)
            ac(rt[:, 0:SEQ], bank(6), ACT.Copy).then_inc(S["nrt_ready"], 1)
            act.wait_ge(S["lam_sum"], 1)
            ac(stat_at(LAMS, 2), stat_at(LAMS, 2), ACT.Exp).then_inc(S["lam_exp"], 1)

            def exps(s, q):
                n = P * (q + 1)
                act.wait_ge(S["mx_ready"], (s * NT + (q + 1)).v)
                own.mark(ac(stat_at(A_NB + 2 * q, 2), stat_at(A_MX + 2 * q, 2), ACT.Copy, scale=-0.125))
                for i in range(2):
                    part = asc[:, P * q * (q + 1) + n * i:P * q * (q + 1) + n * i + n]
                    ac(part, part, ACT.Exp, bias=stat_at(A_NB + 2 * q + i, 1), scale=0.125,
                       accum_out=stat_at(A_SUM + 2 * q + i, 1)).then_inc(S["ex_ready"], 1)

            def copy_weights(b, q0, q1, s, n):
                first, last = q0 * (q0 + 1) // 2, q1 * (q1 + 1) // 2
                act.wait_ge(S["wt_tp"], (s * 3 + n).v)
                ac(awt[:, first:last, :].rearrange("p a b -> p (a b)"), bank(b)[:, 0:P * (last - first)],
                   ACT.Copy).then_inc(S["wt_ready"], 1)

            def out_high(f):
                act.wait_ge(S["og_ready"], (f + 1).v)
                ac(row(b_hi, f + KT, 0, SEQ), aog, ACT.Copy, scale=spl[:, 5, 0:1]).then_inc(S["oh_ready"], 1)

            def head(n, project=True, attend=True, finish=True):
                u, m, s, f = n * 4 + U_ATT, n * 4 + M_ATT, n - 1, n - 2
                prep = hi if project else (lambda u: None)
                prep(u + 2)
                if attend:
                    exps(s, 0)
                    exps(s, 1)
                prep(u + 3)
                if attend:
                    exps(s, 2)
                    exps(s, 3)
                    copy_weights(6, 0, 2, s, 1)
                prep(u + 4)
                if project:
                    act.wait_ge(S["vt_tp"], (n + 1).v)
                    ac(avt[:, n.par, :, :].rearrange("p a b -> p (a b)"), bank(2), ACT.Copy
                       ).then_inc(S["vt_ready"], 1)
                if finish:
                    out_high(f)
                prep(u + 5)
                if attend:
                    copy_weights(4, 2, 3, s, 2)
                    copy_weights(5, 3, 4, s, 3)
                if project:
                    act.wait_ge(S["acc_read"], (m + 4).v)
                    ac(asg[:, n.par, :], agt, ACT.Silu).then_inc(S["sg_ready"], 1)
                if attend:
                    act.wait_ge(S["o_ready"], (s + 1).v)
                    for q in range(NT):
                        ins = ac(afm2[:, P * q:P * q + P], bank(7)[:, P * q:P * q + P], ACT.Square,
                                 accum_out=stat_at(O_SUM + q, 1))
                    own.mark(ins)
                    root(stat_at(O_SD), stat_at(O_SUM), eps1, 1.0 / P, S["osd_ready"])

            head(Lin(0), attend=False, finish=False)
            head(Lin(1), finish=False)
            with act.Fori(0, 3) as i:
                own.enter(i, 10)
                head(Lin(2, 2, i))
                head(Lin(3, 2, i))
                own.leave(3)
            head(Lin(8), project=False)
            out_high(Lin(7))

            act.wait_ge(S["acc_read"], M_ATT + 4 * HEADS)
            ac(sq[:, :, 0:META], h[:, :, 0:META], ACT.Square).then_inc(S["meta_sq"], 1)
            own.mark(ac(spl[:, 0, :], par[:, C_LAM:C_LAM + 4], ACT.Abs))
            ac(spl[:, 0, :], spl[:, 0, :], ACT.Exp, scale=-1.0).then_inc(S["sp_exp"], 1)
            with act.Fori(0, 4) as i:
                for m in (Lin(0, 2, i), Lin(1, 2, i)):
                    hi(m + (U_BOUT + 2))
                    act.wait_ge(S["acc_read"], (m + (M_BOUT + 1)).v)
                    ac(row(a_hi, m, META, T2), row(h, m, META, T2), ACT.Copy,
                       scale=col(gfm, m)).then_inc(S["yh_ready"], 1)
                    ac(row(sq, m, META, T2), row(h, m, META, T2), ACT.Square).then_inc(S["sq_ready"], 1)
                    ac(row(sq2, m, 0, SEQ), row(h, m, META, T2), ACT.Square,
                       scale=par[:, ds((m + C_FIN).v, 1)]).then_inc(S["s2_ready"], 1)
            act.wait_ge(S["nst_ready"], 2)
            ac(stat[0:META, N_SD + 4:N_SD + 5], psum[0:META, 7, 8:9], ACT.Sqrt, scale=1.0 / D,
               bias=eps2[0:META, :]).then_inc(S["act_own"], 1)
            own.n += 1
            root(stat_at(N_SD), bank(7)[:, 0:NT], eps1, 1.0 / D, S["nsd_ready"])
            act.wait_ge(S["r1_ready"], 1)
            root(stat_at(N_SD), stat_at(N_R2), eps2, 1.0 / D, S["nsd_ready"])
            hi(Lin(U_IN2 + 2))
            act.wait_ge(S["rrb_ready"], 3)
            ac(rr[:, META:T2], bank(4), ACT.Copy).then_inc(S["rr_ready"], 1)
            ac(rr[:, 0:META], bank(6)[:, 0:META], ACT.Copy).then_inc(S["rr_ready"], 1)
            ac(rt[:, META:T2], bank(5), ACT.Copy).then_inc(S["rr_ready"], 1)

            def gate_sigmoids(j):
                act.wait_ge(S["rg_ready"], j + 1)
                if j >= 2:
                    act.wait_ge(S["scan_ready"], j - 1)
                for a, c in enumerate((C_BA, C_BX)):
                    ac(halves(rtmp[:, 4 * (j % 2) + a, :]), psum[:, 4 + 2 * a:6 + 2 * a, 0:HALF2], ACT.Sigmoid,
                       bias=par[:, c + j:c + j + 1]).then_inc(S["rga_ready"] if a else S["act_own"], 1)
                own.n += 1

            def gate_exps(js):
                own.wait()
                act.wait_ge(S["sp_done"], 1)
                for j in js:
                    r = rtmp[:, 4 * (j % 2), :]
                    ac(rtmp[:, 4 * (j % 2) + 2, :], r, ACT.Exp, scale=rga[:, 0, j:j + 1]).then_inc(S["at_ready"], 1)
                    ac(rtmp[:, 4 * (j % 2) + 3, :], r, ACT.Tanh, scale=rga[:, 1, j:j + 1]).then_inc(S["at_ready"], 1)
                for j in js:
                    act.wait_ge(S["m2_ready"], j + 1)
                    m2 = rtmp[:, 4 * (j % 2) + 3, :]
                    ac(m2, m2, ACT.Sqrt).then_inc(S["mu_ready"], 1)

            for n in range(14):
                if n:
                    hi(Lin(U_IN2 + n + 2))
                if n in (1, 3):
                    act.wait_ge(S["acc_read"], M_IN2 + n + 1)
                    ac(bgt, bgt, ACT.Sigmoid).then_inc(S["bg_ready"], 1)
                if 6 <= n < 10:
                    gate_sigmoids(n - 6)
                if n in (7, 9):
                    gate_exps((n - 7, n - 6))
                if n == 11:
                    act.wait_ge(S["acc_read"], M_IN2 + 12)
                    for j in range(4):
                        ac(cg[:, j, :], cg[:, j, :], ACT.Gelu_apprx_tanh).then_inc(S["ge_ready"], 1)
            for j in range(4):
                act.wait_ge(S["yc_ready"], j + 1)
                ac(b_hi[:, 4 + j, :], xc[:, j, :], ACT.Copy).then_inc(S["yh_ready"], 1)
            act.wait_ge(S["poolm_ready"], 1)
            for j in range(2):
                ac(halves(b_hi[:, j, :]), psum[:, 2 * j:2 * j + 2, 0:HALF2], ACT.Copy,
                   scale=par[:, C_PSC + j:C_PSC + j + 1]).then_inc(S["yh_ready"], 1)
            act.wait_ge(S["ln_stat"], 1)
            root(stat_at(N_SD, 5), bnag[:, :, 1], eps2, 1.0, S["ln_sd"])
            act.wait_ge(S["lnb_tp"], 1)
            for j in range(2):
                ac(dwo[:, j, :], psum[:, 2 * j:2 * j + 2, :].rearrange("p a b -> p (a b)")[:, 0:T2], ACT.Silu,
                   scale=par[:, C_LNG + j:C_LNG + j + 1],
                   bias=par[:, C_LNB + j:C_LNB + j + 1]).then_inc(S["cs_ready"], 1)
            act.wait_ge(S["pwm_ready"], 1)
            for j in range(2):
                ac(halves(b_hi[:, 2 + j, :]), psum[:, 4 + 2 * j:6 + 2 * j, 0:HALF2], ACT.Copy
                   ).then_inc(S["yh_ready"], 1)
            with act.Fori(0, 4) as i:
                for m in (Lin(0, 2, i), Lin(1, 2, i)):
                    hi(m + (U_OUT2 + 2))
                    act.wait_ge(S["acc_read"], (m + (M_OUT2 + 1)).v)
                    ac(row(a_hi, m, 0, T2), row(h, m, 0, T2), ACT.Copy,
                       scale=par[:, ds((m + C_MLP).v, 1)]).then_inc(S["ah_ready"], 1)
                    ac(row(sq, m, 0, T2), row(h, m, 0, T2), ACT.Square).then_inc(S["sq_ready"], 1)

            act.wait_ge(S["nst_ready"], 3)
            ac(stat[0:META, N_SD + 4:N_SD + 5], psum[0:META, 7, 4:5], ACT.Sqrt, scale=1.0 / D,
               bias=eps2[0:META, :]).then_inc(S["act_own"], 1)
            own.n += 1
            root(stat_at(N_SD), bank(7)[:, 0:NT], eps2, 1.0 / D, S["nsd_ready"])
            hi(Lin(U_MLP + 2))
            act.wait_ge(S["nrb_ready"], 2)
            ac(rt[:, :], psum[:, 4:6, :].rearrange("p a b -> p (a b)")[:, 0:T2], ACT.Copy
               ).then_inc(S["nrt_ready"], 1)

            def up(m, half, prep=True):
                if prep:
                    hi(m + (U_MLP + 32 * half + 2))
                act.wait_ge(S["acc_read"], (m + (M_MLP + 24 * half + 1)).v)
                ac(row(b_hi, m, 0, T2), ft, ACT.Square).then_inc(S["fh_ready"], 1)

            def down(m, half):
                hi(m * 2 + (U_MLP + 32 * half + 18))
                hi(m * 2 + (U_MLP + 32 * half + 19))

            up(Lin(0), 0, prep=False)
            up(Lin(1), 0)
            for half in range(2):
                with act.Fori(0, 7 + half) as i:
                    for j in range(2):
                        up(Lin(2 * (1 - half) + j, 2, i), half)
                with act.Fori(0, 4 - half) as i:
                    for m in (Lin(0, 2, i), Lin(1, 2, i)):
                        down(m, half)
            down(Lin(6), 1)
            for i in range(NT):
                act.wait_ge(S["otp_ready"], i + 1)
                own.mark(ac(scratch, psum[:, 4 + 2 * (i % 2):6 + 2 * (i % 2), :].rearrange("p a b -> p (a b)"),
                            ACT.Square, accum_out=stat_at(O_SUM + i, 1)))
                root(stat_at(O_SD + i, 1), stat_at(O_SUM + i, 1), eps2, 1.0 / D, S["osum_ready"])

        @block.vector
        def _(dve):
            own = Steps(dve, S["dve_own"])
            tt, ts, stt, cp = (nc.vector.tensor_tensor, nc.vector.tensor_scalar, nc.vector.scalar_tensor_tensor,
                               nc.vector.tensor_copy)

            def f32(v):
                return v.bitcast(F32)

            def lo(u):
                dve.wait_ge(S["hi_ready"], (u + 1).v)
                tt(w_lo[:, u.par, :, :], w_raw[:, u.par, :, :], f32(w_hi[:, u.par, :, :]), ALU.subtract
                   ).then_inc(S["lo_ready"], 1)

            def log1p_of(e, w, z, z2, mx, out):
                own.mark(ts(w, e, 2.0, None, ALU.add))
                own.mark(nc.vector.reciprocal(w, w))
                own.mark(tt(z, e, w, ALU.mult))
                own.mark(tt(z2, z, z, ALU.mult))
                own.mark(ts(out, z2, 1.0 / (2 * LOG1P_TERMS + 1), None, ALU.mult))
                for k in range(LOG1P_TERMS - 1, 0, -1):
                    own.mark(stt(out, out, 1.0 / (2 * k + 1), z2, ALU.add, ALU.mult))
                own.mark(stt(out, out, 1.0, z, ALU.add, ALU.mult))
                own.mark(stt(out, out, 2.0, mx, ALU.mult, ALU.add))

            nc.vector.memset(stat[:, :], 1.0).then_inc(S["consts_set"], 1)
            nc.vector.memset(pre[:, 0:3], 0.0).then_inc(S["consts_set"], 1)
            nc.vector.memset(one, 1.0).then_inc(S["consts_set"], 1)
            nc.vector.memset(eps1, EPS1).then_inc(S["consts_set"], 1)
            nc.vector.memset(eps2, EPS2).then_inc(S["consts_set"], 1)
            dve.wait_ge(S["par_in"], 16)
            dve.wait_ge(S["con_in"], 16)
            own(tt(gfm[:, :], par[:, C_FIN:C_FIN + KT], par[:, C_MIX:C_MIX + KT], ALU.mult))
            own(cp(gconv[:, :], par[:, C_GROUP:C_GROUP + 20]))
            own(ts(spl[:, 5, 0:1], par[:, C_SUBG:C_SUBG + 1], 1.0 - LAMBDA_INIT, None, ALU.mult))
            lo(Lin(0))
            for k in range(KT):
                dve.wait_ge(S["x_hi"], k + 1)
                stt(a_lo[:, k, 0:SEQ], bank(2 + k % 4), par[:, C_ANORM + k:C_ANORM + k + 1],
                    f32(a_hi[:, k, 0:SEQ]), ALU.mult, ALU.subtract).then_inc(S["x_lo"], 1)
                cp(h[:, k, META:T2], bank(2 + k % 4)).then_inc(S["x_cp"], 1)
            dve.wait_ge(S["xsd_ready"], 1)
            nc.vector.reciprocal(stat_at(X_RS), stat_at(X_SD)).then_inc(S["rs_ready"], 1)
            lo(Lin(1))
            dve.wait_ge(S["meta_tp"], 1)
            cp(h[:, :, 0:META], bank(6)[:, 0:KT * META].rearrange("p (a b) -> p a b", a=KT)
               ).then_inc(S["meta_cp"], 1)

            rows = slice(96, 128)
            d = [v[rows, :] for v in dts]
            dve.wait_ge(S["rt_ready"], 1)
            dve.wait_ge(S["unit_done"], 1)
            tt(d[0], psum[rows, 0, :], rt[rows, 0:SEQ], ALU.mult).then_inc(S["acc_read"], 1)
            dve.wait_ge(S["acc_read"], 1)
            ts(d[2], d[0], par[rows, C_DTB:C_DTB + 1], 0.0, ALU.add, ALU.max).then_inc(S["dt_pre"], 1)
            lo(Lin(U_MAMBA + 1))

            def conv_tile(g, j, between=None):
                n, m = g * 6 + j, g * 6 + (M_MAMBA + j)
                dve.wait_ge(S["unit_done"], (g * 6 + (U_MAMBA + j + 1)).v)
                if n.reg is not None or n.c >= 2:
                    dve.wait_ge(S["silu_done"], (n - 1).v)
                if j < 2:
                    tt(conv[:, j, :], acc(m), rt[:, 0:SEQ], ALU.mult).then_inc(S["acc_read"], 1)
                    return
                c = conv[:, j % 2, :]
                w = [gconv[:, 5 * (j - 2) + k:5 * (j - 2) + k + 1] for k in range(5)]
                tt(pre[:, 3:3 + SEQ], acc(m), rt[:, 0:SEQ], ALU.mult).then_inc(S["acc_read"], 1)
                dve.wait_ge(S["acc_read"], (m + 1).v)
                own.mark(ts(c, pre[:, 3:3 + SEQ], w[3], w[4], ALU.mult, ALU.add))
                own.mark(stt(c, pre[:, 2:2 + SEQ], w[2], c, ALU.mult, ALU.add))
                own.mark(stt(c, pre[:, 1:1 + SEQ], w[1], c, ALU.mult, ALU.add))
                stt(c, pre[:, 0:SEQ], w[0], c, ALU.mult, ALU.add).then_inc(S["pre_silu"], 1)

            g = Lin(0)
            conv_tile(g, 0)
            dve.wait_ge(S["dt_exp"], 2)
            log1p_of(d[1], d[3], d[3], d[4], d[2], d[5])
            own.mark(ts(d[0], d[5], stat[rows, EA:EA + 1], -1.0, ALU.mult, ALU.mult))
            for c in range(NT):
                ins = nc.vector.tensor_tensor_scan(d[6][:, P * c:P * c + P], cst[rows, 0:1].to_broadcast([32, P]),
                                                   d[0][:, P * c:P * c + P], 0.0, ALU.mult, ALU.add)
            ins.then_inc(S["dt_acs"], 1)
            lo(Lin(U_MAMBA + 2))
            dve.wait_ge(S["dt_acs"], 1)
            for c in range(NT):
                ins = ts(d[7][:, P * c:P * c + P], d[6][:, P * c:P * c + P], d[6][:, P * c + P - 1:P * c + P], -1.0,
                         ALU.subtract, ALU.mult)
            ins.then_inc(S["dt_acs"], 1)
            conv_tile(g, 1)
            lo(Lin(U_MAMBA + 3))
            dve.wait_ge(S["dt_endexp"], 1)
            tt(d[7], d[7], d[5], ALU.mult).then_inc(S["dt_tok"], 1)
            conv_tile(g, 2)
            lo(Lin(U_MAMBA + 4))
            conv_tile(g, 3)
            lo(Lin(U_MAMBA + 5))
            conv_tile(g, 4)
            lo(Lin(U_MAMBA + 6))
            dve.wait_ge(S["tok_ready"], 1)

            def group(g, project=True):
                u, s = g * 6 + U_MAMBA, g - 1
                conv_tile(s, 5)
                lo(u + 1)
                own(cp(ggate[:, :], par[:, ds((s * GW + (C_GROUP + 20)).v, 4)]))
                own.mark(cp(gtok[:, :, :, :], tok[:, :, :, ds((s * HPG).v, HPG)]))
                dve.wait_ge(S["ab_in"], (s * 16 + 16).v)
                for r in range(HPG):
                    for c in range(NT):
                        ins = ts(mix[:, r, c, :], decay_in[:, r, c, :], gtok[:, 0, c, r:r + 1], 0.0,
                                 ALU.subtract, ALU.min)
                ins.then_inc(S["seg_ready"], 1)
                if project:
                    own(cp(gconv[:, :], par[:, ds((g * GW + C_GROUP).v, 20)]))
                    conv_tile(g, 0)
                    lo(u + 2)
                dve.wait_ge(S["tpx_ready"], (s + 1).v)
                xt = psum[:, 4:6, :].rearrange("p b (c r f) -> p (b c) r f", c=2, r=HPG)
                own(tt(xdt.rearrange("p c (r f) -> p c r f", r=HPG), xt,
                       gtok[:, 1, :, :].unsqueeze(3).to_broadcast([P, NT, HPG, 64]), ALU.mult))
                own(tt(xend.rearrange("p c (r f) -> p c r f", r=HPG), xt[:, 0:NT - 1],
                       gtok[:, 2, 0:NT - 1, :].unsqueeze(3).to_broadcast([P, NT - 1, HPG, 64]), ALU.mult))
                dve.wait_ge(S["cb_ready"], (s + 1).v)
                own.mark(tt(cb, bank(3).rearrange("p (c l) -> p c l", c=NT),
                            causal.unsqueeze(1).to_broadcast([P, NT, P]), ALU.mult))
                dve.wait_ge(S["mexp_ready"], (s + 1).v)
                tt(mix, mix, cb.unsqueeze(1).to_broadcast([P, HPG, NT, P]), ALU.mult).then_inc(S["m_ready"], 1)
                if project:
                    conv_tile(g, 1)
                    lo(u + 3)
                dve.wait_ge(S["st_ready"], (s + 1).v)
                dve.wait_ge(S["dec_ready"], (s + 1).v)
                own.mark(cp(state[:, 0, :], bank(2)[:, 0:256]))
                for c in (1, 2):
                    dec = stat[:, DEC + c - 1:DEC + 8:2].unsqueeze(2).to_broadcast([P, HPG, 64])
                    own.mark(tt(state[:, c, :].rearrange("p (r f) -> p r f", r=HPG),
                                state[:, c - 1, :].rearrange("p (r f) -> p r f", r=HPG), dec, ALU.mult))
                    ins = tt(state[:, c, :], state[:, c, :], bank(2 + c // 2)[:, 256 * (c % 2):256 * (c % 2) + 256],
                             ALU.add)
                    if c == 1:
                        own.mark(ins)
                    else:
                        ins.then_inc(S["s_ready"], 1)
                if project:
                    conv_tile(g, 2)
                    lo(u + 4)
                dve.wait_ge(S["y_ready"], (s + 1).v)
                dve.wait_ge(S["e_ready"], (s * HPG + HPG).v)
                for j in range(2):
                    own(stt(y[:, j, :], sx[:, 2 + j, :], ggate[:, j:j + 1], bank(4 + j), ALU.mult, ALU.add))
                own.mark(tt(yoff, psum[:, 6:8, P:SEQ], edec, ALU.mult))
                if project:
                    conv_tile(g, 3)
                    lo(u + 5)
                own.mark(tt(y[:, :, P:SEQ], y[:, :, P:SEQ], yoff, ALU.add))
                dve.wait_ge(S["silu_done"], (s * 6 + 2).v)
                tt(y, y, sz[:, s.par, :].rearrange("p (a b) -> p a b", a=2), ALU.mult).then_inc(S["u_ready"], 1)
                if project:
                    conv_tile(g, 4)
                    lo(u + 6)
                dve.wait_ge(S["gsd_ready"], (s + 1).v)
                nc.vector.reciprocal(stat_at(G_RS), stat_at(G_SD)).then_inc(S["grs_ready"], 1)
                dve.wait_ge(S["grb_ready"], (s + 1).v)
                tt(gun, y, bank(7).unsqueeze(1).to_broadcast([P, 2, SEQ]), ALU.mult).then_inc(S["un_ready"], 1)
                dve.wait_ge(S["uh_ready"], (s * 2 + 2).v)
                for j in range(2):
                    ins = stt(row(b_lo, s * 2 + j, 0, SEQ), gun[:, j, :], ggate[:, 2 + j:3 + j],
                              f32(row(b_hi, s * 2 + j, 0, SEQ)), ALU.mult, ALU.subtract)
                ins.then_inc(S["ul_ready"], 1)

            group(Lin(1))
            with dve.Fori(0, 3) as i:
                own.enter(i, GROUP_STEPS)
                group(Lin(2, 2, i))
                group(Lin(3, 2, i))
                own.leave(3)
            group(Lin(8), project=False)

            with dve.Fori(0, 4) as i:
                for m in (Lin(0, 2, i), Lin(1, 2, i)):
                    u = m * 2 + U_WOUT
                    lo(u + 2)
                    dve.wait_ge(S["unit_done"], (u + 2).v)
                    tt(row(h, m, META, T2), row(h, m, META, T2), acc(m + M_WOUT), ALU.add).then_inc(S["acc_read"], 1)
                    lo(u + 3)
                    dve.wait_ge(S["ah_ready"], (m + 1).v)
                    stt(row(a_lo, m, 0, SEQ), row(h, m, META, T2), par[:, ds((m + C_KVN).v, 1)],
                        f32(row(a_hi, m, 0, SEQ)), ALU.mult, ALU.subtract).then_inc(S["al_ready"], 1)
            dve.wait_ge(S["nsd_ready"], 1)
            nc.vector.reciprocal(stat_at(N_RS), stat_at(N_SD)).then_inc(S["nrs_ready"], 1)
            for k in range(KT):
                dve.wait_ge(S["bh_ready"], k + 1)
                stt(b_lo[:, k, 0:SEQ], h[:, k, META:T2], par[:, C_BN + k:C_BN + k + 1],
                    f32(b_hi[:, k, 0:SEQ]), ALU.mult, ALU.subtract).then_inc(S["bl_ready"], 1)
            dve.wait_ge(S["lam_in"], 16)
            lv = lamt.rearrange("p (a b d) -> p a b d", a=2, b=2)
            own.mark(tt(lamp, lv[:, :, 0, :], lv[:, :, 1, :], ALU.mult))
            nc.vector.tensor_reduce(stat_at(LAMS, 2), lamp, AX.X, ALU.add).then_inc(S["lam_sum"], 1)
            dve.wait_ge(S["nrt_ready"], 1)

            def evacuate(n, j):
                dve.wait_ge(S["unit_done"], (n * 4 + (U_ATT + j + 1)).v)
                if n.reg is not None or n.c > 0:
                    if j == 1:
                        dve.wait_ge(S["vt_tp"], n.v)
                    if j == 3:
                        dve.wait_ge(S["sg_ready"], n.v)
                dst = (ak[:, n.par, :], afm, aq[:, n.par, :], agt)[j]
                tt(dst, acc(n * 4 + (M_ATT + j)), rt[:, 0:SEQ], ALU.mult).then_inc(S["acc_read"], 1)

            def biased(s, q):
                n, at = P * (q + 1), P * q * (q + 1)
                dve.wait_ge(S["sc_ready"], (s * NT + (q + 1)).v)
                for i in range(2):
                    ins = stt(asc[:, at + n * i:at + n * i + n], dist[:, SEQ - n:SEQ], stat_at(SLOPE, 1),
                              bank(2 + 2 * (q % 2) + i)[:, 0:n], ALU.mult, ALU.add)
                ins.then_inc(S["scs_ready"], 1)
                dve.wait_ge(S["scs_ready"], (s * NT + (q + 1)).v)
                nc.vector.tensor_reduce(stat_at(A_MX + 2 * q, 2), asc[:, at:at + 2 * n].rearrange(
                    "p (a b) -> p a b", a=2), AX.X, ALU.max).then_inc(S["mx_ready"], 1)

            def weigh(s, q):
                n, at = P * (q + 1), P * q * (q + 1)
                dve.wait_ge(S["ex_ready"], (s * 8 + (2 * q + 2)).v)
                own.mark(nc.vector.reciprocal(stat_at(A_RC + 2 * q, 2), stat_at(A_SUM + 2 * q, 2)))
                own.mark(ts(asc[:, at + n:at + 2 * n], asc[:, at + n:at + 2 * n], stat_at(A_RC + 2 * q + 1, 1),
                            stat_at(LAM, 1), ALU.mult, ALU.mult))
                stt(asc[:, at:at + n], asc[:, at:at + n], stat_at(A_RC + 2 * q, 1), asc[:, at + n:at + 2 * n],
                    ALU.mult, ALU.add).then_inc(S["w_ready"], 1)

            def gate_out(f):
                dve.wait_ge(S["ont_ready"], (f + 1).v)
                dve.wait_ge(S["sg_ready"], (f + 1).v)
                tt(aog, bank(3), asg[:, f.par, :], ALU.mult).then_inc(S["og_ready"], 1)

            def out_low(f):
                dve.wait_ge(S["oh_ready"], (f + 1).v)
                stt(row(b_lo, f + KT, 0, SEQ), aog, spl[:, 5, 0:1], f32(row(b_hi, f + KT, 0, SEQ)),
                    ALU.mult, ALU.subtract).then_inc(S["ol_ready"], 1)

            def head(n, project=True, attend=True, finish=True):
                u, s, f = n * 4 + U_ATT, n - 1, n - 2
                if project:
                    evacuate(n, 0)
                    lo(u + 2)
                if attend:
                    own.mark(cp(stat_at(SLOPE, 1), con[:, ds((s + K_SLOPE).v, 1)]))
                    biased(s, 0)
                    biased(s, 1)
                if project:
                    evacuate(n, 1)
                    lo(u + 3)
                if attend:
                    biased(s, 2)
                    biased(s, 3)
                    weigh(s, 0)
                    weigh(s, 1)
                if finish:
                    gate_out(f)
                if project:
                    evacuate(n, 2)
                    lo(u + 4)
                if attend:
                    weigh(s, 2)
                    weigh(s, 3)
                if finish:
                    out_low(f)
                if project:
                    evacuate(n, 3)
                    lo(u + 5)
                if attend:
                    dve.wait_ge(S["osd_ready"], (s + 1).v)
                    own.mark(nc.vector.reciprocal(stat_at(O_RS), stat_at(O_SD)))
                    tt(aon.rearrange("p (a b) -> p a b", a=NT), bank(7).rearrange("p (a b) -> p a b", a=NT),
                       stat_at(O_RS).unsqueeze(2).to_broadcast([P, NT, P]), ALU.mult).then_inc(S["on_ready"], 1)

            head(Lin(0), attend=False, finish=False)
            dve.wait_ge(S["lam_exp"], 1)
            dve.wait_ge(S["dist_in"], 16)
            own.mark(stt(stat_at(LAM, 1), stat_at(LAMS + 1, 1), -LAMBDA_INIT, stat_at(LAMS, 1),
                         ALU.add, ALU.subtract))
            head(Lin(1), finish=False)
            with dve.Fori(0, 3) as i:
                own.enter(i, 20)
                head(Lin(2, 2, i))
                head(Lin(3, 2, i))
                own.leave(3)
            head(Lin(8), project=False)
            gate_out(Lin(7))
            out_low(Lin(7))

            own.mark(tt(mg[:, :, :], h[:, :, 0:META],
                        par[:, C_MIX:C_MIX + KT].unsqueeze(2).to_broadcast([P, KT, META]), ALU.mult))
            own.mark(cp(a_hi[:, :, 0:META], mg[:, :, :]))
            own(tt(a_lo[:, :, 0:META], mg[:, :, :], f32(a_hi[:, :, 0:META]), ALU.subtract))
            own(ts(spl[:, 1, :], par[:, C_LAM:C_LAM + 4], -1.0, 0.0, ALU.mult, ALU.max))
            dve.wait_ge(S["sp_exp"], 1)
            log1p_of(spl[:, 0, :], spl[:, 2, :], spl[:, 2, :], spl[:, 3, :], spl[:, 1, :], spl[:, 4, :])
            own(ts(rga[:, 0, :], spl[:, 4, :], -8.0, None, ALU.mult))
            ts(rga[:, 1, :], spl[:, 4, :], 8.0, None, ALU.mult).then_inc(S["sp_done"], 1)
            with dve.Fori(0, 4) as i:
                for m in (Lin(0, 2, i), Lin(1, 2, i)):
                    dve.wait_ge(S["unit_done"], (m + (U_BOUT + 1)).v)
                    tt(row(h, m, META, T2), row(h, m, META, T2), acc(m + M_BOUT), ALU.add).then_inc(S["acc_read"], 1)
                    lo(m + (U_BOUT + 2))
                    dve.wait_ge(S["yh_ready"], (m + 1).v)
                    stt(row(a_lo, m, META, T2), row(h, m, META, T2), col(gfm, m), f32(row(a_hi, m, META, T2)),
                        ALU.mult, ALU.subtract).then_inc(S["yl_ready"], 1)
            dve.wait_ge(S["nsd_ready"], 2)
            own(nc.vector.reciprocal(stat[0:META, N_R2 + 4:N_R2 + 5], stat[0:META, N_SD + 4:N_SD + 5]))
            own.mark(nc.vector.reciprocal(stat_at(N_RS), stat_at(N_SD)))
            own.mark(tt(stat_at(N_R2), stat_at(N_RS), stat_at(N_RS), ALU.mult))
            tt(stat_at(N_R2), stat_at(N_R2), bank(7)[:, 4:8], ALU.mult).then_inc(S["r1_ready"], 1)
            dve.wait_ge(S["nsd_ready"], 3)
            own.mark(nc.vector.reciprocal(stat_at(N_R2), stat_at(N_SD)))
            tt(stat_at(N_R2), stat_at(N_R2), stat_at(N_RS), ALU.mult).then_inc(S["nrs_ready"], 1)
            lo(Lin(U_IN2 + 2))
            own(nc.vector.memset(cu[:, :, 0:DW_K - 1], 0.0))
            own(nc.vector.memset(cxp[:, 0:3], 0.0))
            own(nc.vector.memset(plp[:, :, 0:POOL_PAD], 0.0))
            own.wait()
            dve.wait_ge(S["rr_ready"], 3)

            taps = [(j, k) for j in range(2) for k in range(DW_K)]

            def long_conv(n):
                for j, k in taps[:n]:
                    src = cu[:, j, DW_K - 1 - k:DW_K - 1 - k + T2]
                    w = par[:, C_DWW + DW_K * j + DW_K - 1 - k:C_DWW + DW_K * j + DW_K - k]
                    if k == 0:
                        own.mark(ts(dwo[:, j, :], src, w, par[:, C_DWB + j:C_DWB + j + 1], ALU.mult, ALU.add))
                        continue
                    ins = stt(dwo[:, j, :], src, w, dwo[:, j, :], ALU.mult, ALU.add)
                    if k == DW_K - 1:
                        ins.then_inc(S["dw_ready"], 1)
                    else:
                        own.mark(ins)
                del taps[:n]

            def short_conv(j):
                dve.wait_ge(S["acc_read"], M_IN2 + 5 + j)
                c = xc[:, j, :]
                w = [par[:, C_RGW + 4 * j + k:C_RGW + 4 * j + k + 1] for k in range(4)]
                own.mark(ts(c, cxp[:, 3:3 + T2], w[3], par[:, C_RGB + j:C_RGB + j + 1], ALU.mult, ALU.add))
                own.mark(stt(c, cxp[:, 2:2 + T2], w[2], c, ALU.mult, ALU.add))
                own.mark(stt(c, cxp[:, 1:1 + T2], w[1], c, ALU.mult, ALU.add))
                stt(c, cxp[:, 0:T2], w[0], c, ALU.mult, ALU.add).then_inc(S["xc_ready"], 1)

            def one_minus_a2(j):
                b = 4 * (j % 2)
                dve.wait_ge(S["at_ready"], 2 * j + 2)
                own.mark(tt(rtmp[:, b, :], rtmp[:, b + 2, :], rtmp[:, b + 2, :], ALU.mult))
                stt(rtmp[:, b + 3, :], rtmp[:, b, :], 1.0, rtmp[:, b + 3, :], ALU.add, ALU.mult
                    ).then_inc(S["m2_ready"], 1)

            def scan(j):
                b = 4 * (j % 2)
                dve.wait_ge(S["rga_ready"], j + 1)
                own.mark(tt(rtmp[:, b + 1, :], rtmp[:, b + 1, :], xc[:, j, :], ALU.mult))
                dve.wait_ge(S["mu_ready"], j + 1)
                own.mark(tt(rtmp[:, b + 1, :], rtmp[:, b + 1, :], rtmp[:, b + 3, :], ALU.mult))
                nc.vector.tensor_tensor_scan(xc[:, j, :], rtmp[:, b + 2, :], rtmp[:, b + 1, :], 0.0,
                                             ALU.mult, ALU.add).then_inc(S["scan_ready"], 1)

            def pool_mix(j):
                dve.wait_ge(S["acc_read"], M_IN2 + 13 + j)
                n = POOL_PAD + T2
                a, b = pls[:, 0, :], pls[:, 1, :]
                u = plp[:, j, :]
                own.mark(tt(a[:, 1:n], u[:, 1:n], u[:, 0:n - 1], ALU.add))
                if j == 0:
                    own.mark(tt(b[:, 3:n], a[:, 3:n], a[:, 1:n - 2], ALU.add))
                else:
                    own.mark(tt(b[:, 3:n], a[:, 3:n], a[:, 1:n - 2], ALU.add))
                    own.mark(tt(a[:, 7:n], b[:, 7:n], b[:, 3:n - 4], ALU.add))
                    own.mark(tt(b[:, 15:n], a[:, 15:n], a[:, 7:n - 8], ALU.add))
                for rows, v in ((slice(0, 64), a), (slice(64, 128), b)):
                    x = v[rows, POOL_PAD:POOL_PAD + 16]
                    own(tt(x, x, con[rows, K_INV + 16 * j:K_INV + 16 * j + 16], ALU.mult))
                own.wait()
                for rows, v in ((slice(0, 64), a), (slice(64, 128), b)):
                    own(tt(plp[rows, j, POOL_PAD:POOL_PAD + 16], v[rows, POOL_PAD:POOL_PAD + 16],
                           plp[rows, j, POOL_PAD:POOL_PAD + 16], ALU.subtract))
                    ins = stt(plp[rows, j, POOL_PAD + 16:n], v[rows, POOL_PAD + 16:n],
                              con[rows, K_WIN + j:K_WIN + j + 1], plp[rows, j, POOL_PAD + 16:n],
                              ALU.mult, ALU.subtract)
                    if rows.start:
                        ins.then_inc(S["pool_ready"], 1)
                    else:
                        own(ins)

            for n in range(14):
                dve.wait_ge(S["unit_done"], U_IN2 + n + 1)
                if n < 4:
                    j = n // 2
                    dst = bgt if n % 2 else bvt
                elif n < 8:
                    dst = cxp[:, 3:3 + T2]
                elif n < 12:
                    dst = cg[:, n - 8, :]
                else:
                    dst = plp[:, n - 12, POOL_PAD:POOL_PAD + T2]
                tt(halves(dst), acc2(Lin(M_IN2 + n)), halves(rr), ALU.mult).then_inc(S["acc_read"], 1)
                if n:
                    lo(Lin(U_IN2 + n + 2))
                if n in (1, 3):
                    dve.wait_ge(S["bg_ready"], j + 1)
                    own.mark(tt(cu[:, j, DW_K - 1:DW_K - 1 + T2], bvt, bgt, ALU.mult))
                    long_conv(2)
                if n == 0:
                    for k in range(KT):
                        own(stt(h[:, k, META:T2], h[:, k, META:T2], par[:, C_FIN + k:C_FIN + k + 1], rt[:, META:T2],
                                ALU.mult, ALU.mult))
                if n == 2:
                    long_conv(4)
                if 4 <= n < 8:
                    short_conv(n - 4)
                    long_conv(1)
                if n in (7, 9):
                    one_minus_a2(n - 7)
                    one_minus_a2(n - 6)
                if n in (8, 10):
                    scan(n - 8)
                    scan(n - 7)
                if n in (8, 9, 10, 11):
                    long_conv(5)
                if n == 12:
                    for j in range(4):
                        dve.wait_ge(S["ge_ready"], j + 1)
                        tt(xc[:, j, :], xc[:, j, :], cg[:, j, :], ALU.mult).then_inc(S["yc_ready"], 1)
                if n == 12:
                    own.mark(nc.vector.memset(pls[:, :, 0:1], 0.0))
                if n >= 12:
                    pool_mix(n - 12)
            for j in range(4):
                dve.wait_ge(S["yh_ready"], KT + 1 + j)
                tt(b_lo[:, 4 + j, :], xc[:, j, :], f32(b_hi[:, 4 + j, :]), ALU.subtract).then_inc(S["yl_ready"], 1)
            for j in range(2):
                dve.wait_ge(S["yh_ready"], KT + 5 + j)
                stt(halves(b_lo[:, j, :]), psum[:, 2 * j:2 * j + 2, 0:HALF2], par[:, C_PSC + j:C_PSC + j + 1],
                    f32(halves(b_hi[:, j, :])), ALU.mult, ALU.subtract).then_inc(S["yl_ready"], 1)
            long_conv(len(taps))
            dve.wait_ge(S["ln_tp"], 1)
            own.mark(nc.vector.memset(bnag[:, :, :], 1.0))
            for i, (c0, cn) in enumerate(TOKENS2):
                own(nc.vector.bn_stats(bnst[0:cn, i, :], psum[0:cn, 4 + i // 2, 256 * (i % 2):256 * (i % 2) + 256]))
            own.wait()
            for i, (c0, cn) in enumerate(TOKENS2):
                ins = nc.vector.bn_aggr(bnag[0:cn, i, :], bnst[0:cn, i, :])
            ins.then_inc(S["ln_stat"], 1)
            dve.wait_ge(S["ln_sd"], 1)
            own.mark(nc.vector.reciprocal(stat_at(N_RS, 5), stat_at(N_SD, 5)))
            for i, (c0, cn) in enumerate(TOKENS2):
                ins = ts(lnt[0:cn, i, :], psum[0:cn, 4 + i // 2, 256 * (i % 2):256 * (i % 2) + 256],
                         bnag[0:cn, i, 0:1], stat[0:cn, N_RS + i:N_RS + i + 1], ALU.subtract, ALU.mult)
            ins.then_inc(S["ln_ready"], 1)
            for j in range(2):
                dve.wait_ge(S["yh_ready"], KT + 7 + j)
                tt(halves(b_lo[:, 2 + j, :]), psum[:, 4 + 2 * j:6 + 2 * j, 0:HALF2], f32(halves(b_hi[:, 2 + j, :])),
                   ALU.subtract).then_inc(S["yl_ready"], 1)
            with dve.Fori(0, 4) as i:
                for m in (Lin(0, 2, i), Lin(1, 2, i)):
                    dve.wait_ge(S["unit_done"], (m + (U_OUT2 + 1)).v)
                    hm = halves(row(h, m, 0, T2))
                    tt(hm, hm, acc2(m + M_OUT2), ALU.add).then_inc(S["acc_read"], 1)
                    lo(m + (U_OUT2 + 2))
                    dve.wait_ge(S["ah_ready"], (m + (KT + 1)).v)
                    stt(row(a_lo, m, 0, T2), row(h, m, 0, T2), par[:, ds((m + C_MLP).v, 1)],
                        f32(row(a_hi, m, 0, T2)), ALU.mult, ALU.subtract).then_inc(S["al_ready"], 1)

            dve.wait_ge(S["nsd_ready"], 4)
            nc.vector.reciprocal(stat_at(N_RS, 5), stat_at(N_SD, 5)).then_inc(S["nrs_ready"], 1)
            lo(Lin(U_MLP + 2))
            dve.wait_ge(S["nrt_ready"], 2)

            def up(m, half, prep=True):
                n = m + 16 * half
                dve.wait_ge(S["unit_done"], (m + (U_MLP + 32 * half + 1)).v)
                stt(halves(ft), acc2(m + (M_MLP + 24 * half)), 0.0, halves(rt[:, :]), ALU.max, ALU.mult
                    ).then_inc(S["acc_read"], 1)
                if prep:
                    lo(m + (U_MLP + 32 * half + 2))
                dve.wait_ge(S["acc_read"], (m + (M_MLP + 24 * half + 1)).v)
                own.mark(tt(fs, ft, ft, ALU.mult))
                dve.wait_ge(S["fh_ready"], (n + 1).v)
                tt(row(b_lo, m, 0, T2), fs, f32(row(b_hi, m, 0, T2)), ALU.subtract).then_inc(S["fl_ready"], 1)

            def down(m, half, prep=True):
                u = m * 2 + (U_MLP + 32 * half + 16)
                if prep:
                    lo(u + 2)
                dve.wait_ge(S["unit_done"], (u + 2).v)
                hm = halves(row(h, m, 0, T2))
                tt(hm, hm, acc2(m + (M_MLP + 24 * half + 16)), ALU.add).then_inc(S["acc_read"], 1)
                if prep:
                    lo(u + 3)

            up(Lin(0), 0, prep=False)
            up(Lin(1), 0)
            for half in range(2):
                with dve.Fori(0, 7 + half) as i:
                    own.enter(i, 2)
                    for j in range(2):
                        up(Lin(2 * (1 - half) + j, 2, i), half)
                    own.leave(7 + half)
                with dve.Fori(0, 4 - half) as i:
                    for m in (Lin(0, 2, i), Lin(1, 2, i)):
                        down(m, half)
            down(Lin(6), 1)
            down(Lin(7), 1, prep=False)
            dve.wait_ge(S["gout_in"], 16)
            for i in range(NT):
                dve.wait_ge(S["osum_ready"], i + 1)
                own.mark(nc.vector.reciprocal(stat_at(O_RS + i, 1), stat_at(O_SD + i, 1)))
                if i >= 2:
                    dve.wait_ge(S[f"out{i % 2}"], 16 * (i // 2))
                stt(osb[:, i % 2, :], psum[:, 4 + 2 * (i % 2):6 + 2 * (i % 2), :].rearrange("p a b -> p (a b)"),
                    stat_at(O_RS + i, 1), gout, ALU.mult, ALU.mult).then_inc(S["o_done"], 1)


def ssd_cols(g):
    return [g * 256, g * 256 + P, g * P + 2 * DINNER, g * P + (2 * DINNER + D), g * 256 + DINNER,
            g * 256 + (DINNER + P)]


IN2_TILES = [2, 4, 3, 5, 10, 11, 12, 13, 6, 7, 8, 9, 0, 1]
GROUP_STEPS = 52


def col(v, m):
    return v[:, ds(m.v, 1)]


def row(v, m, c0, c1):
    if m.reg is None:
        return v[:, m.c, c0:c1]
    return v[:, ds(m.v, 1), c0:c1].rearrange("p a b -> p (a b)")


def constants():
    import numpy as np

    con = np.zeros((P, NCONST), np.float32)
    p, j = np.arange(P)[:, None], np.arange(SEQ)[None, :]
    con[:, K_ID:K_ID + P] = np.eye(P)
    con[:, K_CAUSAL:K_CAUSAL + P] = j[:, :P] >= p
    windows = np.array([[2, 8], [4, 16]])
    for t in range(2):
        for half in range(2):
            w = windows[half, t]
            rows = slice(64 * half, 64 * half + 64)
            con[rows, K_INV + 16 * t:K_INV + 16 * t + 16] = 1.0 / np.minimum(np.arange(1, 17), w)
            con[rows, K_WIN + t] = 1.0 / w
    con[:, K_SLOPE:K_SLOPE + HEADS] = -8.0 * 2.0 ** -np.arange(1.0, HEADS + 1)
    return con


def distances():
    import numpy as np

    p, j = np.arange(P)[:, None], np.arange(SEQ)[None, :]
    dist = np.abs(p + (SEQ - P) - j).astype(np.float32)
    dist[(p < 64) & (j >= SEQ - 64)] = 1e30
    return dist


def kernel(**inputs):
    import numpy as np
    import concourse.bacc as bacc
    from concourse.bass_utils import run_bass_kernel_spmd

    x = {k: np.asarray(v) for k, v in inputs.items()}
    par = np.zeros((P, NPAR), np.float32)
    cw, cb = x["a_conv_w"][0].reshape(4, 32, P), x["a_conv_b"][0].reshape(32, P)
    skip = np.repeat(x["a_d_skip"][0], 64).reshape(16, P)
    gate = x["a_gate_norm_g"][0].reshape(16, P)
    for g in range(GROUPS):
        for j, tile in enumerate((16 + g, 24 + g, 2 * g, 2 * g + 1)):
            par[:, GW * g + 5 * j:GW * g + 5 * j + 4] = cw[:, tile].T
            par[:, GW * g + 5 * j + 4] = cb[tile]
        for j in range(2):
            par[:, GW * g + 20 + j] = skip[2 * g + j]
            par[:, GW * g + 22 + j] = gate[2 * g + j]
    for at, name in ((C_ANORM, "a_norm_g"), (C_KVN, "kv_norm_g"), (C_BN, "b_norm_g"), (C_FIN, "final_norm_g"),
                     (C_MIX, "mix_norm_g_2"), (C_MLP, "mlp_norm_g_2"), (C_SUBG, "b_sub_g"), (C_PSC, "pool_scale_2"),
                     (C_DWB, "convb_dw_b_2"), (C_LNG, "convb_ln_g_2"), (C_LNB, "convb_ln_b_2"),
                     (C_RGB, "rg_conv_b_2"), (C_BA, "rg_b_a_2"), (C_BX, "rg_b_x_2"), (C_LAM, "rg_lambda_2")):
        v = x[name].reshape(-1, P).T
        par[:, at:at + v.shape[1]] = v
    par[96:, C_DTB] = x["a_dt_bias"][0]
    par[96:, C_ALOG] = x["a_a_log"][0]
    for j in range(2):
        par[:, C_DWW + DW_K * j:C_DWW + DW_K * j + DW_K] = x["convb_dw_w_2"][0][:, P * j:P * j + P].T
    for j in range(4):
        par[:, C_RGW + 4 * j:C_RGW + 4 * j + 4] = x["rg_conv_w_2"][0][:, P * j:P * j + P].T
    bd = np.zeros((P, 10, P), np.float32)
    for at, name, n in ((0, "pool_w_2", 4), (2, "rg_w_a_2", 8), (6, "rg_w_x_2", 8)):
        for k in range(n):
            o = 64 * (k % 2)
            bd[o:o + 64, at + k // 2, o:o + 64] = x[name][0][k]
    arrays = {
        "x": x["x"][0], "a_w_in": x["a_w_in"][0], "a_w_out": x["a_w_out"][0], "w_kv": x["w_kv"],
        "b_w_in": x["b_w_in"][0], "b_w_out": x["b_w_out"][0], "w_in_2": x["w_in_2"][0], "w_out_2": x["w_out_2"][0],
        "w_up_2": x["w_up_2"][0], "w_down_2": x["w_down_2"][0], "b_lambda": x["b_lambda"],
        "meta_tokens_2": x["meta_tokens_2"], "convb_pw_w_2": x["convb_pw_w_2"][0],
        "final_norm_g_2": x["final_norm_g_2"], "params": par, "blockdiag": bd, "consts": constants(), "dist": distances(),
    }
    arrays = {k: np.ascontiguousarray(v) for k, v in arrays.items()}
    nc = bacc.Bacc("TRN2", target_bir_lowering=False, num_devices=1)
    t = {k: nc.dram_tensor(k, v.shape, F32, kind="ExternalInput").ap() for k, v in arrays.items()}
    t["acs"] = nc.dram_tensor("acs", (32, SEQ), F32, kind="Internal").ap()
    t["out"] = nc.dram_tensor("out", (SEQ, D), F32, kind="ExternalOutput").ap()
    build(nc, t)
    r = run_bass_kernel_spmd(nc, [arrays], core_ids=[0])
    return r.results[0]["out"].reshape(1, SEQ, D)
```

```python
import math
from contextlib import ExitStack

import concourse.bass as bass
from concourse import mybir

ALU = mybir.AluOpType
ACT = mybir.ActivationFunctionType
AX = mybir.AxisListType
F32 = mybir.dt.float32
F32R = mybir.dt.float32r

P = 128
D = 1024
KT = D // P
SEQ = 512
META = 16
T2 = SEQ + META
HALF2 = T2 // 2
NT = SEQ // P
GROUPS = 8
HPG = 4
DINNER = 2048
CONV_DIM = 4096
HEADS = 8
EPS1, EPS2 = 1e-5, 1e-6
LAMBDA_INIT = 0.8 - 0.6 * math.exp(-0.3)
DW_K = 31
POOL_PAD = 16

U_DT = 0
U_MAMBA = 1
U_WOUT = U_MAMBA + 6 * GROUPS
U_ATT = U_WOUT + 16
U_BOUT = U_ATT + 4 * HEADS
U_IN2 = U_BOUT + 8
U_OUT2 = U_IN2 + 14
U_MLP = U_OUT2 + 8
U_END = U_MLP + 64
M_MAMBA = 1
M_WOUT = M_MAMBA + 6 * GROUPS
M_ATT = M_WOUT + 8
M_BOUT = M_ATT + 4 * HEADS
M_IN2 = M_BOUT + 8
M_OUT2 = M_IN2 + 14
M_MLP = M_OUT2 + 8

C_GROUP = 0
GW = 24
C_ANORM = C_GROUP + GW * GROUPS
C_KVN = C_ANORM + 8
C_BN = C_KVN + 8
C_FIN = C_BN + 8
C_MIX = C_FIN + 8
C_MLP = C_MIX + 8
C_SUBG = C_MLP + 8
C_DTB = C_SUBG + 1
C_ALOG = C_DTB + 1
C_PSC = C_ALOG + 1
C_DWW = C_PSC + 2
C_DWB = C_DWW + 2 * DW_K
C_LNG = C_DWB + 2
C_LNB = C_LNG + 2
C_RGW = C_LNB + 2
C_RGB = C_RGW + 16
C_BA = C_RGB + 4
C_BX = C_BA + 4
C_LAM = C_BX + 4
NPAR = C_LAM + 4

K_ID = 0
K_CAUSAL = K_ID + P
K_INV = K_CAUSAL + P
K_SLOPE = K_INV + 2 * POOL_PAD
K_WIN = K_SLOPE + HEADS
NCONST = K_WIN + 2


class Lin:

    def __init__(self, c, k=0, reg=None):
        self.c, self.k, self.reg = c, k, reg

    def __add__(self, n):
        return Lin(self.c + n, self.k, self.reg)

    def __sub__(self, n):
        return self + (-n)

    def __mul__(self, n):
        return Lin(self.c * n, self.k * n, self.reg)

    @property
    def half(self):
        assert self.k % 2 == 0
        return Lin(self.c // 2, self.k // 2, self.reg)

    @property
    def par(self):
        assert self.k % 2 == 0
        return self.c % 2

    @property
    def v(self):
        return self.c if self.reg is None or self.k == 0 else self.reg * self.k + self.c


class Steps:

    def __init__(self, eng, sem):
        self.eng, self.sem, self.base, self.n = eng, sem, Lin(0), 0

    def __call__(self, ins):
        ins.then_inc(self.sem, 1)
        self.n += 1

    def wait(self):
        self.eng.wait_ge(self.sem, (self.base + self.n).v)

    def mark(self, ins):
        self(ins)
        self.wait()

    def enter(self, reg, per):
        self.start, self.per = self.base.c + self.n, per
        self.base, self.n = Lin(self.start, per, reg), 0

    def leave(self, count):
        assert self.n == self.per, self.n
        self.base, self.n = Lin(self.start + count * self.per), 0


def ds(at, n):
    return bass.ds(at, n) if not isinstance(at, int) else slice(at, at + n)


TOKENS2 = [(0, 128), (128, 128), (256, 128), (384, 128), (512, META)]
LOG1P_TERMS = 7


def build(nc, t):
    with ExitStack() as ctx:
        def sb(name, shape, dt=F32):
            return ctx.enter_context(nc.sbuf_tensor(name, shape, dt))

        w_raw = sb("w_raw", [P, 2, KT, P])
        w_hi = sb("w_hi", [P, 2, KT, P], F32R)
        w_lo = sb("w_lo", [P, 2, KT, P], F32R)
        a_hi = sb("a_hi", [P, KT, T2], F32R)
        a_lo = sb("a_lo", [P, KT, T2], F32R)
        b_hi = sb("b_hi", [P, 2 * KT, T2], F32R)
        b_lo = sb("b_lo", [P, 2 * KT, T2], F32R)
        h = sb("h", [P, KT, T2])
        rt = sb("rt", [P, T2])
        par = sb("par", [P, NPAR])
        con = sb("con", [P, NCONST])
        gconv = sb("gconv", [P, 20])
        ggate = sb("ggate", [P, 4])
        gtok = sb("gtok", [P, 2, NT, HPG])
        gacs = sb("gacs", [P, NT * HPG])[:, :]
        gfm = sb("gfm", [P, KT])
        spl = sb("spl", [P, 6, 4])
        rga = sb("rga", [P, 2, 4])
        bnst = sb("bnst", [P, 5, 6])
        bnag = sb("bnag", [P, 5, 2])
        cst = sb("cst", [P, 3])
        stat = sb("stat", [P, 96])
        psum = ctx.enter_context(nc.psum_tensor("psum", [P, 8, 512], F32))
        ARENA = 14248
        arena = sb("arena", [P, ARENA])
        mixw = sb("mixw", [P, 14 * P])
        top = [0]

        def place(*shape, at=None):
            at = top[0] if at is None else at
            n = math.prod(shape)
            top[0] = at + n
            assert top[0] <= ARENA, top[0]
            v = arena[:, at:at + n]
            if len(shape) == 2:
                v = v.rearrange("p (a b) -> p a b", a=shape[0])
            if len(shape) == 3:
                v = v.rearrange("p (a b c) -> p a b c", a=shape[0], b=shape[1])
            return v

        one, eps1, eps2 = cst[:, 0:1], cst[:, 1:2], cst[:, 2:3]
        ident = con[:, K_ID:K_ID + P]
        causal = con[:, K_CAUSAL:K_CAUSAL + P]
        decay_in = place(HPG, NT, P, at=0)
        MIX = top[0]
        mix = place(HPG, NT, P)
        sx = place(4, SEQ)
        sz = place(2, SEQ)
        pre = place(3 + SEQ)
        conv = place(2, SEQ)
        y = mixw[:, 0:2 * SEQ].rearrange("p (a b) -> p a b", a=2)
        edec = mixw[:, 2 * SEQ:14 * P].rearrange("p (a b) -> p a b", a=2)
        DTS = top[0]
        cb = place(NT, P)
        b_tok = place(NT - 1, P)
        xdt = place(NT, 2 * P)
        xend = place(NT - 1, 2 * P)
        state = place(NT - 1, 2 * P)
        gun = place(2, SEQ)
        tok = place(3, NT, 32)
        gsq = place(2, SEQ, at=MIX)
        yoff = place(2, SEQ - P, at=MIX)
        x_tok = place(NT, D, at=0)
        dts = [place(SEQ, at=DTS + SEQ * i) for i in range(8)]
        meta_tok = place(D, at=MIX + 4 * SEQ)
        sq = place(2, T2, at=0)
        sq2 = place(2, T2)
        ssq = place(T2)
        ssq2 = place(T2)
        asc = place(2 * P * 10, at=0)
        awt = place(10, P)
        aq = place(2, SEQ, at=KT * T2)
        ak = place(2, SEQ)
        asg = place(2, SEQ)
        avt = place(2, NT, P)
        afm = place(SEQ)
        agt = place(SEQ)
        aon = place(SEQ)
        aog = place(SEQ)
        afm2 = place(SEQ)
        dist = place(SEQ)
        lamt = place(4 * 64)
        lamp = place(2, 64)
        mg = place(KT, META)
        sqm = place(KT, META)
        bdw = mixw[:, 0:10 * P].rearrange("p (a b) -> p a b", a=10)
        pwt = mixw[:, 10 * P:14 * P].rearrange("p (a b c) -> p a b c", a=2, b=2)
        rr = place(T2, at=0)
        cu = place(2, DW_K - 1 + T2)
        pls = place(2, POOL_PAD + T2)
        bvt, bgt = pls[:, 0, 0:T2], pls[:, 1, 0:T2]
        dwo = place(2, T2)
        cxp = place(POOL_PAD + T2)
        xc = place(4, T2)
        cg = place(4, T2)
        plp = place(2, POOL_PAD + T2)
        pool_sums = ((pls[:, 0, :], pls[:, 1, :]), (cu[:, 1, 0:POOL_PAD + T2], cxp))
        products = (bvt, bgt, cg[:, 2, :], cg[:, 3, :])
        rtmp = place(8, T2)
        lnt = place(5, 2 * P, at=top[0] - 8 * T2)
        ft = place(T2, at=6 * T2)
        fs = place(T2)
        osb = place(2, D, at=0)
        gout = place(D)
        scratch = place(D)

        S = {}
        for name in (
            "par_in con_in x_in0 x_in1 x_in2 x_in3 meta_in lam_in dist_in bd_in pw_in raw0 raw1 ab_in acs_out gout_in out0 out1 "
            "hi_ready lo_ready unit_done acc_read "
            "act_own dve_own pool_own seg_ready relu_done "
            "consts_set x_tp x_hi x_lo x_cp meta_tp meta_cp xsum_ready xsd_ready rs_ready rb_ready rt_ready "
            "dt_pre dt_exp dt_acs dt_endexp dt_tok dt_tp tok_ready gt_ready tap_ready "
            "pre_silu silu_done mexp_ready dec_ready e_ready tpx_ready cb_ready bt_ready xw_ready m_ready "
            "st_ready s_ready y_ready u_ready gsq_ready gadd_ready gst_ready gsd_ready grs_ready grb_ready un_ready uh_ready "
            "ul_ready "
            "sq_ready ss_ready nst_ready ah_ready al_ready nsd_ready nrs_ready nrb_ready nrt_ready bh_ready bl_ready "
            "sc_ready scs_ready mx_ready ex_ready w_ready wt_tp wt_ready vt_tp vt_ready sg_ready o_ready osd_ready "
            "on_ready ont_ready og_ready oh_ready ol_ready "
            "meta_sq s2_ready r1_ready rr_ready "
            "bg_ready cu_ready dw_ready ln_tp ln_sd ln_ready lnb_tp cs_ready pwm_ready prod_ready prod_used psum_ready "
            "sp_done tanh_done ln_stat xc_ready rg_ready rga_ready at_ready m2_ready mu_ready scan_ready ge_ready yc_ready "
            "pool_ready poolm_ready yh_ready yl_ready "
            "lam_sum lam_exp sp_pre sp_exp "
            "ft_ready fh_ready fl_ready otp_ready osum_ready ors_ready o_done").split():
            S[name] = ctx.enter_context(nc.semaphore(name))
        block = ctx.enter_context(nc.Block())

        def bank(i):
            return psum[:, i, :]

        def acc(m):
            return psum[:, m.par, :]

        def acc2(m):
            return psum[:, 2 * m.par:2 * m.par + 2, 0:HALF2]

        def halves(v):
            return v.rearrange("p (a b) -> p a b", a=2)

        def stat_at(c, n=NT, rows=P):
            return stat[0:rows, c:c + n]

        X_SUM, X_SD, X_RS = 0, 4, 8
        G_SD, G_RS, DEC = 12, 16, 20
        A_MX, A_NB, A_SUM, A_RC = 28, 36, 44, 52
        O_SUM, O_SD, O_RS = 60, 64, 68
        LAM, SLOPE, EA, LAMS = 72, 73, 74, 94
        N_SD, N_RS, N_R2 = 76, 82, 88

        @block.sync
        def _(sp):
            def load(u, w, k0, col):
                if u.reg is not None or u.c >= 2:
                    sp.wait_ge(S["lo_ready"], (u - 1).v)
                src = w.rearrange("(k p) m -> p k m", p=P)[:, k0:k0 + KT, ds(col.v, P)]
                sp.dma_start(w_raw[:, u.par, :, :], src).then_inc(S[f"raw{u.par}"], 16)

            def group(g):
                for j, c in enumerate(ssd_cols(g)):
                    load(g * 6 + (U_MAMBA + j), t["a_w_in"], 0, c)

            sp.dma_start(con[:, :], t["consts"]).then_inc(S["con_in"], 16)
            for i in range(4):
                sp.dma_start(x_tok[:, :, 256 * i:256 * i + 256], t["x"].rearrange("(t p) d -> p t d", p=P)
                             [:, :, 256 * i:256 * i + 256]).then_inc(S[f"x_in{i}"], 16)
            load(Lin(U_DT), t["a_w_in"], 0, Lin(DINNER + CONV_DIM + 32 - P))
            group(Lin(0))
            group(Lin(1))
            with sp.Fori(0, 3) as i:
                group(Lin(2, 2, i))
                group(Lin(3, 2, i))
            with sp.Fori(0, 4) as i:
                for k in range(2):
                    for m in range(2):
                        load(Lin(U_WOUT + 2 * k + m, 4, i), t["a_w_out"], k * KT, Lin(m, 2, i) * P)

            def head(n):
                load(n * 4 + U_ATT, t["w_kv"], 0, n * P)
                load(n * 4 + (U_ATT + 1), t["w_kv"], 0, n * P + D)
                load(n * 4 + (U_ATT + 2), t["b_w_in"], 0, n * P)
                load(n * 4 + (U_ATT + 3), t["b_w_in"], 0, n * P + D)

            with sp.Fori(0, HEADS) as i:
                head(Lin(0, 1, i))
            with sp.Fori(0, 4) as i:
                for m in (Lin(0, 2, i), Lin(1, 2, i)):
                    load(m + U_BOUT, t["b_w_out"], 0, m * P)
            for n, c in enumerate(IN2_TILES):
                load(Lin(U_IN2 + n), t["w_in_2"], 0, Lin(c * P))
            with sp.Fori(0, 4) as i:
                for m in (Lin(0, 2, i), Lin(1, 2, i)):
                    load(m + U_OUT2, t["w_out_2"], 0, m * P)
            for half in range(2):
                u0 = U_MLP + 32 * half
                with sp.Fori(0, 8) as i:
                    for m in (Lin(0, 2, i), Lin(1, 2, i)):
                        load(m + u0, t["w_up_2"], 0, m * P + 2048 * half)
                with sp.Fori(0, 4) as i:
                    for m in (Lin(0, 2, i), Lin(1, 2, i)):
                        for k in range(2):
                            load(m * 2 + (u0 + 16 + k), t["w_down_2"], 16 * half + k * KT, m * P)
            for i in range(NT):
                sp.wait_ge(S["o_done"], i + 1)
                sp.dma_start(t["out"][P * i:P * i + P, :], osb[:, i % 2, :]).then_inc(S[f"out{i % 2}"], 16)
            for i in range(2):
                sp.wait_ge(S[f"out{i}"], 16 * NT // 2)

        @block.gpsimd
        def _(pool):
            pool.dma_start(par[:, :], t["params"]).then_inc(S["par_in"], 16)
            pool.dma_start(meta_tok[0:META, :], t["meta_tokens_2"]).then_inc(S["meta_in"], 16)
            pool.wait_ge(S["dt_acs"], 1)
            pool.dma_start(t["acs"], dts[6][96:128, :]).then_inc(S["acs_out"], 16)
            pool.wait_ge(S["acs_out"], 16)
            pool.wait_ge(S["xsum_ready"], 1)
            pool.wait_ge(S["x_tp"], KT)

            def spread(g):
                pool.dma_start(decay_in.rearrange("p h c l -> p (h c l)"),
                               t["acs"][ds((g * HPG).v, HPG), :].rearrange("h l -> (h l)").partition_broadcast(P)
                               ).then_inc(S["ab_in"], 16)

            def exponents(s):
                pool.wait_ge(S["ab_in"], (s * 16 + 16).v)
                nc.gpsimd.tensor_copy(gacs.rearrange("p (c h) -> p c h", h=HPG), tok[:, 0, :, ds((s * HPG).v, HPG)]
                                      ).then_inc(S["pool_own"], 1)
                pool.wait_ge(S["pool_own"], (s + 1).v)
                nc.gpsimd.tensor_tensor(mix, decay_in, gacs.rearrange("p (c h) -> p h c", h=HPG).unsqueeze(3)
                                        .to_broadcast([P, HPG, NT, P]), ALU.subtract).then_inc(S["seg_ready"], 1)

            def add_squares(s):
                pool.wait_ge(S["gsq_ready"], (s + 1).v)
                nc.gpsimd.tensor_tensor(gsq[:, 0, :], gsq[:, 0, :], gsq[:, 1, :], ALU.add
                                        ).then_inc(S["gadd_ready"], 1)

            spread(Lin(0))
            pool.wait_ge(S["tok_ready"], 1)
            exponents(Lin(0))
            with pool.Fori(1, GROUPS) as i:
                pool.wait_ge(S["e_ready"], i * HPG)
                pool.wait_ge(S["seg_ready"], i)
                spread(Lin(0, 1, i))
                add_squares(Lin(-1, 1, i))
                pool.wait_ge(S["gst_ready"], i)
                exponents(Lin(0, 1, i))
            add_squares(Lin(GROUPS - 1))
            pool.wait_ge(S["ul_ready"], GROUPS)
            pool.dma_start(lamt, t["b_lambda"].rearrange("l a b -> (l a b)").partition_broadcast(P)
                           ).then_inc(S["lam_in"], 16)
            pool.dma_start(dist, t["dist"]).then_inc(S["dist_in"], 16)
            pool.dma_start(bdw, t["blockdiag"]).then_inc(S["bd_in"], 16)
            pool.dma_start(pwt, t["convb_pw_w_2"].rearrange("(k p) (m n) -> p k m n", p=P, n=P)
                           ).then_inc(S["pw_in"], 16)
            for k in range(1, DW_K):
                pool.wait_ge(S["prod_ready"], k + 1)
                if k > 1:
                    pool.wait_ge(S["prod_used"], k - 1)
                nc.gpsimd.tensor_tensor(dwo[:, 1, :], dwo[:, 1, :], products[k % 4], ALU.add
                                        ).then_inc(S["prod_used"], 1)
            pool.wait_ge(S["prod_used"], DW_K - 1)
            steps = Steps(pool, S["pool_own"])
            steps.base = Lin(GROUPS)
            add = nc.gpsimd.tensor_tensor
            n = POOL_PAD + T2
            pool.wait_ge(S["xc_ready"], 4)
            for j in range(2):
                pool.wait_ge(S["acc_read"], M_IN2 + 9 + j)
                (a, b), u = pool_sums[j], plp[:, j, :]
                steps.mark(add(a[:, 1:n], u[:, 1:n], u[:, 0:n - 1], ALU.add))
                steps.mark(add(b[:, 3:n], a[:, 3:n], a[:, 1:n - 2], ALU.add))
                if j == 1:
                    steps.mark(add(a[:, 7:n], b[:, 7:n], b[:, 3:n - 4], ALU.add))
                    steps.mark(add(b[:, 15:n], a[:, 15:n], a[:, 7:n - 8], ALU.add))
                for rows, v in ((slice(0, 64), a), (slice(64, 128), b)):
                    x = v[rows, POOL_PAD:POOL_PAD + 16]
                    ins = add(x, x, con[rows, K_INV + 16 * j:K_INV + 16 * j + 16], ALU.mult)
                    if rows.start:
                        ins.then_inc(S["psum_ready"], 1)
                        pool.wait_ge(S["psum_ready"], j + 1)
                    else:
                        steps.mark(ins)
            for j in range(4):
                pool.wait_ge(S["ge_ready"], j + 1)
                pool.wait_ge(S["scan_ready"], j + 1)
                nc.gpsimd.tensor_tensor(xc[:, j, :], xc[:, j, :], cg[:, j, :], ALU.mult).then_inc(S["yc_ready"], 1)
            pool.wait_ge(S["fl_ready"], 32)
            pool.dma_start(gout, t["final_norm_g_2"].partition_broadcast(P)).then_inc(S["gout_in"], 16)

        @block.tensor
        def _(pe):
            mm, tp = nc.tensor.matmul, nc.tensor.transpose

            def tile_of(u, m, xh, xl, wide, k0=0, first=True, last=True, ks=range(KT), ready=None,
                        begin=None, end=None):
                begin = ks[0] == 0 if begin is None else begin
                end = ks[-1] == KT - 1 if end is None else end
                if first and begin and (m.reg is not None or m.c >= 2):
                    pe.wait_ge(S["acc_read"], (m - 1).v)
                pe.wait_ge(S["lo_ready"], (u + 1).v)
                if wide:
                    outs = [(psum[:, 2 * m.par + a, 0:HALF2], HALF2 * a, HALF2) for a in range(2)]
                else:
                    outs = [(acc(m), 0, SEQ)]
                for i, k in enumerate(ks):
                    if ready is not None:
                        pe.wait_ge(S[ready[0]], ready[1] + i)
                    for n, (wv, xv) in enumerate(((w_hi, xh), (w_hi, xl), (w_lo, xh))):
                        for out, c0, cn in outs:
                            ins = mm(out, wv[:, u.par, k, :], xv[:, k0 + k, c0:c0 + cn],
                                     start=(first and begin and i == 0 and n == 0),
                                     stop=(last and end and i == len(ks) - 1 and n == 2), skip_group_check=True)
                if end:
                    ins.then_inc(S["unit_done"], 1)

            def sums(out, v, tiles, ready):
                for i, (c0, cn) in enumerate(tiles):
                    ins = mm(out[0:cn, i:i + 1], v[:, c0:c0 + cn], one, start=True, stop=True,
                             skip_group_check=True)
                ins.then_inc(ready, 1)

            def spread(out, col, tiles, ready):
                for i, (c0, cn) in enumerate(tiles):
                    ins = tp(out[:, c0:c0 + cn], col[0:cn, i:i + 1].to_broadcast([cn, P]), ident[0:cn, 0:cn])
                ins.then_inc(ready, 1)

            TOKENS1 = TOKENS2[:NT]

            pe.wait_ge(S["con_in"], 16)
            for k in range(KT):
                if k % 2 == 0:
                    pe.wait_ge(S[f"x_in{k // 2}"], 16)
                if k >= 4:
                    pe.wait_ge(S["x_lo"], k - 3)
                    pe.wait_ge(S["x_cp"], (k - 2) // 2)
                for i in range(NT):
                    ins = tp(bank(2 + k % 4)[:, P * i:P * i + P], x_tok[:, i, P * k:P * k + P], ident)
                ins.then_inc(S["x_tp"], 1)
            tile_of(Lin(U_DT), Lin(0), a_hi, a_lo, False, ready=("x_lo", 1))
            pe.wait_ge(S["meta_in"], 16)
            for k in range(KT):
                ins = tp(bank(6)[:, META * k:META * k + META], meta_tok[0:META, P * k:P * k + P],
                         ident[0:META, 0:META])
            ins.then_inc(S["meta_tp"], 1)
            u, m = Lin(U_MAMBA), Lin(M_MAMBA)
            tile_of(u, m, a_hi, a_lo, False, ks=range(5))
            pe.wait_ge(S["rs_ready"], 1)
            spread(bank(7), stat_at(X_RS), TOKENS1, S["rb_ready"])
            tile_of(u, m, a_hi, a_lo, False, ks=range(5, KT))

            def ssd_turn(s):
                pe.wait_ge(S["silu_done"], (s * 6 + 4).v)
                if s.reg is not None or s.c > 0:
                    pe.wait_ge(S["u_ready"], s.v)
                for c in range(NT):
                    for j in range(2):
                        ins = tp(bank(4 + c // 2)[:, 256 * (c % 2) + P * j:256 * (c % 2) + P * j + P],
                                 sx[:, 2 + j, P * c:P * c + P], ident)
                ins.then_inc(S["tpx_ready"], 1)
                for c in range(NT - 1):
                    tp(bank(2)[:, P * c:P * c + P], sx[:, 0, P * c:P * c + P], ident)
                for c in range(NT):
                    ins = mm(bank(3)[:, P * c:P * c + P], sx[:, 0, P * c:P * c + P], sx[:, 1, P * c:P * c + P],
                             start=True, stop=True, skip_group_check=True)
                ins.then_inc(S["cb_ready"], 1)

            def ssd_states(s):
                pe.wait_ge(S["bt_ready"], (s + 1).v)
                pe.wait_ge(S["xw_ready"], (s + 1).v)
                for c in range(NT - 1):
                    ins = mm(bank(2 + c // 2)[:, 256 * (c % 2):256 * (c % 2) + 256], b_tok[:, c, :],
                             xend[:, c, :], start=True, stop=True, skip_group_check=True)
                ins.then_inc(S["st_ready"], 1)

            def ssd_y(s):
                pe.wait_ge(S["m_ready"], (s + 1).v)
                for c in range(NT):
                    for r in range(HPG):
                        mm(bank(4 + r // 2)[64 * (r % 2):64 * (r % 2) + 64, P * c:P * c + P],
                           xdt[:, c, 64 * r:64 * r + 64], mix[:, r, c, :],
                           start=True, stop=True, skip_group_check=True)
                pe.wait_ge(S["s_ready"], (s + 1).v)
                if s.reg is not None or s.c > 0:
                    pe.wait_ge(S["un_ready"], s.v)
                for c in range(1, NT):
                    for j in range(2):
                        ins = mm(bank(6 + j)[:, P * c:P * c + P], state[:, c - 1, P * j:P * j + P],
                                 sx[:, 1, P * c:P * c + P], start=True, stop=True, skip_group_check=True)
                ins.then_inc(S["y_ready"], 1)

            def group_sums(s):
                pe.wait_ge(S["gadd_ready"], (s + 1).v)
                sums(bank(6), gsq[:, 0, :], TOKENS1, S["gst_ready"])

            def group_spread(s):
                pe.wait_ge(S["grs_ready"], (s + 1).v)
                spread(bank(7), stat_at(G_RS), TOKENS1, S["grb_ready"])

            def group(g):
                u, m, s = g * 6 + U_MAMBA, g * 6 + M_MAMBA, g - 1
                tile_of(u, m, a_hi, a_lo, False)
                ssd_turn(s)
                tile_of(u + 1, m + 1, a_hi, a_lo, False)
                ssd_states(s)
                tile_of(u + 2, m + 2, a_hi, a_lo, False)
                ssd_y(s)
                tile_of(u + 3, m + 3, a_hi, a_lo, False)
                tile_of(u + 4, m + 4, a_hi, a_lo, False)
                group_sums(s)
                tile_of(u + 5, m + 5, a_hi, a_lo, False, ks=range(4))
                group_spread(s)
                tile_of(u + 5, m + 5, a_hi, a_lo, False, ks=range(4, KT))

            for j in range(1, 6):
                tile_of(Lin(U_MAMBA + j), Lin(M_MAMBA + j), a_hi, a_lo, False)
            pe.wait_ge(S["dt_tok"], 1)
            pe.wait_ge(S["meta_cp"], 1)
            for n, v in enumerate((dts[6], dts[5], dts[7])):
                for c in range(NT):
                    ins = tp(bank(6)[:, P * n + 32 * c:P * n + 32 * c + 32], v[96:128, P * c:P * c + P],
                             con[96:128, K_ID + 96:K_ID + 128])
            ins.then_inc(S["dt_tp"], 1)
            group(Lin(1))
            with pe.Fori(0, 3) as i:
                group(Lin(2, 2, i))
                group(Lin(3, 2, i))

            def wout(j, m, k, ks=range(KT)):
                tile_of(m * 2 + (U_WOUT + j), m + (M_WOUT + j % 2), b_hi, b_lo, False, k * KT, k == 0, k == 1, ks)

            def square_sums(n, v, b=7):
                pe.wait_ge(S["ss_ready"], n)
                sums(bank(b), v, TOKENS1, S["nst_ready"])

            s, m = Lin(GROUPS - 1), Lin(0)
            ssd_turn(s)
            pe.wait_ge(S["ul_ready"], GROUPS // 2)
            wout(0, m, 0)
            ssd_states(s)
            wout(1, m, 0)
            ssd_y(s)
            pe.wait_ge(S["ul_ready"], GROUPS - 1)
            wout(2, m, 1, range(6))
            group_sums(s)
            wout(3, m, 1, range(6))
            group_spread(s)
            pe.wait_ge(S["ul_ready"], GROUPS)
            wout(2, m, 1, range(6, KT))
            wout(3, m, 1, range(6, KT))
            with pe.Fori(0, 3) as i:
                m = Lin(2, 2, i)
                wout(0, m, 0)
                wout(1, m, 0)
                wout(2, m, 1)
                wout(3, m, 1)

            def scores(s, q):
                for i in range(2):
                    ins = mm(bank(2 + 2 * (q % 2) + i)[:, 0:P * (q + 1)],
                             aq[64 * i:64 * i + 64, s.par, P * q:P * q + P],
                             ak[64 * i:64 * i + 64, s.par, 0:P * (q + 1)],
                             start=True, stop=True, skip_group_check=True)
                ins.then_inc(S["sc_ready"], 1)

            def turn_weights(b, q0, q1, s):
                pe.wait_ge(S["w_ready"], (s * NT + q1).v)
                n = 0
                for q in range(q0, q1):
                    for k in range(q + 1):
                        ins = tp(bank(b)[:, P * n:P * n + P], asc[:, P * q * (q + 1) + P * k:][:, 0:P], ident)
                        n += 1
                ins.then_inc(S["wt_tp"], 1)

            def values(s, q):
                for k in range(q + 1):
                    ins = mm(bank(7)[:, P * q:P * q + P], awt[:, q * (q + 1) // 2 + k, :], avt[:, s.par, k, :],
                             start=(k == 0), stop=(k == q), skip_group_check=True)
                return ins

            def turn_v(n):
                pe.wait_ge(S["acc_read"], (n * 4 + (M_ATT + 2)).v)
                for k in range(NT):
                    ins = tp(bank(2)[:, P * k:P * k + P], afm[:, P * k:P * k + P], ident)
                ins.then_inc(S["vt_tp"], 1)

            def turn_out(f):
                pe.wait_ge(S["on_ready"], (f + 1).v)
                for k in range(NT):
                    ins = tp(bank(3)[:, P * k:P * k + P], aon[:, P * k:P * k + P], ident)
                ins.then_inc(S["ont_ready"], 1)

            def head(n, project=True, attend=True, finish=True):
                u, m, s, f = n * 4 + U_ATT, n * 4 + M_ATT, n - 1, n - 2

                def proj(j):
                    first = n.reg is None and n.c == 0
                    if project:
                        tile_of(u + j, m + j, *((a_hi, a_lo) if j < 2 else (b_hi, b_lo)), False,
                                ready={0: ("al_ready", 1), 2: ("bl_ready", 1)}.get(j) if first else None)
                    elif j < 2:
                        bout(j, range(6))

                if project:
                    proj(0)
                if project and n.reg is None and n.c == 0:
                    square_sums(KT - 1, ssq)
                if attend:
                    pe.wait_ge(S["acc_read"], (s * 4 + (M_ATT + 3)).v)
                    pe.wait_ge(S["vt_ready"], (s + 1).v)
                    if finish:
                        pe.wait_ge(S["wt_ready"], (f * 3 + 3).v)
                    scores(s, 0)
                    scores(s, 1)
                if not project:
                    proj(0)
                if project and n.reg is None and n.c == 0:
                    tile_of(u + 1, m + 1, a_hi, a_lo, False, ks=range(3))
                    pe.wait_ge(S["nrs_ready"], 1)
                    spread(bank(6), stat_at(N_RS), TOKENS1, S["nrb_ready"])
                    tile_of(u + 1, m + 1, a_hi, a_lo, False, ks=range(3, KT))
                if not (project and n.reg is None and n.c == 0):
                    proj(1)
                if attend:
                    pe.wait_ge(S["scs_ready"], (s * NT + 1).v)
                    scores(s, 2)
                    pe.wait_ge(S["scs_ready"], (s * NT + 2).v)
                    scores(s, 3)
                proj(2)
                if attend and finish:
                    pe.wait_ge(S["scs_ready"], (s * NT + 4).v)
                    turn_out(f)
                if project:
                    if attend:
                        pe.wait_ge(S["scs_ready"], (s * NT + 3).v)
                    turn_v(n)
                if attend:
                    turn_weights(6, 0, 2, s)
                proj(3)
                if attend:
                    turn_weights(4, 2, 3, s)
                    turn_weights(5, 3, 4, s)
                    pe.wait_ge(S["wt_ready"], (s * 3 + 1).v)
                    if finish:
                        pe.wait_ge(S["on_ready"], (f + 1).v)
                    values(s, 0)
                    values(s, 1)
                    pe.wait_ge(S["wt_ready"], (s * 3 + 2).v)
                    values(s, 2)
                    pe.wait_ge(S["wt_ready"], (s * 3 + 3).v)
                    values(s, 3).then_inc(S["o_ready"], 1)

            def bout(j, ks=range(KT), m=Lin(0)):
                tile_of(m + (U_BOUT + j), m + (M_BOUT + j), b_hi, b_lo, False, KT, ks=ks)

            head(Lin(0), attend=False, finish=False)
            head(Lin(1), finish=False)
            with pe.Fori(0, 3) as i:
                head(Lin(2, 2, i))
                head(Lin(3, 2, i))
            pe.wait_ge(S["ol_ready"], 6)
            head(Lin(8), project=False)
            turn_out(Lin(7))
            pe.wait_ge(S["ol_ready"], HEADS)
            bout(0, range(6, KT))
            pe.wait_ge(S["meta_sq"], 1)
            for k in range(KT):
                ins = mm(bank(5)[0:META, 0:1], sqm[:, k, :], one, start=(k == 0), stop=(k == KT - 1),
                         skip_group_check=True)
            ins.then_inc(S["nst_ready"], 1)
            bout(1, range(6, KT))
            with pe.Fori(0, 3) as i:
                m = Lin(2, 2, i)
                bout(0, m=m)
                bout(1, m=m)

            def in2(n, ready=None, ks=range(KT)):
                tile_of(Lin(U_IN2 + n), Lin(M_IN2 + n), a_hi, a_lo, True, ready=ready, ks=ks)

            in2(0, ("yl_ready", 1))
            square_sums(2 * (KT - 1), ssq)
            square_sums(2 * (KT - 1), ssq2, 6)

            def gates(j):
                pe.wait_ge(S["xc_ready"], j + 1)
                if j:
                    pe.wait_ge(S["rga_ready"], j)
                for a in range(2):
                    for c in range(2):
                        ins = mm(psum[:, 4 + 2 * a + c, 0:HALF2], bdw[:, 2 + 4 * a + j, :],
                                 xc[:, j, HALF2 * c:HALF2 * c + HALF2], start=True, stop=True, skip_group_check=True)
                ins.then_inc(S["rg_ready"], 1)

            pe.wait_ge(S["bd_in"], 16)
            pe.wait_ge(S["pw_in"], 16)
            for n in range(1, 14):
                in2(n, ks=range(5) if n == 1 else range(KT))
                if n == 1:
                    pe.wait_ge(S["nrs_ready"], 2)
                    spread(bank(5), stat_at(N_RS), TOKENS1, S["nrb_ready"])
                    tp(bank(7)[:, 0:META], stat[0:META, N_R2 + 4:N_R2 + 5].to_broadcast([META, P]),
                       ident[0:META, 0:META])
                    spread(bank(4), stat_at(N_R2), TOKENS1, S["nrb_ready"])
                    in2(n, ks=range(5, KT))
                if n == 6:
                    pe.wait_ge(S["rr_ready"], 3)
                if n in GATE_STEPS:
                    gates(GATE_STEPS.index(n))
                if n == 12:
                    pe.wait_ge(S["rga_ready"], 4)
                    pe.wait_ge(S["dw_ready"], 1)
                    pe.wait_ge(S["prod_used"], DW_K - 1)
                    for i, (c0, cn) in enumerate(TOKENS2):
                        for j in range(2):
                            ins = tp(psum[0:cn, 4 + i // 2, 256 * (i % 2) + P * j:256 * (i % 2) + P * j + P],
                                     dwo[:, j, c0:c0 + cn], ident)
                    ins.then_inc(S["ln_tp"], 1)
            pe.wait_ge(S["ln_ready"], 1)
            for j in range(2):
                for i, (c0, cn) in enumerate(TOKENS2):
                    ins = tp(psum[:, 4 + 2 * j + c0 // 512, c0 % 512:c0 % 512 + cn], lnt[0:cn, i, P * j:P * j + P],
                             ident[0:cn, 0:cn])
            ins.then_inc(S["lnb_tp"], 1)
            pe.wait_ge(S["acc_read"], M_IN2 + 14)
            pe.wait_ge(S["pool_ready"], 2)
            for j in range(2):
                for c in range(2):
                    ins = mm(psum[:, 2 * j + c, 0:HALF2], bdw[:, j, :],
                             plp[:, j, POOL_PAD + HALF2 * c:POOL_PAD + HALF2 * c + HALF2],
                             start=True, stop=True, skip_group_check=True)
            ins.then_inc(S["poolm_ready"], 1)
            pe.wait_ge(S["cs_ready"], 2)
            for j in range(2):
                for c in range(2):
                    for k in range(2):
                        ins = mm(psum[:, 4 + 2 * j + c, 0:HALF2], pwt[:, k, j, :],
                                 dwo[:, k, HALF2 * c:HALF2 * c + HALF2],
                                 start=(k == 0), stop=(k == 1), skip_group_check=True)
            ins.then_inc(S["pwm_ready"], 1)

            def out2(m, *part):
                tile_of(m + U_OUT2, m + M_OUT2, b_hi, b_lo, True, 0, True, True, *(part or (range(KT),)))

            pe.wait_ge(S["yl_ready"], KT + 6)
            out2(Lin(0), (4, 5, 6, 7, 0, 1), None, True, False)
            out2(Lin(0), (2, 3), ("yl_ready", KT + 7), False, True)
            out2(Lin(1))
            with pe.Fori(0, 3) as i:
                m = Lin(2, 2, i)
                out2(m)
                out2(m + 1)

            for half in range(2):
                u0, m0 = U_MLP + 32 * half, M_MLP + 24 * half
                if half == 0:
                    tile_of(Lin(u0), Lin(m0), a_hi, a_lo, True, ready=("al_ready", KT + 1))
                    pe.wait_ge(S["ss_ready"], 3 * (KT - 1))
                    sums(bank(7), ssq, TOKENS2, S["nst_ready"])
                    tile_of(Lin(u0 + 1), Lin(m0 + 1), a_hi, a_lo, True, ks=range(4))
                    pe.wait_ge(S["nrs_ready"], 3)
                    spread(psum[:, 4:6, :].rearrange("p a b -> p (a b)"), stat_at(N_RS, 5), TOKENS2, S["nrb_ready"])
                    tile_of(Lin(u0 + 1), Lin(m0 + 1), a_hi, a_lo, True, ks=range(4, KT))
                with pe.Fori(0, 7 + half) as i:
                    for j in range(2):
                        m = Lin(2 * (1 - half) + j, 2, i)
                        tile_of(m + u0, m + m0, a_hi, a_lo, True)
                pe.wait_ge(S["fl_ready"], 16 * half + KT)
                with pe.Fori(0, 4) as i:
                    for m in (Lin(0, 2, i), Lin(1, 2, i)):
                        for k in range(2):
                            if k == 1 and m.c == 0:
                                pe.wait_ge(S["fl_ready"], 16 * half + 16)
                            tile_of(m * 2 + (u0 + 16 + k), m + (m0 + 16), b_hi, b_lo, True, k * KT, k == 0, k == 1)
            pe.wait_ge(S["acc_read"], M_MLP + 48)
            for i in range(NT):
                if i >= 2:
                    pe.wait_ge(S["o_done"], i - 1)
                for k in range(KT):
                    ins = tp(psum[:, 4 + 2 * (i % 2) + k // 4, P * (k % 4):P * (k % 4) + P],
                             h[:, k, META + P * i:META + P * i + P], ident)
                ins.then_inc(S["otp_ready"], 1)

        @block.scalar
        def _(act):
            own = Steps(act, S["act_own"])
            ac = nc.scalar.activation

            def hi(u):
                act.wait_ge(S[f"raw{u.par}"], (u.half * 16 + 16).v)
                if u.reg is not None or u.c >= 2:
                    act.wait_ge(S["unit_done"], (u - 1).v)
                ac(w_hi[:, u.par, :, :], w_raw[:, u.par, :, :], ACT.Copy).then_inc(S["hi_ready"], 1)

            def root(out, in_, eps, scale, ready):
                ac(out, in_, ACT.Sqrt, scale=scale, bias=eps[0:out.shape[0], :]).then_inc(ready, 1)

            act.wait_ge(S["par_in"], 16)
            for k in range(KT):
                if k == 4:
                    hi(Lin(0))
                act.wait_ge(S["x_tp"], k + 1)
                ins = ac(a_hi[:, k, 0:SEQ], bank(2 + k % 4), ACT.Copy,
                         scale=par[:, C_ANORM + k:C_ANORM + k + 1])
                if k % 2:
                    ins = ac(h[:, k, META:T2], bank(2 + k % 4), ACT.Copy)
                ins.then_inc(S["x_hi"], 1)
            hi(Lin(1))
            for i in range(NT):
                ins = ac(b_hi[:, 2 * i:2 * i + 2, 0:SEQ], x_tok[:, i, :].rearrange("p (a b) -> p a b", a=2), ACT.Square,
                         accum_out=stat[:, X_SUM + i:X_SUM + i + 1])
            ins.then_inc(S["xsum_ready"], 1)
            act.wait_ge(S["xsum_ready"], 1)
            act.wait_ge(S["consts_set"], 3)
            root(stat_at(X_SD), stat_at(X_SUM), eps1, 1.0 / D, S["xsd_ready"])
            hi(Lin(2))
            act.wait_ge(S["rb_ready"], 1)
            ac(rt[:, 0:SEQ], bank(7), ACT.Copy).then_inc(S["rt_ready"], 1)

            def first_tap(g, j):
                if g.reg is not None or g.c > 0 or j > 1:
                    act.wait_ge(S["silu_done"], (g * 6 + (j - 1)).v)
                act.wait_ge(S["acc_read"], (g * 6 + (M_MAMBA + j + 1)).v)
                ac(conv[:, j % 2, :], pre[:, 3:3 + SEQ], ACT.Identity, scale=gconv[:, 5 * j + 3:5 * j + 4],
                   bias=gconv[:, 5 * j + 4:5 * j + 5]).then_inc(S["tap_ready"], 1)

            def silu(g, j):
                if j < 4:
                    act.wait_ge(S["pre_silu"], (g * 4 + (j + 1)).v)
                    dst = sx[:, j, :]
                else:
                    act.wait_ge(S["acc_read"], (g * 6 + (M_MAMBA + j + 1)).v)
                    dst = sz[:, j - 4, :]
                ac(dst, conv[:, j % 2, :], ACT.Silu).then_inc(S["silu_done"], 1)

            def decays(s):
                act.wait_ge(S["seg_ready"], (s + 1).v)
                ac(mix, mix, ACT.Relu, scale=-1.0).then_inc(S["relu_done"], 1)
                act.wait_ge(S["cb_ready"], (s + 1).v)
                ac(b_tok.rearrange("p c n -> p (c n)"), bank(2)[:, 0:(NT - 1) * P],
                   ACT.Copy).then_inc(S["bt_ready"], 1)
                act.wait_ge(S["relu_done"], (s + 1).v)
                ac(mix, mix, ACT.Exp, scale=-1.0).then_inc(S["mexp_ready"], 1)
                ac(stat[:, DEC:DEC + 8].rearrange("p (h c) -> p h c", h=HPG),
                   decay_in[:, :, 1:3, P - 1], ACT.Exp).then_inc(S["dec_ready"], 1)

            def token_decays(s):
                for r in range(HPG):
                    rows = slice(64 * (r % 2), 64 * (r % 2) + 64)
                    ac(edec[rows, r // 2, :].rearrange("p (c l) -> p c l", l=P), decay_in[rows, r, 1:NT, :],
                       ACT.Exp).then_inc(S["e_ready"], 1)

            def output_squares(s):
                act.wait_ge(S["u_ready"], (s + 1).v)
                ac(gsq, y, ACT.Square).then_inc(S["gsq_ready"], 1)

            def group_root(s):
                act.wait_ge(S["gst_ready"], (s + 1).v)
                root(stat_at(G_SD), bank(6)[:, 0:NT], eps1, 1.0 / 256, S["gsd_ready"])

            def output_high(s):
                act.wait_ge(S["un_ready"], (s + 1).v)
                for j in range(2):
                    ac(row(b_hi, s * 2 + j, 0, SEQ), gun[:, j, :], ACT.Copy,
                       scale=ggate[:, 2 + j:3 + j]).then_inc(S["uh_ready"], 1)

            def group(g):
                u, s = g * 6 + U_MAMBA, g - 1
                hi(u + 2)
                first_tap(g, 0)
                decays(s)
                hi(u + 3)
                first_tap(g, 1)
                token_decays(s)
                silu(g, 0)
                hi(u + 4)
                first_tap(g, 2)
                act.wait_ge(S["y_ready"], (s + 1).v)
                silu(g, 1)
                hi(u + 5)
                output_squares(s)
                first_tap(g, 3)
                silu(g, 2)
                hi(u + 6)
                silu(g, 3)
                silu(g, 4)
                group_root(s)
                output_high(s)
                hi(u + 7)
                silu(g, 5)

            g, u = Lin(0), Lin(U_MAMBA)
            hi(u + 2)
            first_tap(g, 0)
            act.wait_ge(S["dt_pre"], 1)
            own.mark(ac(dts[1][96:128, :], dts[0][96:128, :], ACT.Abs, bias=par[96:128, C_DTB:C_DTB + 1]))
            ac(dts[1][96:128, :], dts[1][96:128, :], ACT.Exp, scale=-1.0).then_inc(S["dt_exp"], 1)
            ac(stat[96:128, EA:EA + 1], par[96:128, C_ALOG:C_ALOG + 1], ACT.Exp).then_inc(S["dt_exp"], 1)
            silu(g, 0)
            hi(u + 3)
            first_tap(g, 1)
            silu(g, 1)
            hi(u + 4)
            first_tap(g, 2)
            silu(g, 2)
            hi(u + 5)
            first_tap(g, 3)
            act.wait_ge(S["dt_acs"], 2)
            ac(dts[7][96:128, :], dts[7][96:128, :], ACT.Exp).then_inc(S["dt_endexp"], 1)
            silu(g, 3)
            hi(u + 6)
            silu(g, 4)
            hi(u + 7)
            act.wait_ge(S["dt_tp"], 1)
            ac(tok.rearrange("p a b c -> p (a b c)"), bank(6)[:, 0:3 * P], ACT.Copy).then_inc(S["tok_ready"], 1)
            silu(g, 5)
            group(Lin(1))
            with act.Fori(0, 3) as i:
                group(Lin(2, 2, i))
                group(Lin(3, 2, i))

            def squares_at(m, sq, ssq):
                return ssq if m.reg is None and m.c == 0 else sq[:, m.par, :]

            def wout_tile(m, j, prep=True):
                if prep:
                    hi(m * 2 + (U_WOUT + 4 + j))
                m = m + j
                act.wait_ge(S["acc_read"], (m + (M_WOUT + 1)).v)
                ac(squares_at(m, sq, ssq)[:, 0:SEQ], row(h, m, META, T2), ACT.Square).then_inc(S["sq_ready"], 1)
                ac(row(a_hi, m, 0, SEQ), row(h, m, META, T2), ACT.Copy,
                   scale=par[:, ds((m + C_KVN).v, 1)]).then_inc(S["ah_ready"], 1)

            s = Lin(GROUPS - 1)
            decays(s)
            hi(Lin(U_WOUT + 2))
            token_decays(s)
            hi(Lin(U_WOUT + 3))
            output_squares(s)
            group_root(s)
            output_high(s)
            wout_tile(Lin(0), 0)
            wout_tile(Lin(0), 1)
            with act.Fori(0, 3) as i:
                m = Lin(2, 2, i)
                hi(m * 2 + (U_WOUT + 2))
                hi(m * 2 + (U_WOUT + 3))
                wout_tile(m, 0)
                wout_tile(m, 1)

            def b_operand(ks):
                for k in ks:
                    ac(b_hi[:, k, 0:SEQ], h[:, k, META:T2], ACT.Copy,
                       scale=par[:, C_BN + k:C_BN + k + 1]).then_inc(S["bh_ready"], 1)

            act.wait_ge(S["unit_done"], U_WOUT + 14)
            b_operand(range(4))
            hi(Lin(U_ATT + 2))
            act.wait_ge(S["nst_ready"], 1)
            root(stat_at(N_SD), bank(7)[:, 0:NT], eps1, 1.0 / D, S["nsd_ready"])
            act.wait_ge(S["nrb_ready"], 1)
            ac(rt[:, 0:SEQ], bank(6), ACT.Copy).then_inc(S["nrt_ready"], 1)
            b_operand(range(4, KT))
            act.wait_ge(S["lam_sum"], 1)
            ac(stat_at(LAMS, 2), stat_at(LAMS, 2), ACT.Exp).then_inc(S["lam_exp"], 1)
            ac(sqm, h[:, :, 0:META], ACT.Square).then_inc(S["meta_sq"], 1)

            def exps(s, q):
                n = P * (q + 1)
                act.wait_ge(S["mx_ready"], (s * NT + (q + 1)).v)
                own.mark(ac(stat_at(A_NB + 2 * q, 2), stat_at(A_MX + 2 * q, 2), ACT.Copy, scale=-0.125))
                for i in range(2):
                    part = asc[:, P * q * (q + 1) + n * i:P * q * (q + 1) + n * i + n]
                    ac(part, part, ACT.Exp, bias=stat_at(A_NB + 2 * q + i, 1), scale=0.125,
                       accum_out=stat_at(A_SUM + 2 * q + i, 1)).then_inc(S["ex_ready"], 1)

            def copy_weights(b, q0, q1, s, n):
                first, last = q0 * (q0 + 1) // 2, q1 * (q1 + 1) // 2
                act.wait_ge(S["wt_tp"], (s * 3 + n).v)
                ac(awt[:, first:last, :].rearrange("p a b -> p (a b)"), bank(b)[:, 0:P * (last - first)],
                   ACT.Copy).then_inc(S["wt_ready"], 1)

            def out_high(f):
                act.wait_ge(S["og_ready"], (f + 1).v)
                ac(row(b_hi, f + KT, 0, SEQ), aog, ACT.Copy, scale=spl[:, 5, 0:1]).then_inc(S["oh_ready"], 1)

            def head(n, project=True, attend=True, finish=True):
                u, m, s, f = n * 4 + U_ATT, n * 4 + M_ATT, n - 1, n - 2
                prep = hi if project else (lambda u: None)
                if attend:
                    prep(u + 2)
                    exps(s, 0)
                    exps(s, 1)
                prep(u + 3)
                if attend:
                    exps(s, 2)
                    exps(s, 3)
                    copy_weights(6, 0, 2, s, 1)
                prep(u + 4)
                if project:
                    act.wait_ge(S["vt_tp"], (n + 1).v)
                    ac(avt[:, n.par, :, :].rearrange("p a b -> p (a b)"), bank(2), ACT.Copy
                       ).then_inc(S["vt_ready"], 1)
                if finish:
                    out_high(f)
                prep(u + 5)
                if attend:
                    copy_weights(4, 2, 3, s, 2)
                    copy_weights(5, 3, 4, s, 3)
                if project:
                    act.wait_ge(S["acc_read"], (m + 4).v)
                    ac(asg[:, n.par, :], agt, ACT.Silu).then_inc(S["sg_ready"], 1)
                if attend:
                    act.wait_ge(S["o_ready"], (s + 1).v)
                    for q in range(NT):
                        ins = ac(afm2[:, P * q:P * q + P], bank(7)[:, P * q:P * q + P], ACT.Square,
                                 accum_out=stat_at(O_SUM + q, 1))
                    own.mark(ins)
                    root(stat_at(O_SD), stat_at(O_SUM), eps1, 1.0 / P, S["osd_ready"])

            head(Lin(0), attend=False, finish=False)
            head(Lin(1), finish=False)
            with act.Fori(0, 3) as i:
                own.enter(i, 10)
                head(Lin(2, 2, i))
                head(Lin(3, 2, i))
                own.leave(3)
            head(Lin(8), project=False)
            out_high(Lin(7))

            own.mark(ac(spl[:, 0, :], par[:, C_LAM:C_LAM + 4], ACT.Abs))
            ac(spl[:, 0, :], spl[:, 0, :], ACT.Exp, scale=-1.0).then_inc(S["sp_exp"], 1)

            def bout_tile(m):
                hi(m + (U_BOUT + 2))
                act.wait_ge(S["acc_read"], (m + (M_BOUT + 1)).v)
                ac(row(a_hi, m, META, T2), row(h, m, META, T2), ACT.Copy,
                   scale=col(gfm, m)).then_inc(S["yh_ready"], 1)
                ac(squares_at(m, sq, ssq)[:, 0:SEQ], row(h, m, META, T2), ACT.Square).then_inc(S["act_own"], 1)
                ac(squares_at(m, sq2, ssq2)[:, 0:SEQ], row(h, m, META, T2), ACT.Square,
                   scale=par[:, ds((m + C_FIN).v, 1)]).then_inc(S["s2_ready"], 1)

            bout_tile(Lin(0))
            bout_tile(Lin(1))
            with act.Fori(0, 3) as i:
                bout_tile(Lin(2, 2, i))
                bout_tile(Lin(3, 2, i))
            own.n += KT
            hi(Lin(U_IN2 + 2))
            act.wait_ge(S["nst_ready"], 4)
            ac(stat[0:META, N_SD + 4:N_SD + 5], bank(5)[0:META, 0:1], ACT.Sqrt, scale=1.0 / D,
               bias=eps2[0:META, :]).then_inc(S["nsd_ready"], 1)
            root(stat_at(N_SD), bank(7)[:, 0:NT], eps1, 1.0 / D, S["nsd_ready"])
            act.wait_ge(S["r1_ready"], 1)
            root(stat_at(N_SD), stat_at(N_R2), eps2, 1.0 / D, S["nsd_ready"])
            act.wait_ge(S["nrb_ready"], 3)
            ac(rr[:, META:T2], bank(4), ACT.Copy).then_inc(S["rr_ready"], 1)
            ac(rr[:, 0:META], bank(7)[:, 0:META], ACT.Copy).then_inc(S["rr_ready"], 1)
            ac(rt[:, META:T2], bank(5), ACT.Copy).then_inc(S["rr_ready"], 1)

            def gate_sigmoids(j):
                act.wait_ge(S["rg_ready"], j + 1)
                if j >= 2:
                    act.wait_ge(S["scan_ready"], j - 1)
                for a, c in enumerate((C_BA, C_BX)):
                    ac(halves(rtmp[:, 4 * (j % 2) + a, :]), psum[:, 4 + 2 * a:6 + 2 * a, 0:HALF2], ACT.Sigmoid,
                       bias=par[:, c + j:c + j + 1]).then_inc(S["rga_ready"] if a else S["act_own"], 1)
                own.n += 1

            def gate_exps(js):
                own.wait()
                act.wait_ge(S["sp_done"], 1)
                for j in js:
                    r = rtmp[:, 4 * (j % 2), :]
                    own.mark(ac(rtmp[:, 4 * (j % 2) + 2, :], r, ACT.Exp, scale=rga[:, 0, j:j + 1]))
                    ac(rtmp[:, 4 * (j % 2) + 3, :], r, ACT.Tanh, scale=rga[:, 1, j:j + 1]).then_inc(S["tanh_done"], 1)
                    act.wait_ge(S["tanh_done"], j + 1)
                    ac(r, rtmp[:, 4 * (j % 2) + 2, :], ACT.Square).then_inc(S["at_ready"], 1)

            def gate_roots(js):
                for j in js:
                    act.wait_ge(S["m2_ready"], j + 1)
                    m2 = rtmp[:, 4 * (j % 2) + 3, :]
                    ac(m2, m2, ACT.Sqrt).then_inc(S["mu_ready"], 1)

            def tap_products(k0, k1):
                for k in range(k0, k1):
                    src = cu[:, 1, DW_K - 1 - k:DW_K - 1 - k + T2]
                    w = par[:, C_DWW + 2 * DW_K - 1 - k:C_DWW + 2 * DW_K - k]
                    if k == 0:
                        ac(dwo[:, 1, :], src, ACT.Identity, scale=w, bias=par[:, C_DWB + 1:C_DWB + 2]
                           ).then_inc(S["prod_ready"], 1)
                        continue
                    if k > 4:
                        act.wait_ge(S["prod_used"], k - 4)
                    ac(products[k % 4], src, ACT.Copy, scale=w).then_inc(S["prod_ready"], 1)

            def gelus(j0):
                act.wait_ge(S["acc_read"], M_IN2 + 12 + j0)
                for j in (j0, j0 + 1):
                    ac(cg[:, j, :], cg[:, j, :], ACT.Gelu_apprx_tanh).then_inc(S["ge_ready"], 1)

            def rnn_high(p):
                for j in (2 * p, 2 * p + 1):
                    act.wait_ge(S["yc_ready"], j + 1)
                    ac(b_hi[:, 4 + j, :], xc[:, j, :], ACT.Copy).then_inc(S["yh_ready"], 1)

            PRODUCTS = {3: (0, 5), 4: (5, 9), 5: (9, 13), 6: (13, 17), 7: (17, 20), 8: (20, 24), 9: (24, 28),
                        10: (28, 31)}
            for n in range(14):
                if n:
                    hi(Lin(U_IN2 + n + 2))
                if n in (1, 3):
                    act.wait_ge(S["acc_read"], M_IN2 + n + 1)
                    ac(bgt, bgt, ACT.Sigmoid).then_inc(S["bg_ready"], 1)
                if n == 8:
                    gate_roots((0, 1))
                if n in GATE_STEPS:
                    gate_sigmoids(GATE_STEPS.index(n))
                if n in PRODUCTS:
                    if n == 3:
                        act.wait_ge(S["cu_ready"], 1)
                    tap_products(*PRODUCTS[n])
                if n == 7:
                    gate_exps((0, 1))
                if n == 10:
                    gate_exps((2, 3))
                if n == 11:
                    gate_roots((2, 3))
                if n == 12:
                    act.wait_ge(S["ln_stat"], 1)
                    root(stat_at(N_SD, 5), bnag[:, :, 1], eps2, 1.0, S["ln_sd"])
                if n in (12, 13):
                    gelus(2 * n - 24)
            act.wait_ge(S["lnb_tp"], 1)
            for j in range(2):
                ac(dwo[:, j, :], psum[:, 4 + 2 * j:6 + 2 * j, :].rearrange("p a b -> p (a b)")[:, 0:T2], ACT.Silu,
                   scale=par[:, C_LNG + j:C_LNG + j + 1],
                   bias=par[:, C_LNB + j:C_LNB + j + 1]).then_inc(S["cs_ready"], 1)
            rnn_high(0)
            rnn_high(1)
            act.wait_ge(S["poolm_ready"], 1)
            for j in range(2):
                ac(halves(b_hi[:, j, :]), psum[:, 2 * j:2 * j + 2, 0:HALF2], ACT.Copy,
                   scale=par[:, C_PSC + j:C_PSC + j + 1]).then_inc(S["yh_ready"], 1)
            act.wait_ge(S["pwm_ready"], 1)
            for j in range(2):
                ac(halves(b_hi[:, 2 + j, :]), psum[:, 4 + 2 * j:6 + 2 * j, 0:HALF2], ACT.Copy
                   ).then_inc(S["yh_ready"], 1)
            def out2_tile(m):
                hi(m + (U_OUT2 + 2))
                act.wait_ge(S["acc_read"], (m + (M_OUT2 + 1)).v)
                ac(squares_at(m, sq, ssq), row(h, m, 0, T2), ACT.Square).then_inc(S["sq_ready"], 1)
                ac(row(a_hi, m, 0, T2), row(h, m, 0, T2), ACT.Copy,
                   scale=par[:, ds((m + C_MLP).v, 1)]).then_inc(S["ah_ready"], 1)

            out2_tile(Lin(0))
            out2_tile(Lin(1))
            with act.Fori(0, 3) as i:
                out2_tile(Lin(2, 2, i))
                out2_tile(Lin(3, 2, i))

            hi(Lin(U_MLP + 2))
            act.wait_ge(S["nst_ready"], 5)
            ac(stat[0:META, N_SD + 4:N_SD + 5], bank(7)[0:META, 4:5], ACT.Sqrt, scale=1.0 / D,
               bias=eps2[0:META, :]).then_inc(S["nsd_ready"], 1)
            root(stat_at(N_SD), bank(7)[:, 0:NT], eps2, 1.0 / D, S["nsd_ready"])
            act.wait_ge(S["nrb_ready"], 4)
            ac(rt[:, :], psum[:, 4:6, :].rearrange("p a b -> p (a b)")[:, 0:T2], ACT.Copy
               ).then_inc(S["nrt_ready"], 1)

            def up(m, half, prep=True):
                if prep:
                    hi(m + (U_MLP + 32 * half + 2))
                act.wait_ge(S["acc_read"], (m + (M_MLP + 24 * half + 1)).v)
                ac(row(b_hi, m, 0, T2), ft, ACT.Square).then_inc(S["fh_ready"], 1)

            def down(m, half):
                hi(m * 2 + (U_MLP + 32 * half + 18))
                hi(m * 2 + (U_MLP + 32 * half + 19))

            up(Lin(0), 0, prep=False)
            up(Lin(1), 0)
            for half in range(2):
                with act.Fori(0, 7 + half) as i:
                    for j in range(2):
                        up(Lin(2 * (1 - half) + j, 2, i), half)
                with act.Fori(0, 4 - half) as i:
                    for m in (Lin(0, 2, i), Lin(1, 2, i)):
                        down(m, half)
            down(Lin(6), 1)
            for i in range(NT):
                act.wait_ge(S["otp_ready"], i + 1)
                own.mark(ac(scratch, psum[:, 4 + 2 * (i % 2):6 + 2 * (i % 2), :].rearrange("p a b -> p (a b)"),
                            ACT.Square, accum_out=stat_at(O_SUM + i, 1)))
                root(stat_at(O_SD + i, 1), stat_at(O_SUM + i, 1), eps2, 1.0 / D, S["osum_ready"])

        @block.vector
        def _(dve):
            own = Steps(dve, S["dve_own"])
            tt, ts, stt, cp = (nc.vector.tensor_tensor, nc.vector.tensor_scalar, nc.vector.scalar_tensor_tensor,
                               nc.vector.tensor_copy)

            def f32(v):
                return v.bitcast(F32)

            def lo(u):
                dve.wait_ge(S["hi_ready"], (u + 1).v)
                tt(w_lo[:, u.par, :, :], w_raw[:, u.par, :, :], f32(w_hi[:, u.par, :, :]), ALU.subtract
                   ).then_inc(S["lo_ready"], 1)

            def log1p_start(e, w, z, z2, out):
                own.mark(ts(w, e, 2.0, None, ALU.add))
                own.mark(nc.vector.reciprocal(w, w))
                own.mark(tt(z, e, w, ALU.mult))
                own.mark(tt(z2, z, z, ALU.mult))
                own.mark(ts(out, z2, 1.0 / (2 * LOG1P_TERMS + 1), None, ALU.mult))

            def log1p_terms(z2, out, ks):
                for k in ks:
                    own.mark(stt(out, out, 1.0 / (2 * k + 1), z2, ALU.add, ALU.mult))

            def log1p_end(z, mx, out):
                own.mark(stt(out, out, 1.0, z, ALU.add, ALU.mult))
                own.mark(stt(out, out, 2.0, mx, ALU.mult, ALU.add))

            nc.vector.memset(stat[:, :], 1.0).then_inc(S["consts_set"], 1)
            nc.vector.memset(pre[:, 0:3], 0.0).then_inc(S["consts_set"], 1)
            nc.vector.memset(one, 1.0).then_inc(S["consts_set"], 1)
            nc.vector.memset(eps1, EPS1).then_inc(S["consts_set"], 1)
            nc.vector.memset(eps2, EPS2).then_inc(S["consts_set"], 1)
            dve.wait_ge(S["par_in"], 16)
            dve.wait_ge(S["con_in"], 16)
            own(tt(gfm[:, :], par[:, C_FIN:C_FIN + KT], par[:, C_MIX:C_MIX + KT], ALU.mult))
            own(ts(spl[:, 5, 0:1], par[:, C_SUBG:C_SUBG + 1], 1.0 - LAMBDA_INIT, None, ALU.mult))
            for k in range(KT):
                if k == 4:
                    lo(Lin(0))
                dve.wait_ge(S["x_hi"], k + 1)
                stt(a_lo[:, k, 0:SEQ], bank(2 + k % 4), par[:, C_ANORM + k:C_ANORM + k + 1],
                    f32(a_hi[:, k, 0:SEQ]), ALU.mult, ALU.subtract).then_inc(S["x_lo"], 1)
                if k % 2 == 0:
                    cp(h[:, k, META:T2], bank(2 + k % 4)).then_inc(S["x_cp"], 1)
            lo(Lin(1))
            dve.wait_ge(S["xsd_ready"], 1)
            nc.vector.reciprocal(stat_at(X_RS), stat_at(X_SD)).then_inc(S["rs_ready"], 1)
            dve.wait_ge(S["meta_tp"], 1)
            cp(h[:, :, 0:META], bank(6)[:, 0:KT * META].rearrange("p (a b) -> p a b", a=KT)
               ).then_inc(S["meta_cp"], 1)

            rows = slice(96, 128)
            d = [v[rows, :] for v in dts]
            lo(Lin(2))
            dve.wait_ge(S["rt_ready"], 1)
            dve.wait_ge(S["unit_done"], 1)
            tt(d[0], psum[rows, 0, :], rt[rows, 0:SEQ], ALU.mult).then_inc(S["acc_read"], 1)
            dve.wait_ge(S["acc_read"], 1)
            ts(d[2], d[0], par[rows, C_DTB:C_DTB + 1], 0.0, ALU.add, ALU.max).then_inc(S["dt_pre"], 1)

            def evacuate_in(g, j):
                n, m = g * 6 + j, g * 6 + (M_MAMBA + j)
                if j == 0:
                    own(cp(gconv[:, :], par[:, ds((g * GW + C_GROUP).v, 20)]))
                dve.wait_ge(S["unit_done"], (g * 6 + (U_MAMBA + j + 1)).v)
                if j < 4:
                    if g.reg is not None or g.c + j > 0:
                        dve.wait_ge(S["pre_silu"], (g * 4 + j).v)
                    tt(pre[:, 3:3 + SEQ], acc(m), rt[:, 0:SEQ], ALU.mult).then_inc(S["acc_read"], 1)
                    return
                dve.wait_ge(S["silu_done"], (n - 1).v)
                tt(conv[:, j % 2, :], acc(m), rt[:, 0:SEQ], ALU.mult).then_inc(S["acc_read"], 1)

            def taps_of(g, j):
                c = conv[:, j % 2, :]
                w = [gconv[:, 5 * j + k:5 * j + k + 1] for k in range(3)]
                dve.wait_ge(S["tap_ready"], (g * 4 + (j + 1)).v)
                own.mark(stt(c, pre[:, 2:2 + SEQ], w[2], c, ALU.mult, ALU.add))
                own.mark(stt(c, pre[:, 1:1 + SEQ], w[1], c, ALU.mult, ALU.add))
                stt(c, pre[:, 0:SEQ], w[0], c, ALU.mult, ALU.add).then_inc(S["pre_silu"], 1)

            g, u = Lin(0), Lin(U_MAMBA)
            evacuate_in(g, 0)
            lo(u + 2)
            taps_of(g, 0)
            dve.wait_ge(S["dt_exp"], 2)
            log1p_start(d[1], d[3], d[3], d[4], d[5])
            evacuate_in(g, 1)
            lo(u + 3)
            taps_of(g, 1)
            log1p_terms(d[4], d[5], range(LOG1P_TERMS - 1, 3, -1))
            evacuate_in(g, 2)
            lo(u + 4)
            taps_of(g, 2)
            log1p_terms(d[4], d[5], range(3, 0, -1))
            log1p_end(d[3], d[2], d[5])
            evacuate_in(g, 3)
            lo(u + 5)
            own.mark(ts(d[0], d[5], stat[rows, EA:EA + 1], -1.0, ALU.mult, ALU.mult))
            for c in range(NT):
                ins = nc.vector.tensor_tensor_scan(d[6][:, P * c:P * c + P], cst[rows, 0:1].to_broadcast([32, P]),
                                                   d[0][:, P * c:P * c + P], 0.0, ALU.mult, ALU.add)
            ins.then_inc(S["dt_acs"], 1)
            dve.wait_ge(S["dt_acs"], 1)
            for c in range(NT):
                ins = ts(d[7][:, P * c:P * c + P], d[6][:, P * c:P * c + P], d[6][:, P * c + P - 1:P * c + P], -1.0,
                         ALU.subtract, ALU.mult)
            ins.then_inc(S["dt_acs"], 1)
            taps_of(g, 3)
            evacuate_in(g, 4)
            lo(u + 6)
            dve.wait_ge(S["dt_endexp"], 1)
            tt(d[7], d[7], d[5], ALU.mult).then_inc(S["dt_tok"], 1)
            evacuate_in(g, 5)
            lo(u + 7)
            dve.wait_ge(S["tok_ready"], 1)
            dve.wait_ge(S["acs_out"], 16)

            def group_columns(s):
                if s.reg is not None or s.c > 0:
                    dve.wait_ge(S["ul_ready"], s.v)
                own(cp(ggate[:, :], par[:, ds((s * GW + (C_GROUP + 20)).v, 4)]))
                cp(gtok[:, :, :, :], tok[:, 1:3, :, ds((s * HPG).v, HPG)]).then_inc(S["gt_ready"], 1)

            def weigh_x(s):
                dve.wait_ge(S["gt_ready"], (s + 1).v)
                dve.wait_ge(S["tpx_ready"], (s + 1).v)
                xt = psum[:, 4:6, :].rearrange("p b (c r f) -> p (b c) r f", c=2, r=HPG)
                own(tt(xdt.rearrange("p c (r f) -> p c r f", r=HPG), xt,
                       gtok[:, 0, :, :].unsqueeze(3).to_broadcast([P, NT, HPG, 64]), ALU.mult))
                own(tt(xend.rearrange("p c (r f) -> p c r f", r=HPG), xt[:, 0:NT - 1],
                       gtok[:, 1, 0:NT - 1, :].unsqueeze(3).to_broadcast([P, NT - 1, HPG, 64]), ALU.mult))
                dve.wait_ge(S["cb_ready"], (s + 1).v)
                tt(cb, bank(3).rearrange("p (c l) -> p c l", c=NT),
                   causal.unsqueeze(1).to_broadcast([P, NT, P]), ALU.mult).then_inc(S["xw_ready"], 1)

            def weigh_pairs(s):
                dve.wait_ge(S["xw_ready"], (s + 1).v)
                dve.wait_ge(S["mexp_ready"], (s + 1).v)
                tt(mix, mix, cb.unsqueeze(1).to_broadcast([P, HPG, NT, P]), ALU.mult).then_inc(S["m_ready"], 1)

            def states(s):
                dve.wait_ge(S["st_ready"], (s + 1).v)
                dve.wait_ge(S["dec_ready"], (s + 1).v)
                own.mark(cp(state[:, 0, :], bank(2)[:, 0:256]))
                for c in (1, 2):
                    dec = stat[:, DEC + c - 1:DEC + 8:2].unsqueeze(2).to_broadcast([P, HPG, 64])
                    own.mark(tt(state[:, c, :].rearrange("p (r f) -> p r f", r=HPG),
                                state[:, c - 1, :].rearrange("p (r f) -> p r f", r=HPG), dec, ALU.mult))
                    ins = tt(state[:, c, :], state[:, c, :], bank(2 + c // 2)[:, 256 * (c % 2):256 * (c % 2) + 256],
                             ALU.add)
                    if c == 1:
                        own.mark(ins)
                    else:
                        ins.then_inc(S["s_ready"], 1)

            def output(s):
                dve.wait_ge(S["y_ready"], (s + 1).v)
                dve.wait_ge(S["e_ready"], (s * HPG + HPG).v)
                own(tt(yoff, psum[:, 6:8, P:SEQ], edec, ALU.mult))
                for j in range(2):
                    own(stt(y[:, j, :], sx[:, 2 + j, :], ggate[:, j:j + 1], bank(4 + j), ALU.mult, ALU.add))
                own.wait()
                own.mark(tt(y[:, :, P:SEQ], y[:, :, P:SEQ], yoff, ALU.add))
                dve.wait_ge(S["silu_done"], (s * 6 + 6).v)
                tt(y, y, sz, ALU.mult).then_inc(S["u_ready"], 1)

            def norm(s):
                dve.wait_ge(S["gsd_ready"], (s + 1).v)
                nc.vector.reciprocal(stat_at(G_RS), stat_at(G_SD)).then_inc(S["grs_ready"], 1)

            def normed(s):
                dve.wait_ge(S["grb_ready"], (s + 1).v)
                tt(gun, y, bank(7).unsqueeze(1).to_broadcast([P, 2, SEQ]), ALU.mult).then_inc(S["un_ready"], 1)

            def output_low(s):
                dve.wait_ge(S["uh_ready"], (s * 2 + 2).v)
                for j in range(2):
                    ins = stt(row(b_lo, s * 2 + j, 0, SEQ), gun[:, j, :], ggate[:, 2 + j:3 + j],
                              f32(row(b_hi, s * 2 + j, 0, SEQ)), ALU.mult, ALU.subtract)
                ins.then_inc(S["ul_ready"], 1)

            def group(g):
                u, s = g * 6 + U_MAMBA, g - 1
                group_columns(s)
                evacuate_in(g, 0)
                lo(u + 2)
                taps_of(g, 0)
                weigh_x(s)
                evacuate_in(g, 1)
                lo(u + 3)
                weigh_pairs(s)
                states(s)
                taps_of(g, 1)
                evacuate_in(g, 2)
                lo(u + 4)
                taps_of(g, 2)
                output(s)
                evacuate_in(g, 3)
                lo(u + 5)
                taps_of(g, 3)
                evacuate_in(g, 4)
                lo(u + 6)
                norm(s)
                normed(s)
                evacuate_in(g, 5)
                lo(u + 7)
                output_low(s)

            group(Lin(1))
            with dve.Fori(0, 3) as i:
                own.enter(i, GROUP_STEPS)
                group(Lin(2, 2, i))
                group(Lin(3, 2, i))
                own.leave(3)
            s = Lin(GROUPS - 1)
            group_columns(s)
            weigh_x(s)
            lo(Lin(U_WOUT + 2))
            weigh_pairs(s)
            states(s)
            lo(Lin(U_WOUT + 3))
            output(s)
            norm(s)
            normed(s)
            output_low(s)

            def add_squares(m, n, base):
                if m.reg is None and m.c == 0:
                    return
                dve.wait_ge(S["sq_ready"], (m + (base + 1)).v)
                if m.reg is not None:
                    dve.wait_ge(S["ss_ready"], (m + (2 * (base - base // KT) - 1)).v)
                tt(ssq[:, 0:n], ssq[:, 0:n], sq[:, m.par, 0:n], ALU.add).then_inc(S["ss_ready"], 1)

            def wout_tile(m, j):
                u = m * 2 + (U_WOUT + 2 + j)
                dve.wait_ge(S["unit_done"], (u + 1).v)
                m = m + j
                tt(row(h, m, META, T2), row(h, m, META, T2), acc(m + M_WOUT), ALU.add).then_inc(S["acc_read"], 1)
                lo(u + 2)
                add_squares(m, SEQ, 0)
                dve.wait_ge(S["ah_ready"], (m + 1).v)
                stt(row(a_lo, m, 0, SEQ), row(h, m, META, T2), par[:, ds((m + C_KVN).v, 1)],
                    f32(row(a_hi, m, 0, SEQ)), ALU.mult, ALU.subtract).then_inc(S["al_ready"], 1)

            wout_tile(Lin(0), 0)
            wout_tile(Lin(0), 1)
            with dve.Fori(0, 3) as i:
                m = Lin(2, 2, i)
                lo(m * 2 + (U_WOUT + 2))
                lo(m * 2 + (U_WOUT + 3))
                wout_tile(m, 0)
                wout_tile(m, 1)

            def b_operand(ks):
                for k in ks:
                    dve.wait_ge(S["bh_ready"], k + 1)
                    stt(b_lo[:, k, 0:SEQ], h[:, k, META:T2], par[:, C_BN + k:C_BN + k + 1],
                        f32(b_hi[:, k, 0:SEQ]), ALU.mult, ALU.subtract).then_inc(S["bl_ready"], 1)

            b_operand(range(4))
            lo(Lin(U_ATT + 2))
            dve.wait_ge(S["nsd_ready"], 1)
            nc.vector.reciprocal(stat_at(N_RS), stat_at(N_SD)).then_inc(S["nrs_ready"], 1)
            dve.wait_ge(S["lam_in"], 16)
            lv = lamt.rearrange("p (a b d) -> p a b d", a=2, b=2)
            own.mark(tt(lamp, lv[:, :, 0, :], lv[:, :, 1, :], ALU.mult))
            nc.vector.tensor_reduce(stat_at(LAMS, 2), lamp, AX.X, ALU.add).then_inc(S["lam_sum"], 1)

            def evacuate(n, j):
                dve.wait_ge(S["unit_done"], (n * 4 + (U_ATT + j + 1)).v)
                if n.reg is not None or n.c > 0:
                    if j == 1:
                        dve.wait_ge(S["vt_tp"], n.v)
                    if j == 3:
                        dve.wait_ge(S["sg_ready"], n.v)
                dst = (ak[:, n.par, :], afm, aq[:, n.par, :], agt)[j]
                tt(dst, acc(n * 4 + (M_ATT + j)), rt[:, 0:SEQ], ALU.mult).then_inc(S["acc_read"], 1)

            def biased(s, q):
                n, at = P * (q + 1), P * q * (q + 1)
                dve.wait_ge(S["sc_ready"], (s * NT + (q + 1)).v)
                for i in range(2):
                    ins = stt(asc[:, at + n * i:at + n * i + n], dist[:, SEQ - n:SEQ], stat_at(SLOPE, 1),
                              bank(2 + 2 * (q % 2) + i)[:, 0:n], ALU.mult, ALU.add)
                ins.then_inc(S["scs_ready"], 1)
                dve.wait_ge(S["scs_ready"], (s * NT + (q + 1)).v)
                nc.vector.tensor_reduce(stat_at(A_MX + 2 * q, 2), asc[:, at:at + 2 * n].rearrange(
                    "p (a b) -> p a b", a=2), AX.X, ALU.max).then_inc(S["mx_ready"], 1)

            def weigh(s, q):
                n, at = P * (q + 1), P * q * (q + 1)
                dve.wait_ge(S["ex_ready"], (s * 8 + (2 * q + 2)).v)
                own.mark(nc.vector.reciprocal(stat_at(A_RC + 2 * q, 2), stat_at(A_SUM + 2 * q, 2)))
                own.mark(ts(asc[:, at + n:at + 2 * n], asc[:, at + n:at + 2 * n], stat_at(A_RC + 2 * q + 1, 1),
                            stat_at(LAM, 1), ALU.mult, ALU.mult))
                stt(asc[:, at:at + n], asc[:, at:at + n], stat_at(A_RC + 2 * q, 1), asc[:, at + n:at + 2 * n],
                    ALU.mult, ALU.add).then_inc(S["w_ready"], 1)

            def gate_out(f):
                dve.wait_ge(S["ont_ready"], (f + 1).v)
                dve.wait_ge(S["sg_ready"], (f + 1).v)
                tt(aog, bank(3), asg[:, f.par, :], ALU.mult).then_inc(S["og_ready"], 1)

            def out_low(f):
                dve.wait_ge(S["oh_ready"], (f + 1).v)
                stt(row(b_lo, f + KT, 0, SEQ), aog, spl[:, 5, 0:1], f32(row(b_hi, f + KT, 0, SEQ)),
                    ALU.mult, ALU.subtract).then_inc(S["ol_ready"], 1)

            def head(n, project=True, attend=True, finish=True):
                u, s, f = n * 4 + U_ATT, n - 1, n - 2
                if project:
                    evacuate(n, 0)
                    if attend:
                        lo(u + 2)
                    else:
                        b_operand(range(4, KT))
                if attend:
                    own.mark(cp(stat_at(SLOPE, 1), con[:, ds((s + K_SLOPE).v, 1)]))
                    biased(s, 0)
                    biased(s, 1)
                if project:
                    evacuate(n, 1)
                    lo(u + 3)
                if attend:
                    biased(s, 2)
                    biased(s, 3)
                    weigh(s, 0)
                    weigh(s, 1)
                if finish:
                    gate_out(f)
                if project:
                    evacuate(n, 2)
                    lo(u + 4)
                if attend:
                    weigh(s, 2)
                    weigh(s, 3)
                if finish:
                    out_low(f)
                if project:
                    evacuate(n, 3)
                    lo(u + 5)
                if attend:
                    dve.wait_ge(S["osd_ready"], (s + 1).v)
                    own.mark(nc.vector.reciprocal(stat_at(O_RS), stat_at(O_SD)))
                    tt(aon.rearrange("p (a b) -> p a b", a=NT), bank(7).rearrange("p (a b) -> p a b", a=NT),
                       stat_at(O_RS).unsqueeze(2).to_broadcast([P, NT, P]), ALU.mult).then_inc(S["on_ready"], 1)

            dve.wait_ge(S["nrt_ready"], 1)
            head(Lin(0), attend=False, finish=False)
            dve.wait_ge(S["lam_exp"], 1)
            dve.wait_ge(S["dist_in"], 16)
            own.mark(stt(stat_at(LAM, 1), stat_at(LAMS + 1, 1), -LAMBDA_INIT, stat_at(LAMS, 1),
                         ALU.add, ALU.subtract))
            head(Lin(1), finish=False)
            with dve.Fori(0, 3) as i:
                own.enter(i, 20)
                head(Lin(2, 2, i))
                head(Lin(3, 2, i))
                own.leave(3)
            head(Lin(8), project=False)
            gate_out(Lin(7))
            out_low(Lin(7))

            own.mark(tt(mg[:, :, :], h[:, :, 0:META],
                        par[:, C_MIX:C_MIX + KT].unsqueeze(2).to_broadcast([P, KT, META]), ALU.mult))
            own.mark(cp(a_hi[:, :, 0:META], mg[:, :, :]))
            own(tt(a_lo[:, :, 0:META], mg[:, :, :], f32(a_hi[:, :, 0:META]), ALU.subtract))
            own(ts(spl[:, 1, :], par[:, C_LAM:C_LAM + 4], -1.0, 0.0, ALU.mult, ALU.max))
            dve.wait_ge(S["sp_exp"], 1)
            log1p_start(spl[:, 0, :], spl[:, 2, :], spl[:, 2, :], spl[:, 3, :], spl[:, 4, :])
            log1p_terms(spl[:, 3, :], spl[:, 4, :], range(LOG1P_TERMS - 1, 0, -1))
            log1p_end(spl[:, 2, :], spl[:, 1, :], spl[:, 4, :])
            own(ts(rga[:, 0, :], spl[:, 4, :], -8.0, None, ALU.mult))
            ts(rga[:, 1, :], spl[:, 4, :], 8.0, None, ALU.mult).then_inc(S["sp_done"], 1)
            def bout_tile(m):
                dve.wait_ge(S["unit_done"], (m + (U_BOUT + 1)).v)
                tt(row(h, m, META, T2), row(h, m, META, T2), acc(m + M_BOUT), ALU.add).then_inc(S["acc_read"], 1)
                lo(m + (U_BOUT + 2))
                if m.reg is not None or m.c > 0:
                    dve.wait_ge(S["s2_ready"], (m + 1).v)
                    if m.reg is not None:
                        dve.wait_ge(S["ss_ready"], (m + (KT - 2)).v)
                    own(tt(ssq[:, 0:SEQ], ssq[:, 0:SEQ], sq[:, m.par, 0:SEQ], ALU.add))
                    tt(ssq2[:, 0:SEQ], ssq2[:, 0:SEQ], sq2[:, m.par, 0:SEQ], ALU.add).then_inc(S["ss_ready"], 1)
                dve.wait_ge(S["yh_ready"], (m + 1).v)
                stt(row(a_lo, m, META, T2), row(h, m, META, T2), col(gfm, m), f32(row(a_hi, m, META, T2)),
                    ALU.mult, ALU.subtract).then_inc(S["yl_ready"], 1)

            bout_tile(Lin(0))
            bout_tile(Lin(1))
            with dve.Fori(0, 3) as i:
                own.enter(i, 2)
                bout_tile(Lin(2, 2, i))
                bout_tile(Lin(3, 2, i))
                own.leave(3)
            lo(Lin(U_IN2 + 2))
            dve.wait_ge(S["nsd_ready"], 3)
            own.mark(nc.vector.reciprocal(stat_at(N_RS), stat_at(N_SD)))
            own.mark(tt(stat_at(N_R2), stat_at(N_RS), stat_at(N_RS), ALU.mult))
            tt(stat_at(N_R2), stat_at(N_R2), bank(6)[:, 0:NT], ALU.mult).then_inc(S["r1_ready"], 1)
            dve.wait_ge(S["nsd_ready"], 4)
            own.mark(nc.vector.reciprocal(stat_at(N_R2, 5), stat_at(N_SD, 5)))
            tt(stat_at(N_R2), stat_at(N_R2), stat_at(N_RS), ALU.mult).then_inc(S["nrs_ready"], 1)
            own(nc.vector.memset(cu[:, :, 0:DW_K - 1], 0.0))
            own(nc.vector.memset(cxp[:, 0:3], 0.0))
            own(nc.vector.memset(plp[:, :, 0:POOL_PAD], 0.0))
            own.wait()
            dve.wait_ge(S["rr_ready"], 3)

            taps = list(range(DW_K))

            def long_conv(n):
                for k in taps[:n]:
                    src = cu[:, 0, DW_K - 1 - k:DW_K - 1 - k + T2]
                    w = par[:, C_DWW + DW_K - 1 - k:C_DWW + DW_K - k]
                    if k == 0:
                        own.mark(ts(dwo[:, 0, :], src, w, par[:, C_DWB:C_DWB + 1], ALU.mult, ALU.add))
                        continue
                    ins = stt(dwo[:, 0, :], src, w, dwo[:, 0, :], ALU.mult, ALU.add)
                    if k == DW_K - 1:
                        ins.then_inc(S["dw_ready"], 1)
                    else:
                        own.mark(ins)
                del taps[:n]

            def short_conv(j):
                dve.wait_ge(S["acc_read"], M_IN2 + 5 + j)
                c = xc[:, j, :]
                w = [par[:, C_RGW + 4 * j + k:C_RGW + 4 * j + k + 1] for k in range(4)]
                own.mark(ts(c, cxp[:, 3:3 + T2], w[3], par[:, C_RGB + j:C_RGB + j + 1], ALU.mult, ALU.add))
                own.mark(stt(c, cxp[:, 2:2 + T2], w[2], c, ALU.mult, ALU.add))
                own.mark(stt(c, cxp[:, 1:1 + T2], w[1], c, ALU.mult, ALU.add))
                stt(c, cxp[:, 0:T2], w[0], c, ALU.mult, ALU.add).then_inc(S["xc_ready"], 1)

            def one_minus_a2(j):
                b = 4 * (j % 2)
                dve.wait_ge(S["at_ready"], j + 1)
                stt(rtmp[:, b + 3, :], rtmp[:, b, :], 1.0, rtmp[:, b + 3, :], ALU.add, ALU.mult
                    ).then_inc(S["m2_ready"], 1)

            def scan(j):
                b = 4 * (j % 2)
                dve.wait_ge(S["rga_ready"], j + 1)
                own.mark(tt(rtmp[:, b + 1, :], rtmp[:, b + 1, :], xc[:, j, :], ALU.mult))
                dve.wait_ge(S["mu_ready"], j + 1)
                own.mark(tt(rtmp[:, b + 1, :], rtmp[:, b + 1, :], rtmp[:, b + 3, :], ALU.mult))
                nc.vector.tensor_tensor_scan(xc[:, j, :], rtmp[:, b + 2, :], rtmp[:, b + 1, :], 0.0,
                                             ALU.mult, ALU.add).then_inc(S["scan_ready"], 1)

            def rnn_low(p):
                for j in (2 * p, 2 * p + 1):
                    dve.wait_ge(S["yh_ready"], KT + 1 + j)
                    tt(b_lo[:, 4 + j, :], xc[:, j, :], f32(b_hi[:, 4 + j, :]), ALU.subtract
                       ).then_inc(S["yl_ready"], 1)

            def means(j):
                dve.wait_ge(S["psum_ready"], j + 1)
                for rows, v in zip((slice(0, 64), slice(64, 128)), pool_sums[j]):
                    own(tt(plp[rows, j, POOL_PAD:POOL_PAD + 16], v[rows, POOL_PAD:POOL_PAD + 16],
                           plp[rows, j, POOL_PAD:POOL_PAD + 16], ALU.subtract))
                    ins = stt(plp[rows, j, POOL_PAD + 16:], v[rows, POOL_PAD + 16:],
                              con[rows, K_WIN + j:K_WIN + j + 1], plp[rows, j, POOL_PAD + 16:],
                              ALU.mult, ALU.subtract)
                    if rows.start:
                        ins.then_inc(S["pool_ready"], 1)
                    else:
                        own(ins)

            def layer_norm_sums():
                dve.wait_ge(S["ln_tp"], 1)
                own.mark(nc.vector.memset(bnag[:, :, :], 1.0))
                for i, (c0, cn) in enumerate(TOKENS2):
                    own(nc.vector.bn_stats(bnst[0:cn, i, :], psum[0:cn, 4 + i // 2, 256 * (i % 2):256 * (i % 2) + 256]))
                own.wait()
                for i, (c0, cn) in enumerate(TOKENS2):
                    ins = nc.vector.bn_aggr(bnag[0:cn, i, :], bnst[0:cn, i, :])
                ins.then_inc(S["ln_stat"], 1)

            def layer_norm():
                dve.wait_ge(S["ln_sd"], 1)
                dve.wait_ge(S["scan_ready"], 3)
                own.mark(nc.vector.reciprocal(stat_at(N_RS, 5), stat_at(N_SD, 5)))
                for i, (c0, cn) in enumerate(TOKENS2):
                    ins = ts(lnt[0:cn, i, :], psum[0:cn, 4 + i // 2, 256 * (i % 2):256 * (i % 2) + 256],
                             bnag[0:cn, i, 0:1], stat[0:cn, N_RS + i:N_RS + i + 1], ALU.subtract, ALU.mult)
                ins.then_inc(S["ln_ready"], 1)

            TAPS = {1: 3, 2: 5, 3: 3, 4: 2, 5: 2, 6: 1, 7: 1, 8: 3, 9: 5, 10: 5, 11: 1}
            for n in range(14):
                dve.wait_ge(S["unit_done"], U_IN2 + n + 1)
                if n < 4:
                    j = n // 2
                    dst = bgt if n % 2 else bvt
                elif n < 8:
                    if n > 4:
                        dve.wait_ge(S["xc_ready"], n - 4)
                    dst = cxp[:, 3:3 + T2]
                elif n < 10:
                    dst = plp[:, n - 8, POOL_PAD:POOL_PAD + T2]
                else:
                    dst = cg[:, n - 10, :]
                if n == 12:
                    dve.wait_ge(S["prod_used"], DW_K - 1)
                tt(halves(dst), acc2(Lin(M_IN2 + n)), halves(rr), ALU.mult).then_inc(S["acc_read"], 1)
                if 0 < n < 13:
                    lo(Lin(U_IN2 + n + 2))
                if n == 1:
                    dve.wait_ge(S["bg_ready"], 1)
                    own.mark(tt(cu[:, 0, DW_K - 1:DW_K - 1 + T2], bvt, bgt, ALU.mult))
                if n == 3:
                    dve.wait_ge(S["bg_ready"], 2)
                    tt(cu[:, 1, DW_K - 1:DW_K - 1 + T2], bvt, bgt, ALU.mult).then_inc(S["cu_ready"], 1)
                if 4 <= n < 8:
                    short_conv(n - 4)
                if n == 8:
                    one_minus_a2(0)
                    one_minus_a2(1)
                long_conv(TAPS.get(n, 0))
                if n == 8:
                    scan(0)
                    scan(1)
                if n == 11:
                    one_minus_a2(2)
                    one_minus_a2(3)
                if n == 12:
                    layer_norm_sums()
                    scan(2)
                    layer_norm()
            means(0)
            means(1)
            lo(Lin(U_OUT2 + 1))
            scan(3)
            rnn_low(0)
            rnn_low(1)
            for j in range(2):
                dve.wait_ge(S["yh_ready"], KT + 5 + j)
                stt(halves(b_lo[:, j, :]), psum[:, 2 * j:2 * j + 2, 0:HALF2], par[:, C_PSC + j:C_PSC + j + 1],
                    f32(halves(b_hi[:, j, :])), ALU.mult, ALU.subtract).then_inc(S["yl_ready"], 1)
            for j in range(2):
                dve.wait_ge(S["yh_ready"], KT + 7 + j)
                tt(halves(b_lo[:, 2 + j, :]), psum[:, 4 + 2 * j:6 + 2 * j, 0:HALF2], f32(halves(b_hi[:, 2 + j, :])),
                   ALU.subtract).then_inc(S["yl_ready"], 1)
            def out2_tile(m):
                own.mark(stt(row(h, m, META, T2), row(h, m, META, T2), par[:, ds((m + C_FIN).v, 1)],
                             rt[:, META:T2], ALU.mult, ALU.mult))
                dve.wait_ge(S["unit_done"], (m + (U_OUT2 + 1)).v)
                hm = halves(row(h, m, 0, T2))
                tt(hm, hm, acc2(m + M_OUT2), ALU.add).then_inc(S["acc_read"], 1)
                lo(m + (U_OUT2 + 2))
                add_squares(m, T2, KT)
                dve.wait_ge(S["ah_ready"], (m + (KT + 1)).v)
                stt(row(a_lo, m, 0, T2), row(h, m, 0, T2), par[:, ds((m + C_MLP).v, 1)],
                    f32(row(a_hi, m, 0, T2)), ALU.mult, ALU.subtract).then_inc(S["al_ready"], 1)

            out2_tile(Lin(0))
            out2_tile(Lin(1))
            with dve.Fori(0, 3) as i:
                own.enter(i, 2)
                out2_tile(Lin(2, 2, i))
                out2_tile(Lin(3, 2, i))
                own.leave(3)

            lo(Lin(U_MLP + 2))
            dve.wait_ge(S["nsd_ready"], 6)
            nc.vector.reciprocal(stat_at(N_RS, 5), stat_at(N_SD, 5)).then_inc(S["nrs_ready"], 1)
            dve.wait_ge(S["nrt_ready"], 2)

            def up(m, half, prep=True):
                n = m + 16 * half
                dve.wait_ge(S["unit_done"], (m + (U_MLP + 32 * half + 1)).v)
                stt(halves(ft), acc2(m + (M_MLP + 24 * half)), 0.0, halves(rt[:, :]), ALU.max, ALU.mult
                    ).then_inc(S["acc_read"], 1)
                if prep:
                    lo(m + (U_MLP + 32 * half + 2))
                dve.wait_ge(S["acc_read"], (m + (M_MLP + 24 * half + 1)).v)
                own.mark(tt(fs, ft, ft, ALU.mult))
                dve.wait_ge(S["fh_ready"], (n + 1).v)
                tt(row(b_lo, m, 0, T2), fs, f32(row(b_hi, m, 0, T2)), ALU.subtract).then_inc(S["fl_ready"], 1)

            def down(m, half, prep=True):
                u = m * 2 + (U_MLP + 32 * half + 16)
                if prep:
                    lo(u + 2)
                dve.wait_ge(S["unit_done"], (u + 2).v)
                hm = halves(row(h, m, 0, T2))
                tt(hm, hm, acc2(m + (M_MLP + 24 * half + 16)), ALU.add).then_inc(S["acc_read"], 1)
                if prep:
                    lo(u + 3)

            up(Lin(0), 0, prep=False)
            up(Lin(1), 0)
            for half in range(2):
                with dve.Fori(0, 7 + half) as i:
                    own.enter(i, 2)
                    for j in range(2):
                        up(Lin(2 * (1 - half) + j, 2, i), half)
                    own.leave(7 + half)
                with dve.Fori(0, 4 - half) as i:
                    for m in (Lin(0, 2, i), Lin(1, 2, i)):
                        down(m, half)
            down(Lin(6), 1)
            down(Lin(7), 1, prep=False)
            dve.wait_ge(S["gout_in"], 16)
            for i in range(NT):
                dve.wait_ge(S["osum_ready"], i + 1)
                own.mark(nc.vector.reciprocal(stat_at(O_RS + i, 1), stat_at(O_SD + i, 1)))
                if i >= 2:
                    dve.wait_ge(S[f"out{i % 2}"], 16 * (i // 2))
                stt(osb[:, i % 2, :], psum[:, 4 + 2 * (i % 2):6 + 2 * (i % 2), :].rearrange("p a b -> p (a b)"),
                    stat_at(O_RS + i, 1), gout, ALU.mult, ALU.mult).then_inc(S["o_done"], 1)


def ssd_cols(g):
    return [g * P + 2 * DINNER, g * P + (2 * DINNER + D), g * 256 + DINNER, g * 256 + (DINNER + P),
            g * 256, g * 256 + P]


GATE_STEPS = (6, 7, 9, 10)
IN2_TILES = [2, 4, 3, 5, 10, 11, 12, 13, 0, 1, 6, 7, 8, 9]
GROUP_STEPS = 40


def col(v, m):
    return v[:, ds(m.v, 1)]


def row(v, m, c0, c1):
    if m.reg is None:
        return v[:, m.c, c0:c1]
    return v[:, ds(m.v, 1), c0:c1].rearrange("p a b -> p (a b)")


def constants():
    import numpy as np

    con = np.zeros((P, NCONST), np.float32)
    p, j = np.arange(P)[:, None], np.arange(SEQ)[None, :]
    con[:, K_ID:K_ID + P] = np.eye(P)
    con[:, K_CAUSAL:K_CAUSAL + P] = j[:, :P] >= p
    windows = np.array([[2, 8], [4, 16]])
    for t in range(2):
        for half in range(2):
            w = windows[half, t]
            rows = slice(64 * half, 64 * half + 64)
            con[rows, K_INV + 16 * t:K_INV + 16 * t + 16] = 1.0 / np.minimum(np.arange(1, 17), w)
            con[rows, K_WIN + t] = 1.0 / w
    con[:, K_SLOPE:K_SLOPE + HEADS] = -8.0 * 2.0 ** -np.arange(1.0, HEADS + 1)
    return con


def distances():
    import numpy as np

    p, j = np.arange(P)[:, None], np.arange(SEQ)[None, :]
    dist = np.abs(p + (SEQ - P) - j).astype(np.float32)
    dist[(p < 64) & (j >= SEQ - 64)] = 1e30
    return dist


def kernel(**inputs):
    import numpy as np
    import concourse.bacc as bacc
    from concourse.bass_utils import run_bass_kernel_spmd

    x = {k: np.asarray(v) for k, v in inputs.items()}
    par = np.zeros((P, NPAR), np.float32)
    cw, cb = x["a_conv_w"][0].reshape(4, 32, P), x["a_conv_b"][0].reshape(32, P)
    skip = np.repeat(x["a_d_skip"][0], 64).reshape(16, P)
    gate = x["a_gate_norm_g"][0].reshape(16, P)
    for g in range(GROUPS):
        for j, tile in enumerate((16 + g, 24 + g, 2 * g, 2 * g + 1)):
            par[:, GW * g + 5 * j:GW * g + 5 * j + 4] = cw[:, tile].T
            par[:, GW * g + 5 * j + 4] = cb[tile]
        for j in range(2):
            par[:, GW * g + 20 + j] = skip[2 * g + j]
            par[:, GW * g + 22 + j] = gate[2 * g + j]
    for at, name in ((C_ANORM, "a_norm_g"), (C_KVN, "kv_norm_g"), (C_BN, "b_norm_g"), (C_FIN, "final_norm_g"),
                     (C_MIX, "mix_norm_g_2"), (C_MLP, "mlp_norm_g_2"), (C_SUBG, "b_sub_g"), (C_PSC, "pool_scale_2"),
                     (C_DWB, "convb_dw_b_2"), (C_LNG, "convb_ln_g_2"), (C_LNB, "convb_ln_b_2"),
                     (C_RGB, "rg_conv_b_2"), (C_BA, "rg_b_a_2"), (C_BX, "rg_b_x_2"), (C_LAM, "rg_lambda_2")):
        v = x[name].reshape(-1, P).T
        par[:, at:at + v.shape[1]] = v
    par[96:, C_DTB] = x["a_dt_bias"][0]
    par[96:, C_ALOG] = x["a_a_log"][0]
    for j in range(2):
        par[:, C_DWW + DW_K * j:C_DWW + DW_K * j + DW_K] = x["convb_dw_w_2"][0][:, P * j:P * j + P].T
    for j in range(4):
        par[:, C_RGW + 4 * j:C_RGW + 4 * j + 4] = x["rg_conv_w_2"][0][:, P * j:P * j + P].T
    bd = np.zeros((P, 10, P), np.float32)
    for at, name, n in ((0, "pool_w_2", 4), (2, "rg_w_a_2", 8), (6, "rg_w_x_2", 8)):
        for k in range(n):
            o = 64 * (k % 2)
            bd[o:o + 64, at + k // 2, o:o + 64] = x[name][0][k]
    arrays = {
        "x": x["x"][0], "a_w_in": x["a_w_in"][0], "a_w_out": x["a_w_out"][0], "w_kv": x["w_kv"],
        "b_w_in": x["b_w_in"][0], "b_w_out": x["b_w_out"][0], "w_in_2": x["w_in_2"][0], "w_out_2": x["w_out_2"][0],
        "w_up_2": x["w_up_2"][0], "w_down_2": x["w_down_2"][0], "b_lambda": x["b_lambda"],
        "meta_tokens_2": x["meta_tokens_2"], "convb_pw_w_2": x["convb_pw_w_2"][0],
        "final_norm_g_2": x["final_norm_g_2"], "params": par, "blockdiag": bd, "consts": constants(), "dist": distances(),
    }
    arrays = {k: np.ascontiguousarray(v) for k, v in arrays.items()}
    nc = bacc.Bacc("TRN2", target_bir_lowering=False, num_devices=1)
    t = {k: nc.dram_tensor(k, v.shape, F32, kind="ExternalInput").ap() for k, v in arrays.items()}
    t["acs"] = nc.dram_tensor("acs", (32, SEQ), F32, kind="Internal").ap()
    t["out"] = nc.dram_tensor("out", (SEQ, D), F32, kind="ExternalOutput").ap()
    build(nc, t)
    r = run_bass_kernel_spmd(nc, [arrays], core_ids=[0])
    return r.results[0]["out"].reshape(1, SEQ, D)
```
